# Optimizing a Trainium2 kernel written in Bass

```python
import jax, jax.numpy as jnp
from jax import lax
import numpy as np
import math
import jax
import jax.numpy as jnp

D_MODEL = 1024
BATCH = 1
SEQ = 256
DEPTH = 1

N_HEADS_ATTN = 8
HEAD_DIM = 64
ATTN_WIDTH = N_HEADS_ATTN * HEAD_DIM
IDX_HEADS = 8
IDX_DIM = 32
TOPK_MAX = 256
Q_BLOCK = 128
CONV_WIDTH = D_MODEL - ATTN_WIDTH
CONV_GROUPS = 8
CONV_K = 3
MIX_WIDTH = ATTN_WIDTH + CONV_WIDTH
ROPE_THETA = 500000.0
ROPE_DIM = HEAD_DIM // 4
D_FF = ((-(-8 * D_MODEL // 3)) + 255) // 256 * 256
DEEPNORM_ALPHA = (2.0 * DEPTH) ** 0.25
DEEPNORM_BETA = (8.0 * DEPTH) ** -0.25
EPS = 1e-5
NEG_INF = -1e30

IN_SPLITS = (ATTN_WIDTH, HEAD_DIM, HEAD_DIM, IDX_HEADS * IDX_DIM, IDX_DIM, IDX_HEADS,
             CONV_WIDTH, CONV_WIDTH, CONV_WIDTH)
IN_COLS = sum(IN_SPLITS)


def rope_tables(seq_len):
    pos = jnp.arange(seq_len, dtype=jnp.float32)
    inv = ROPE_THETA ** (-(jnp.arange(0, ROPE_DIM, 2, dtype=jnp.float32) / ROPE_DIM))
    ang = pos[:, None] * inv[None, :]
    return jnp.cos(ang)[:, None, :], jnp.sin(ang)[:, None, :]

def partial_rope(x, cos, sin):
    cos = cos.astype(x.dtype)
    sin = sin.astype(x.dtype)
    half = ROPE_DIM // 2
    x1, x2, rest = x[..., :half], x[..., half:ROPE_DIM], x[..., ROPE_DIM:]
    return jnp.concatenate([x1 * cos - x2 * sin, x2 * cos + x1 * sin, rest], axis=-1)

def layer_norm(x, g, b):
    xf = x.astype(jnp.float32)
    mu = jnp.mean(xf, axis=-1, keepdims=True)
    var = jnp.mean(jnp.square(xf - mu), axis=-1, keepdims=True)
    y = (xf - mu) * lax.rsqrt(var + EPS) * g.astype(jnp.float32) + b.astype(jnp.float32)
    return y.astype(x.dtype)

def group_rms_norm(x, g, n_groups):
    bsz, s, w = x.shape
    xf = x.astype(jnp.float32).reshape(bsz, s, n_groups, w // n_groups)
    xf = xf * lax.rsqrt(jnp.mean(jnp.square(xf), axis=-1, keepdims=True) + EPS)
    return (xf.reshape(bsz, s, w) * g.astype(jnp.float32)).astype(x.dtype)

def modulate(x, shift, scale):
    return x * (1.0 + scale[:, None, :]) + shift[:, None, :]

def sparse_indexer_attention(q, k, v, qi, ki, wi, k_sel):
    bsz, s, h, dh = q.shape
    n_blk = s // Q_BLOCK
    attn_scale = HEAD_DIM ** -0.5
    key_pos = jnp.arange(s)
    ki32 = ki.astype(jnp.float32)

    def to_blocks(a):
        return jnp.moveaxis(a.reshape((bsz, n_blk, Q_BLOCK) + a.shape[2:]), 1, 0)

    def block_fn(args):
        q_b, qi_b, w_b, t_b = args
        rel = jax.nn.relu(jnp.einsum('bqhd,bsd->bqhs', qi_b.astype(jnp.float32), ki32))
        score = jnp.einsum('bqhs,bqh->bqs', rel, w_b.astype(jnp.float32))
        causal = key_pos[None, :] <= t_b[:, None]
        score = jnp.where(causal[None], score, NEG_INF)
        _, sel = lax.top_k(score, k_sel)
        valid = sel <= t_b[None, :, None]
        kg = jax.vmap(lambda kb, ib: kb[ib])(k, sel)
        vg = jax.vmap(lambda vb, ib: vb[ib])(v, sel)
        logits = jnp.einsum('bqhd,bqkd->bhqk', q_b, kg).astype(jnp.float32) * attn_scale
        logits = jnp.where(valid[:, None], logits, NEG_INF)
        p = jax.nn.softmax(logits, axis=-1).astype(v.dtype)
        return jnp.einsum('bhqk,bqkd->bqhd', p, vg)

    t_blocks = key_pos.reshape(n_blk, Q_BLOCK)
    out = lax.map(block_fn, (to_blocks(q), to_blocks(qi), to_blocks(wi), t_blocks))
    return jnp.moveaxis(out, 0, 1).reshape(bsz, s, h, dh)

def token_mixer(h, w_in, conv_w, attn_norm_g, conv_norm_g, w_out, cos, sin):
    bsz, s, _ = h.shape
    k_sel = min(TOPK_MAX, s // 4)
    proj = h @ w_in
    offsets = np.cumsum(IN_SPLITS)[:-1].tolist()
    q, k, v, qi, ki, wi, gate_b, gate_c, hc = jnp.split(proj, offsets, axis=-1)

    q = partial_rope(q.reshape(bsz, s, N_HEADS_ATTN, HEAD_DIM), cos, sin)
    k = partial_rope(k[:, :, None, :], cos, sin)[:, :, 0, :]
    qi = partial_rope(qi.reshape(bsz, s, IDX_HEADS, IDX_DIM), cos, sin)
    ki = partial_rope(ki[:, :, None, :], cos, sin)[:, :, 0, :]
    wi = wi * (IDX_HEADS ** -0.5 * IDX_DIM ** -0.5)
    attn = sparse_indexer_attention(q, k, v, qi, ki, wi, k_sel).reshape(bsz, s, ATTN_WIDTH)
    attn = group_rms_norm(attn, attn_norm_g, N_HEADS_ATTN)

    u = gate_c * hc
    u_pad = jnp.pad(u, ((0, 0), (CONV_K - 1, 0), (0, 0)))
    conv = sum(conv_w[j] * u_pad[:, j:j + s, :] for j in range(CONV_K))
    conv_out = group_rms_norm(gate_b * conv, conv_norm_g, CONV_GROUPS)

    mixed = jnp.concatenate([attn, conv_out], axis=-1)
    return mixed @ w_out

def swiglu(h, w_gate, w_up, w_down):
    return (jax.nn.silu(h @ w_gate) * (h @ w_up)) @ w_down

def first_inputs(seed: int = 0) -> dict:
    key = jax.random.key(seed)
    ks = jax.random.split(key, 17)
    n = jax.random.normal
    f32 = jnp.float32
    L = DEPTH
    return {
        "x": n(ks[0], (BATCH, SEQ, D_MODEL), f32),
        "c": n(ks[1], (BATCH, D_MODEL), f32),
        "w_ada": n(ks[2], (L, D_MODEL, 6 * D_MODEL), f32) * (D_MODEL ** -0.5),
        "b_ada": n(ks[3], (L, 6 * D_MODEL), f32) * 0.02,
        "w_in": n(ks[4], (L, D_MODEL, IN_COLS), f32) * (D_MODEL ** -0.5),
        "conv_w": n(ks[5], (L, CONV_K, CONV_WIDTH), f32) * (CONV_K ** -0.5),
        "attn_norm_g": 1.0 + 0.1 * n(ks[6], (L, ATTN_WIDTH), f32),
        "conv_norm_g": 1.0 + 0.1 * n(ks[7], (L, CONV_WIDTH), f32),
        "w_out": n(ks[8], (L, MIX_WIDTH, D_MODEL), f32) * (MIX_WIDTH ** -0.5) * DEEPNORM_BETA,
        "ln1_g": 1.0 + 0.1 * n(ks[9], (L, D_MODEL), f32),
        "ln1_b": 0.02 * n(ks[10], (L, D_MODEL), f32),
        "w_gate": n(ks[11], (L, D_MODEL, D_FF), f32) * (D_MODEL ** -0.5),
        "w_up": n(ks[12], (L, D_MODEL, D_FF), f32) * (D_MODEL ** -0.5),
        "w_down": n(ks[13], (L, D_FF, D_MODEL), f32) * (D_FF ** -0.5) * DEEPNORM_BETA,
        "ln2_g": 1.0 + 0.1 * n(ks[14], (L, D_MODEL), f32),
        "ln2_b": 0.02 * n(ks[15], (L, D_MODEL), f32),
    }

def first_block(x, c, w_ada, b_ada, w_in, conv_w, attn_norm_g, conv_norm_g, w_out,
              ln1_g, ln1_b, w_gate, w_up, w_down, ln2_g, ln2_b):
    s = x.shape[1]
    cos, sin = rope_tables(s)
    c_act = jax.nn.silu(c)
    for l in range(DEPTH):
        mod = c_act @ w_ada[l] + b_ada[l]
        sh1, sc1, g1, sh2, sc2, g2 = jnp.split(mod, 6, axis=-1)
        mix = token_mixer(modulate(x, sh1, sc1), w_in[l], conv_w[l], attn_norm_g[l],
                          conv_norm_g[l], w_out[l], cos, sin)
        x = layer_norm(DEEPNORM_ALPHA * x + g1[:, None, :] * mix, ln1_g[l], ln1_b[l])
        ff = swiglu(modulate(x, sh2, sc2), w_gate[l], w_up[l], w_down[l])
        x = layer_norm(DEEPNORM_ALPHA * x + g2[:, None, :] * ff, ln2_g[l], ln2_b[l])
    return x


DEPTH_2 = 2

N_MIXERS = 4
N_PER_MIXER = tuple((DEPTH_2 - m + N_MIXERS - 1) // N_MIXERS for m in range(N_MIXERS))
PLE_DIM = 256
ROPE_THETA_2 = 10000.0
EPS_2 = 1e-6
D_FF_2 = (-((-8 * D_MODEL) // 3) + 255) // 256 * 256

GLA_HEADS = 4
GLA_DK = D_MODEL // 2
GLA_DV = D_MODEL
GLA_HK = GLA_DK // GLA_HEADS
GLA_HV = GLA_DV // GLA_HEADS
GLA_RANK = 16
GLA_TAU = 16.0
GLA_CHUNK = 64
GLA_IN = 2 * GLA_DK + 2 * GLA_DV + 2 * GLA_RANK

DIFF_HEAD_DIM = 64
DIFF_HEADS = D_MODEL // (2 * DIFF_HEAD_DIM)
DIFF_IN = 3 * D_MODEL

SSD_D_INNER = 2 * D_MODEL
SSD_HEAD_DIM = 64
SSD_HEADS = SSD_D_INNER // SSD_HEAD_DIM
SSD_GROUPS = 8
SSD_STATE = 128
SSD_CONV = 5
SSD_CHUNK = 128
SSD_CONV_DIM = SSD_D_INNER + 2 * SSD_GROUPS * SSD_STATE
SSD_IN = SSD_D_INNER + SSD_CONV_DIM + 2 * SSD_HEADS

DIL_PAIRS = ((128, 1), (512, 4), (2048, 16))
DIL_GROUPS = len(DIL_PAIRS)
DIL_HEADS = 16
DIL_HEAD_DIM = 64
DIL_WIDTH = DIL_HEADS * DIL_HEAD_DIM
DIL_IN = 3 * DIL_GROUPS * DIL_WIDTH


F32 = jnp.float32

def split_cols(x, sizes):
    out, start = [], 0
    for s in sizes:
        out.append(x[..., start:start + s])
        start += s
    return out

def rms_norm(x, g):
    xf = x.astype(F32)
    y = xf * lax.rsqrt(jnp.mean(xf * xf, axis=-1, keepdims=True) + EPS_2)
    return (y * g.astype(F32)).astype(x.dtype)

def rope(x, pos):
    hd = x.shape[-1]
    half = hd // 2
    inv = ROPE_THETA_2 ** (-jnp.arange(half, dtype=F32) * 2.0 / hd)
    ang = pos.astype(F32)[:, None] * inv[None, :]
    cos = jnp.cos(ang)[:, None, :]
    sin = jnp.sin(ang)[:, None, :]
    xf = x.astype(F32)
    x1, x2 = xf[..., :half], xf[..., half:]
    return jnp.concatenate([x1 * cos - x2 * sin, x2 * cos + x1 * sin], axis=-1).astype(x.dtype)

def swiglu_2(h, w_in, w_out):
    g, u = split_cols(h @ w_in, [D_FF_2, D_FF_2])
    return (jax.nn.silu(g) * u) @ w_out

def gla_chunked(q, k, v, log_a, strict):
    bsz, nh, seq, dk = q.shape
    dv = v.shape[-1]
    c = GLA_CHUNK
    n = seq // c
    qf = q.astype(F32).reshape(bsz, nh, n, c, dk)
    kf = k.astype(F32).reshape(bsz, nh, n, c, dk)
    vf = v.astype(F32).reshape(bsz, nh, n, c, dv)
    b = jnp.cumsum(log_a.astype(F32).reshape(bsz, nh, n, c, dk), axis=3)
    b_last = b[:, :, :, -1:, :]
    q_in = qf * jnp.exp(b)
    scores = jnp.einsum('bhncd,bhnjd->bhncj', q_in, kf * jnp.exp(-b))
    mask = jnp.tril(jnp.ones((c, c), dtype=bool), -1 if strict else 0)
    scores = jnp.where(mask, scores, 0.0)
    o_intra = jnp.einsum('bhncj,bhnje->bhnce', scores, vf)
    u = jnp.einsum('bhncd,bhnce->bhnde', kf * jnp.exp(b_last - b), vf)
    decay = jnp.exp(b_last[:, :, :, 0, :])

    def step(s_prev, inp):
        u_n, a_n = inp
        return s_prev * a_n[..., None] + u_n, s_prev

    s0 = jnp.zeros((bsz, nh, dk, dv), F32)
    _, s_prev = lax.scan(step, s0, (jnp.moveaxis(u, 2, 0), jnp.moveaxis(decay, 2, 0)))
    s_prev = jnp.moveaxis(s_prev, 0, 2)
    o_inter = jnp.einsum('bhncd,bhnde->bhnce', q_in, s_prev)
    return (o_intra + o_inter).reshape(bsz, nh, seq, dv)

def gla_mixer(h, w_in, w_gate_f, b_gate_f, w_gate_b, b_gate_b, g_out, w_out):
    bsz, seq, _ = h.shape
    q, k, v, r, zf, zb = split_cols(h @ w_in, [GLA_DK, GLA_DK, GLA_DV, GLA_DV, GLA_RANK, GLA_RANK])

    def heads(t, hd):
        return t.reshape(bsz, seq, GLA_HEADS, hd).transpose(0, 2, 1, 3)

    qh = heads(q, GLA_HK) * (GLA_HK ** -0.5)
    kh = heads(k, GLA_HK)
    vh = heads(v, GLA_HV)
    la_f = heads(jax.nn.log_sigmoid((zf @ w_gate_f + b_gate_f).astype(F32)) / GLA_TAU, GLA_HK)
    la_b = heads(jax.nn.log_sigmoid((zb @ w_gate_b + b_gate_b).astype(F32)) / GLA_TAU, GLA_HK)

    def flip(t):
        return jnp.flip(t, axis=2)

    o = gla_chunked(qh, kh, vh, la_f, False) + flip(
        gla_chunked(flip(qh), flip(kh), flip(vh), flip(la_b), True))
    o = rms_norm(o.transpose(0, 2, 1, 3).astype(h.dtype), g_out).reshape(bsz, seq, GLA_DV)
    return (o * jax.nn.silu(r)) @ w_out

def diff_attn_mixer(h, pos, w_in, g_q, g_k, lam_q1, lam_k1, lam_q2, lam_k2, g_sub, w_out, lambda_init):
    bsz, seq, _ = h.shape
    nh, dh = DIFF_HEADS, DIFF_HEAD_DIM
    q, k, v = split_cols(h @ w_in, [D_MODEL, D_MODEL, D_MODEL])
    q = rms_norm(q.reshape(bsz, seq, nh, 2, dh), g_q)
    k = rms_norm(k.reshape(bsz, seq, nh, 2, dh), g_k)
    q = rope(q.reshape(bsz, seq, 2 * nh, dh), pos).reshape(bsz, seq, nh, 2, dh)
    k = rope(k.reshape(bsz, seq, 2 * nh, dh), pos).reshape(bsz, seq, nh, 2, dh)
    lam = (jnp.exp(jnp.sum(lam_q1.astype(F32) * lam_k1.astype(F32)))
           - jnp.exp(jnp.sum(lam_q2.astype(F32) * lam_k2.astype(F32))) + lambda_init)
    nb = seq // Q_BLOCK
    qb = q.reshape(bsz, nb, Q_BLOCK, nh, 2, dh).transpose(1, 0, 3, 4, 2, 5)
    kt = k.transpose(0, 2, 3, 1, 4)
    vt = v.reshape(bsz, seq, nh, 2 * dh).transpose(0, 2, 1, 3)
    scale = dh ** -0.5

    def block(q_blk):
        s = jnp.einsum('bhtqd,bhtkd->bhtqk', q_blk, kt).astype(F32) * scale
        pr = jax.nn.softmax(s, axis=-1)
        a = pr[:, :, 0] - lam * pr[:, :, 1]
        return jnp.einsum('bhqk,bhkd->bhqd', a.astype(vt.dtype), vt)

    o = lax.map(block, qb)
    o = o.transpose(1, 0, 3, 2, 4).reshape(bsz, seq, nh, 2 * dh)
    o = rms_norm(o, g_sub) * (1.0 - lambda_init)
    return o.reshape(bsz, seq, D_MODEL) @ w_out

def depthwise_conv_centered(x, w, b):
    width, ch = w.shape
    y = lax.conv_general_dilated(
        x, w[:, None, :].astype(x.dtype), window_strides=(1,),
        padding=[((width - 1) // 2, width // 2)],
        dimension_numbers=('NWC', 'WIO', 'NWC'), feature_group_count=ch)
    return y + b

def ssd_chunked(x, dt, a, bm, cm, strict):
    bsz, seq, nh, hp = x.shape
    ng, ns = bm.shape[2], bm.shape[3]
    hg = nh // ng
    c = SSD_CHUNK
    nc = seq // c
    xdt = (x.astype(F32) * dt[..., None]).reshape(bsz, nc, c, ng, hg, hp)
    acum = jnp.cumsum((dt * a).reshape(bsz, nc, c, ng, hg), axis=2)
    bc = bm.astype(F32).reshape(bsz, nc, c, ng, ns)
    cc = cm.astype(F32).reshape(bsz, nc, c, ng, ns)
    mask = jnp.tril(jnp.ones((c, c), dtype=bool), -1 if strict else 0)[:, :, None, None]
    diff = acum[:, :, :, None] - acum[:, :, None, :]
    lmat = jnp.where(mask, jnp.exp(jnp.where(mask, diff, 0.0)), 0.0)
    cb = jnp.einsum('bnigs,bnjgs->bnijg', cc, bc)
    y_diag = jnp.einsum('bnijg,bnijgh,bnjghp->bnighp', cb, lmat, xdt)
    a_last = acum[:, :, -1]
    decay_states = jnp.exp(a_last[:, :, None] - acum)
    states = jnp.einsum('bnjgs,bnjgh,bnjghp->bnghps', bc, decay_states, xdt)

    def step(s_prev, inp):
        st, dec = inp
        return s_prev * dec[..., None, None] + st, s_prev

    s0 = jnp.zeros((bsz, ng, hg, hp, ns), F32)
    _, prev = lax.scan(step, s0, (jnp.moveaxis(states, 1, 0), jnp.moveaxis(jnp.exp(a_last), 1, 0)))
    prev = jnp.moveaxis(prev, 0, 1)
    y_off = jnp.einsum('bnigs,bnigh,bnghps->bnighp', cc, jnp.exp(acum), prev)
    return (y_diag + y_off).reshape(bsz, seq, nh, hp)

def ssd_mixer(h, w_in, conv_w, conv_b, dt_bias_f, a_log_f, dt_bias_b, a_log_b, d_skip, g_norm, w_out):
    bsz, seq, _ = h.shape
    z, xbc, dt_f, dt_b = split_cols(h @ w_in, [SSD_D_INNER, SSD_CONV_DIM, SSD_HEADS, SSD_HEADS])
    xbc = jax.nn.silu(depthwise_conv_centered(xbc, conv_w, conv_b))
    xs, bm, cm = split_cols(xbc, [SSD_D_INNER, SSD_GROUPS * SSD_STATE, SSD_GROUPS * SSD_STATE])
    xs = xs.reshape(bsz, seq, SSD_HEADS, SSD_HEAD_DIM)
    bm = bm.reshape(bsz, seq, SSD_GROUPS, SSD_STATE)
    cm = cm.reshape(bsz, seq, SSD_GROUPS, SSD_STATE)
    dtf = jax.nn.softplus((dt_f + dt_bias_f).astype(F32))
    dtb = jax.nn.softplus((dt_b + dt_bias_b).astype(F32))
    af = -jnp.exp(a_log_f.astype(F32))
    ab = -jnp.exp(a_log_b.astype(F32))

    def flip(t):
        return jnp.flip(t, axis=1)

    y = ssd_chunked(xs, dtf, af, bm, cm, False) + flip(
        ssd_chunked(flip(xs), flip(dtb), ab, flip(bm), flip(cm), True))
    y = y + xs.astype(F32) * d_skip.astype(F32)[:, None]
    y = y.astype(h.dtype).reshape(bsz, seq, SSD_D_INNER) * jax.nn.silu(z)
    y = rms_norm(y.reshape(bsz, seq, SSD_GROUPS, SSD_D_INNER // SSD_GROUPS),
                 g_norm.reshape(SSD_GROUPS, SSD_D_INNER // SSD_GROUPS))
    return y.reshape(bsz, seq, SSD_D_INNER) @ w_out

def dilated_group(q, k, v, window, dilation):
    bsz, seq, nh, hd = q.shape
    n_side = (window // 2) // dilation
    offsets = dilation * jnp.arange(-n_side, n_side + 1, dtype=jnp.int32)
    nb = seq // Q_BLOCK
    qb = q.reshape(bsz, nb, Q_BLOCK, nh, hd).swapaxes(0, 1)
    starts = jnp.arange(nb, dtype=jnp.int32) * Q_BLOCK
    scale = hd ** -0.5

    def block(args):
        q_blk, start = args
        idx = (start + jnp.arange(Q_BLOCK, dtype=jnp.int32))[:, None] + offsets[None, :]
        valid = (idx >= 0) & (idx < seq)
        idx = jnp.clip(idx, 0, seq - 1)
        kg = k[:, idx]
        vg = v[:, idx]
        s = jnp.einsum('bqhd,bqmhd->bqhm', q_blk, kg).astype(F32) * scale
        s = jnp.where(valid[None, :, None, :], s, -jnp.inf)
        m = jnp.max(s, axis=-1, keepdims=True)
        e = jnp.exp(s - m)
        l = jnp.sum(e, axis=-1, keepdims=True)
        o = jnp.einsum('bqhm,bqmhd->bqhd', (e / l).astype(vg.dtype), vg)
        return o, (m + jnp.log(l))[..., 0]

    o, lse = lax.map(block, (qb, starts))
    return (o.swapaxes(0, 1).reshape(bsz, seq, nh, hd),
            lse.swapaxes(0, 1).reshape(bsz, seq, nh))

def dilated_mixer(h, pos, w_in, g_q, g_k, w_out):
    bsz, seq, _ = h.shape
    qkv = (h @ w_in).reshape(bsz, seq, 3, DIL_GROUPS, DIL_HEADS, DIL_HEAD_DIM)
    q = rms_norm(qkv[:, :, 0], g_q[:, None, :])
    k = rms_norm(qkv[:, :, 1], g_k[:, None, :])
    v = qkv[:, :, 2]
    flat = (bsz, seq, DIL_GROUPS * DIL_HEADS, DIL_HEAD_DIM)
    q = rope(q.reshape(flat), pos).reshape(bsz, seq, DIL_GROUPS, DIL_HEADS, DIL_HEAD_DIM)
    k = rope(k.reshape(flat), pos).reshape(bsz, seq, DIL_GROUPS, DIL_HEADS, DIL_HEAD_DIM)
    outs, lses = [], []
    for gi, (window, dilation) in enumerate(DIL_PAIRS):
        o, lse = dilated_group(q[:, :, gi], k[:, :, gi], v[:, :, gi], window, dilation)
        outs.append(o.astype(F32))
        lses.append(lse)
    wts = jax.nn.softmax(jnp.stack(lses, axis=0), axis=0)
    o = jnp.sum(wts[..., None] * jnp.stack(outs, axis=0), axis=0)
    return o.astype(h.dtype).reshape(bsz, seq, DIL_WIDTH) @ w_out

def second_inputs(seed: int = 0) -> dict:
    key = jax.random.key(seed)
    ks = iter(jax.random.split(key, 48))
    n_a, n_b, n_c, n_d = N_PER_MIXER

    def nrm(shape, std):
        return jax.random.normal(next(ks), shape, F32) * std

    def dense(shape):
        return nrm(shape, shape[-2] ** -0.5)

    def gain(shape):
        return 1.0 + nrm(shape, 0.05)

    x = nrm((BATCH, SEQ, D_MODEL), 1.0)
    p = nrm((DEPTH_2, BATCH, SEQ, PLE_DIM), 1.0)

    def dt_bias(shape):
        dt = jnp.exp(jax.random.uniform(next(ks), shape, F32, math.log(1e-3), math.log(1e-1)))
        return dt + jnp.log(-jnp.expm1(-dt))

    def a_log(shape):
        return jnp.log(jax.random.uniform(next(ks), shape, F32, 1.0, 16.0))

    return {
        'x': x,
        'p': p,
        'norm_mix': gain((DEPTH_2, D_MODEL)),
        'norm_ffn': gain((DEPTH_2, D_MODEL)),
        'ffn_w_in': dense((DEPTH_2, D_MODEL, 2 * D_FF_2)),
        'ffn_w_out': dense((DEPTH_2, D_FF_2, D_MODEL)),
        'ple_norm': gain((DEPTH_2, D_MODEL)),
        'ple_w_gate': dense((DEPTH_2, D_MODEL, D_MODEL)),
        'ple_w_proj': dense((DEPTH_2, PLE_DIM, D_MODEL)),
        'gla_w_in': dense((n_a, D_MODEL, GLA_IN)),
        'gla_w_gate_f': dense((n_a, GLA_RANK, GLA_DK)),
        'gla_b_gate_f': nrm((n_a, GLA_DK), 0.01),
        'gla_w_gate_b': dense((n_a, GLA_RANK, GLA_DK)),
        'gla_b_gate_b': nrm((n_a, GLA_DK), 0.01),
        'gla_g_out': gain((n_a, GLA_HV)),
        'gla_w_out': dense((n_a, GLA_DV, D_MODEL)),
        'diff_w_in': dense((n_b, D_MODEL, DIFF_IN)),
        'diff_g_q': gain((n_b, 2, DIFF_HEAD_DIM)),
        'diff_g_k': gain((n_b, 2, DIFF_HEAD_DIM)),
        'diff_lam_q1': nrm((n_b, DIFF_HEAD_DIM), 0.1),
        'diff_lam_k1': nrm((n_b, DIFF_HEAD_DIM), 0.1),
        'diff_lam_q2': nrm((n_b, DIFF_HEAD_DIM), 0.1),
        'diff_lam_k2': nrm((n_b, DIFF_HEAD_DIM), 0.1),
        'diff_g_sub': gain((n_b, 2 * DIFF_HEAD_DIM)),
        'diff_w_out': dense((n_b, D_MODEL, D_MODEL)),
        'ssd_w_in': dense((n_c, D_MODEL, SSD_IN)),
        'ssd_conv_w': nrm((n_c, SSD_CONV, SSD_CONV_DIM), SSD_CONV ** -0.5),
        'ssd_conv_b': nrm((n_c, SSD_CONV_DIM), 0.01),
        'ssd_dt_bias_f': dt_bias((n_c, SSD_HEADS)),
        'ssd_a_log_f': a_log((n_c, SSD_HEADS)),
        'ssd_dt_bias_b': dt_bias((n_c, SSD_HEADS)),
        'ssd_a_log_b': a_log((n_c, SSD_HEADS)),
        'ssd_d': gain((n_c, SSD_HEADS)),
        'ssd_g_norm': gain((n_c, SSD_D_INNER)),
        'ssd_w_out': dense((n_c, SSD_D_INNER, D_MODEL)),
        'dil_w_in': dense((n_d, D_MODEL, DIL_IN)),
        'dil_g_q': gain((n_d, DIL_GROUPS, DIL_HEAD_DIM)),
        'dil_g_k': gain((n_d, DIL_GROUPS, DIL_HEAD_DIM)),
        'dil_w_out': dense((n_d, DIL_WIDTH, D_MODEL)),
    }

def second_block(x, p, norm_mix, norm_ffn, ffn_w_in, ffn_w_out, ple_norm, ple_w_gate, ple_w_proj,
              gla_w_in, gla_w_gate_f, gla_b_gate_f, gla_w_gate_b, gla_b_gate_b, gla_g_out, gla_w_out,
              diff_w_in, diff_g_q, diff_g_k, diff_lam_q1, diff_lam_k1, diff_lam_q2, diff_lam_k2,
              diff_g_sub, diff_w_out,
              ssd_w_in, ssd_conv_w, ssd_conv_b, ssd_dt_bias_f, ssd_a_log_f, ssd_dt_bias_b,
              ssd_a_log_b, ssd_d, ssd_g_norm, ssd_w_out,
              dil_w_in, dil_g_q, dil_g_k, dil_w_out):
    seq = x.shape[1]
    pos = jnp.arange(seq, dtype=jnp.int32)
    h = x
    for i in range(DEPTH_2):
        kind = i % N_MIXERS
        j = i // N_MIXERS
        hn = rms_norm(h, norm_mix[i])
        if kind == 0:
            mix = gla_mixer(hn, gla_w_in[j], gla_w_gate_f[j], gla_b_gate_f[j], gla_w_gate_b[j],
                            gla_b_gate_b[j], gla_g_out[j], gla_w_out[j])
        elif kind == 1:
            lambda_init = 0.8 - 0.6 * math.exp(-0.3 * i)
            mix = diff_attn_mixer(hn, pos, diff_w_in[j], diff_g_q[j], diff_g_k[j], diff_lam_q1[j],
                                  diff_lam_k1[j], diff_lam_q2[j], diff_lam_k2[j], diff_g_sub[j],
                                  diff_w_out[j], lambda_init)
        elif kind == 2:
            mix = ssd_mixer(hn, ssd_w_in[j], ssd_conv_w[j], ssd_conv_b[j], ssd_dt_bias_f[j],
                            ssd_a_log_f[j], ssd_dt_bias_b[j], ssd_a_log_b[j], ssd_d[j],
                            ssd_g_norm[j], ssd_w_out[j])
        else:
            mix = dilated_mixer(hn, pos, dil_w_in[j], dil_g_q[j], dil_g_k[j], dil_w_out[j])
        h = h + mix
        h = h + swiglu_2(rms_norm(h, norm_ffn[i]), ffn_w_in[i], ffn_w_out[i])
        gate = jax.nn.sigmoid(rms_norm(h, ple_norm[i]) @ ple_w_gate[i])
        h = h + gate * (p[i] @ ple_w_proj[i])
    return h


def setup_inputs(seed=0):
    out = dict(first_inputs(seed))
    for name, value in second_inputs(seed + 1).items():
        if name != "x":
            out[name + "_2"] = value
    return out


def reference(
    x, c, w_ada, b_ada, w_in, conv_w, attn_norm_g, conv_norm_g, w_out, ln1_g, ln1_b, w_gate,
    w_up, w_down, ln2_g, ln2_b, p_2, norm_mix_2, norm_ffn_2, ffn_w_in_2, ffn_w_out_2,
    ple_norm_2, ple_w_gate_2, ple_w_proj_2, gla_w_in_2, gla_w_gate_f_2, gla_b_gate_f_2,
    gla_w_gate_b_2, gla_b_gate_b_2, gla_g_out_2, gla_w_out_2, diff_w_in_2, diff_g_q_2,
    diff_g_k_2, diff_lam_q1_2, diff_lam_k1_2, diff_lam_q2_2, diff_lam_k2_2, diff_g_sub_2,
    diff_w_out_2, ssd_w_in_2, ssd_conv_w_2, ssd_conv_b_2, ssd_dt_bias_f_2, ssd_a_log_f_2,
    ssd_dt_bias_b_2, ssd_a_log_b_2, ssd_d_2, ssd_g_norm_2, ssd_w_out_2, dil_w_in_2, dil_g_q_2,
    dil_g_k_2, dil_w_out_2,
):
    x = first_block(
        x, c, w_ada, b_ada, w_in, conv_w, attn_norm_g, conv_norm_g, w_out, ln1_g, ln1_b, w_gate,
        w_up, w_down, ln2_g, ln2_b,
    )
    return second_block(
        x, p_2, norm_mix_2, norm_ffn_2, ffn_w_in_2, ffn_w_out_2, ple_norm_2, ple_w_gate_2,
        ple_w_proj_2, gla_w_in_2, gla_w_gate_f_2, gla_b_gate_f_2, gla_w_gate_b_2,
        gla_b_gate_b_2, gla_g_out_2, gla_w_out_2, diff_w_in_2, diff_g_q_2, diff_g_k_2,
        diff_lam_q1_2, diff_lam_k1_2, diff_lam_q2_2, diff_lam_k2_2, diff_g_sub_2, diff_w_out_2,
        ssd_w_in_2, ssd_conv_w_2, ssd_conv_b_2, ssd_dt_bias_f_2, ssd_a_log_f_2, ssd_dt_bias_b_2,
        ssd_a_log_b_2, ssd_d_2, ssd_g_norm_2, ssd_w_out_2, dil_w_in_2, dil_g_q_2, dil_g_k_2,
        dil_w_out_2,
    )


_drawn_inputs = setup_inputs


def setup_inputs(seed=0):
    import zlib

    import numpy as np

    out = dict(_drawn_inputs(seed))
    spreads = {}
    factors = {'ple_norm_2': 5.684,
     'gla_b_gate_f_2': 8.0,
     'gla_b_gate_b_2': 8.0,
     'diff_g_q_2': 3.644,
     'diff_g_k_2': 3.703,
     'diff_lam_q1_2': 2.864,
     'diff_lam_k1_2': 5.567,
     'diff_lam_k2_2': 6.176,
     'diff_g_sub_2': 2.796}
    for name, (base, spread) in spreads.items():
        noise = np.random.default_rng([zlib.crc32(name.encode()), seed]).standard_normal(out[name].shape)
        drawn = base * np.exp(spread * noise) if base else spread * noise
        out[name] = jnp.asarray(drawn.astype(out[name].dtype))
    for name, factor in factors.items():
        out[name] = (out[name] * factor).astype(out[name].dtype)
    return out
```

```python
from contextlib import ExitStack

import numpy as np

import concourse.bass as bass
from concourse import mybir

F32 = mybir.dt.float32
F32R = mybir.dt.float32r
ALU = mybir.AluOpType
ACT = mybir.ActivationFunctionType
AX = mybir.AxisListType.X

P = 128
T = 256
D = 1024
KT = D // P
TT = T // P
F = 2816
FT = F // P
HD = 64
NH = 8
IH, ID = 8, 32
TOPK = 64
ALPHA = 2.0 ** 0.25
EPS1, EPS2 = 1e-5, 1e-6
GH, GDK, GDV = 4, 128, 256
CH, NCH = 64, 4
RANK, TAU = 16, 16.0
NEG = -1e30
TAKEN = -3e38
LAMBDA_INIT = 0.8 - 0.6 * float(np.exp(-0.3))
SLAB = 4096

QW = 512
C_K, C_V, C_QI, C_KI, C_WI, C_GB = 512, 576, 640, 896, 928, 936
C_GC, C_HC = C_GB + 512, C_GB + 1024

ROWS_A = [("b_ada", 48), ("ln1_g", 8), ("ln1_b", 8), ("ln2_g", 8), ("ln2_b", 8),
          ("attn_norm_g", 4), ("conv_norm_g", 4), ("conv_w", 12)]
ROWS_B = [("norm_mix_2", 16), ("norm_ffn_2", 16), ("ple_norm_2", 16), ("c", 8), ("gla_b_gate_f_2", 4),
          ("gla_b_gate_b_2", 4), ("gla_g_out_2", 2), ("diff_g_sub_2", 1), ("diff_g_q_2", 1),
          ("diff_g_k_2", 1)]


def column_of(rows):
    at, n = {}, 0
    for name, k in rows:
        at[name] = n
        n += k
    return at, n


COL_A, NA = column_of(ROWS_A)
COL_B, NB = column_of(ROWS_B)

CONSTS = [("ident", P), ("blk", P), ("rot_q", P), ("rot_i", P), ("rot_d", P), ("cos_q", T), ("sin_q", T),
          ("cos_i", T), ("sin_i", T), ("cos_d", T), ("sin_d", T), ("causal", 3 * P), ("gla_mask", 2 * P)]
COL_C, NC = column_of(CONSTS)


def shape_constants():
    out = np.zeros((P, NC), np.float32)

    def put(name, a):
        out[:, COL_C[name]:COL_C[name] + a.shape[1]] = a

    p = np.arange(P)
    put("ident", np.eye(P))
    put("blk", (p[:, None] // HD == p[None, :] // HD) * 1.0)
    pos = np.arange(T, dtype=np.float32)
    for tag, width, half, theta in (("q", HD, 8, 500000.0), ("i", ID, 8, 500000.0), ("d", HD, 32, 10000.0)):
        rot = np.zeros((P, P))
        cos, sin = np.ones((P, T)), np.zeros((P, T))
        inv = (theta ** (-(np.arange(half) * 2.0) / (2 * half))).astype(np.float32)
        ang = (pos[None, :] * inv[:, None]).astype(np.float32).astype(np.float64)
        for m in range(P):
            d = m % width
            if d < 2 * half:
                rot[m + half if d < half else m - half, m] = -1.0 if d < half else 1.0
                cos[m], sin[m] = np.cos(ang[d % half]), np.sin(ang[d % half])
        put("rot_" + tag, rot)
        put("cos_" + tag, cos)
        put("sin_" + tag, sin)
    tri = np.where(p[None, :] <= p[:, None], 0.0, NEG)
    put("causal", np.concatenate([tri, np.zeros((P, P)), tri], 1))
    same = p[:, None] // CH == p[None, :] // CH
    put("gla_mask", np.concatenate([same & (p[:, None] <= p[None, :]), same & (p[:, None] > p[None, :])], 1) * 1.0)
    return out


class Phase:

    def __init__(self, name, n, cols, tiles, dmas, split=True, loop=False, ahead=True):
        self.name, self.n, self.cols, self.tiles, self.dmas = name, n, cols, tiles, dmas
        self.split, self.loop, self.ahead = split, loop, ahead


def plan():
    ffn = lambda k: [Phase(f"gate_up{k}", FT // 2, SLAB, 4, 2, loop=True), Phase(f"down{k}", KT, F, 1, 2, loop=True)]
    ple = lambda k: [Phase(f"ple_proj{k}", 1, 2048, 8, 1), Phase(f"ple_gate{k}", 2, SLAB, 4, 1)]
    phases = [
        Phase("ada_a", 4, SLAB, 0, 1, split=False, ahead=False),
        Phase("in_q", 1, SLAB, 4, 1), Phase("in_idx", 1, SLAB, 4, 7), Phase("in_v", 1, 8 * 72, 2, 2),
        Phase("in_gc", 1, SLAB, 4, 1), Phase("in_hc", 1, SLAB, 4, 1), Phase("in_gb", 1, SLAB, 4, 1, ahead=False),
        Phase("ada_b", 8, SLAB, 0, 1, split=False, ahead=False),
        Phase("out0", 2, SLAB, 4, 1), *ffn(0),
        Phase("gla_z", 1, 8 * 2 * RANK, 0, 1, split=False), Phase("gla_q", 1, SLAB, 4, 1),
        Phase("gla_k", 1, SLAB, 4, 1), Phase("gla_v", 2, SLAB, 2, 1), Phase("gla_r", 2, SLAB, 4, 1),
        Phase("out1", 2, SLAB, 4, 1), *ffn(1), *ple(1),
        Phase("diff_q", 2, SLAB, 4, 1), Phase("diff_k", 2, SLAB, 4, 1), Phase("diff_v", 2, SLAB, 2, 1),
        Phase("out2", 2, SLAB, 4, 1), *ffn(2), *ple(2),
    ]
    slabs = []
    j = plain = tile = 0
    slot_dmas = [0, 0]
    for ph in phases:
        ph.s0, ph.j0, ph.tile0, ph.plain0 = len(slabs), j, tile, plain
        ph.landed, ph.free = [], []
        for _ in range(ph.n):
            s = len(slabs)
            slot_dmas[s % 2] += ph.dmas
            ph.landed.append(16 * slot_dmas[s % 2])
            ph.free.append(slabs[s - 2] if s >= 2 else None)
            j, plain, tile = j + ph.split, plain + (not ph.split), tile + ph.tiles
            slabs.append((ph.split, 4 * j if ph.split else plain))
    for n, ph in enumerate(phases):
        ph.next = next((q for q in phases[n + 1:] if q.split), None) if ph.ahead else None
    return phases


PHASES = plan()
PH = {ph.name: ph for ph in PHASES}


class At:

    def __init__(self, i, it=None, b=None):
        self.i, self.it, self.b = i, it, b
        self.parity = i % 2 if it is None else (1 + b) % 2

    def of(self, values):
        if self.it is None:
            return values[self.i]
        step = values[3 + self.b] - values[1 + self.b]
        return self.it * step + values[1 + self.b]

    def lin(self, base, per):
        return base + self.i * per if self.it is None else self.it * (2 * per) + (base + (1 + self.b) * per)


def rounds(eng, ph, body):
    pairs = (ph.n - 2) // 2 if ph.loop else 0
    if not pairs:
        for i in range(ph.n):
            body(At(i))
        return
    body(At(0))
    with eng.Fori(0, pairs) as it:
        for b in range(2):
            body(At(it * 2 + (1 + b), it, b))
    for i in range(1 + 2 * pairs, ph.n):
        body(At(i))


def wait(eng, sem, value):
    if not isinstance(value, int) or value > 0:
        eng.wait_ge(sem, value)


class Steps:

    def __init__(self, eng, own):
        self.eng, self.own, self.n = eng, own, {}

    def seen(self, sem, k=1):
        self.n[sem.name] = self.n.get(sem.name, 0) + k

    def next(self, sem, k=1):
        self.seen(sem, k)
        self.eng.wait_ge(sem, self.n[sem.name])

    def again(self, sem=None, less=0):
        sem = sem or self.own
        wait(self.eng, sem, self.n.get(sem.name, 0) - less)

    def did(self, ins, sem=None):
        sem = sem or self.own
        self.seen(sem)
        ins.then_inc(sem, 1)

    def link(self, ins, sem=None):
        self.did(ins, sem)
        self.again(sem)


class Banks:

    def __init__(self, pe):
        self.pe, self.n, self.last = pe, {}, {}

    def settle(self, b):
        if b.name in self.last:
            self.pe.wait_ge(*self.last[b.name])

    def claim(self, b, sem):
        self.settle(b)
        self.n[sem.name] = self.n.get(sem.name, 0) + 1
        self.last[b.name] = (sem, self.n[sem.name])
        return self.n[sem.name]

    def skip(self, b, sem, total):
        self.n[sem.name] = max(self.n.get(sem.name, 0), total)
        self.last[b.name] = (sem, total)


def build(nc, a, out, stop=None):
    ctx = ExitStack()
    with ctx:
        BASE = 16640
        ARENA = 53168
        ctx.enter_context(nc.sbuf_tensor("arena", [P, (BASE - nc.sbuf_base + 3) // 4 + ARENA], F32))
        taken = [0]
        place = {}

        def sb(name, words, dt=F32, at=None):
            o = taken[0] if at is None else at
            if at is None:
                taken[0] += (words + 7) // 8 * 8
            assert o + words <= ARENA, (name, o + words)
            place[name] = o
            return nc.alloc_sbuf_tensor_at(name, [P, words], dt, offset=BASE + 4 * o)

        raw = [sb(f"raw{i}", SLAB) for i in range(2)]
        whi = [sb(f"whi{i}", SLAB, F32R) for i in range(2)]
        wlo = [sb(f"wlo{i}", SLAB, F32R) for i in range(2)]
        const = sb("const", NC)
        ones = sb("ones", P)
        cols_a, cols_b = sb("cols_a", NA), sb("cols_b", NB)
        mod = sb("mod", 48)
        fold = sb("fold", 48)
        c_act = sb("c_act", 8)
        lam_in = sb("lam_in", 4 * HD)
        lam = sb("lam", 8)
        eps = sb("eps", 2)
        top8 = sb("top8", 16)
        neg_max = sb("neg_max", 2 * 4)
        sums = sb("sums", 2 * 4)
        rsum = sb("rsum", 2 * 4)
        decay = sb("decay", 32)
        total = sb("total", 32)
        wgate = sb("wgate", 512)
        res = sb("res", KT * T)
        om = sb("om", KT * T)
        ohi, olo = sb("ohi", KT * T, F32R), sb("olo", KT * T, F32R)
        p_hi, p_lo = sb("p_hi", 2 * 2 * T, F32R), sb("p_lo", 2 * 2 * T, F32R)
        mean = sb("mean", T)
        sd = sb("sd", T + 2)
        rstd = sb("rstd", T + 2)
        work = sb("work", 2048)
        acthi, actlo = sb("acthi", FT * T, F32R), sb("actlo", FT * T, F32R)
        U = place["acthi"]

        xin, pin = sb("xin", 2048, at=U), sb("pin", 1024, at=U + 2048)
        rows_a, rows_b = sb("rows_a", P, at=U + 3072), sb("rows_b", P, at=U + 3200)
        sq, pp = sb("sq", 2048, at=U), sb("pp", 2048, at=U + 4096)
        rope_in, rope_out = sb("rope_in", 2048, at=U), sb("rope_out", 2048, at=U + 2048)
        vtok = sb("vtok", 2 * 72, at=U + 4096)
        gc = sb("gc", 4 * T, at=U + 4352)
        upad = sb("upad", 4 * (T + 2), at=U + 5376)
        conv = sb("conv", 4 * T, at=U + 6408)
        mixed = sb("mixed", KT * T, at=U + 7432)
        relu = sb("relu", 2 * 384, at=U + 9480)
        score, kept = sb("score", 384, at=U + 10248), sb("kept", 384, at=U + 10632)
        mix_sq = sb("mix_sq", KT * T, at=U)
        W = place["work"]
        allow = sb("allow", 384, at=W)
        logit = sb("logit", 2 * 384, at=W + 384)
        prob_t = sb("prob_t", 2 * 384, at=W + 1152)
        gt, sg = sb("gt", 2 * T, at=W), sb("sg", 2 * T, at=W + 512)
        ut, prod = sb("ut", 2 * T, at=W + 1024), sb("prod", 2 * T, at=W + 1536)
        g_q, g_k = sb("g_q", 1024, at=U), sb("g_k", 1024, at=U + 1024)
        g_o = sb("g_o", 2048, at=U)
        g_v, g_r = sb("g_v", 2048, at=U + 2048), sb("g_r", 2048, at=U + 4096)
        g_la = [sb(f"g_la{d}", 1024, at=U + 6144 + 1024 * d) for d in range(2)]
        g_b = [sb(f"g_b{d}", 1024, at=U + 8192 + 1024 * d) for d in range(2)]
        g_ke = [sb(f"g_ke{d}", 1024, at=W + 1024 * d) for d in range(2)]
        g_m, g_st = sb("g_m", 512, at=U + 10240), sb("g_st", 512, at=U + 10752)
        g_sq = sb("g_sq", 2048, at=U + 6144)
        g_rs = sb("g_rs", 1024, at=U + 8192)
        O = place["om"]
        seg = [sb(f"seg{d}", 1024, at=O + 1024 * d) for d in range(2)]
        state, kd_tok = sb("state", 1536, at=O), sb("kd_tok", 512, at=O + 1536)
        g_z = sb("g_z", T, at=place["mean"])
        d_q, d_k = sb("d_q", 2048, at=U), sb("d_k", 2048, at=U + 2048)
        d_v, d_o = sb("d_v", 2048, at=U + 4096), sb("d_o", 2048, at=U + 6144)
        d_p, d_pt = sb("d_p", 2048, at=U + 8192), sb("d_pt", 1024, at=U + 10240)
        d_sq, d_rs = sb("d_sq", 1024, at=U + 8192), sb("d_rs", 1024, at=U + 9216)
        d_t1, d_t2 = sb("d_t1", 512, at=U + 10240), sb("d_t2", 512, at=U + 10752)
        d_nsq = sb("d_nsq", 2048, at=U)
        o_tok = sb("o_tok", 2048, at=O)

        G = [ctx.enter_context(nc.psum_tensor(f"gemm{i}", [P, 512], F32)) for i in range(4)]
        X = [ctx.enter_context(nc.psum_tensor(f"aux{i}", [P, 512], F32)) for i in range(4)]

        def sem(name):
            return ctx.enter_context(nc.semaphore(name))

        landed = [sem("landed0"), sem("landed1")]
        params_in, gates_in, const_in, x_in = sem("params_in"), sem("gates_in"), sem("const_in"), sem("x_in")
        set_zero = sem("set_zero")
        hi_ready, lo_ready = sem("hi_ready"), sem("lo_ready")
        plain_used = sem("plain_used")
        tile_done = sem("tile_done")
        dve_read = sem("dve_read")
        act_step, dve_step, pool_step = sem("act_step"), sem("dve_step"), sem("pool_step")
        setup_t, cols_ready, c_ready = sem("setup_t"), sem("cols_ready"), sem("c_ready")
        lam_sum, lam_exp = sem("lam_sum"), sem("lam_exp")
        om_ready, ohi_ready, olo_ready = sem("om_ready"), sem("ohi_ready"), sem("olo_ready")
        sq_ready, stat_done, sd_ready = sem("sq_ready"), sem("stat_done"), sem("sd_ready")
        mean_done, mean_ready, centered, normed, res_ready = (
            sem("mean_done"), sem("mean_ready"), sem("centered"), sem("normed"), sem("res_ready"))
        rope_src, rope_cos, rot_done, rot_read, roped = (
            sem("rope_src"), sem("rope_cos"), sem("rot_done"), sem("rot_read"), sem("roped"))
        v_src, gc_ready, idx_done, relu_done, idx_acc = (
            sem("v_src"), sem("gc_ready"), sem("idx_done"), sem("relu_done"), sem("idx_acc"))
        mixed_ready, mod_read = sem("mixed_ready"), sem("mod_read")
        score_done, score_read, max_ready, exp_done, prob_ready = (
            sem("score_done"), sem("score_read"), sem("max_ready"), sem("exp_done"), sem("prob_ready"))
        trans_done, pt_ready, pv_done, pv_read = sem("trans_done"), sem("pt_ready"), sem("pv_done"), sem("pv_read")
        gate_in, up_in, silu_done, prod_done, acthi_ready, actlo_ready = (
            sem("gate_in"), sem("up_in"), sem("silu_done"), sem("prod_done"), sem("acthi_ready"), sem("actlo_ready"))
        pp_ready, ple_in, ple_sig, ple_prod = sem("pp_ready"), sem("ple_in"), sem("ple_sig"), sem("ple_prod")
        ple_added = sem("ple_added")
        z_ready, la_done, la_read, lg_ready, seg_ready, b_ready = (
            sem("z_ready"), sem("la_done"), sem("la_read"), sem("lg_ready"), sem("seg_ready"),
            sem("b_ready"))
        dist_ready, grow_ready, fall_ready, kd_ready, v_ready, r_ready, r_act = (
            sem("dist_ready"), sem("grow_ready"), sem("fall_ready"), sem("kd_ready"), sem("v_ready"),
            sem("r_ready"), sem("r_act"))
        ke_ready = sem("ke_ready")
        gs_done, gs_read, st_ready, kt_done, kt_ready, u_done, u_read, go_done, go_read, gated = (
            sem("gs_done"), sem("gs_read"), sem("st_ready"), sem("kt_done"), sem("kt_ready"), sem("u_done"),
            sem("u_read"), sem("go_done"), sem("go_read"), sem("gated"))
        qk_src, qk_sq, qk_stat, qk_sd, qk_normed, qk_cos, qk_rot, qk_rot_read, qk_ready = (
            sem("qk_src"), sem("qk_sq"), sem("qk_stat"), sem("qk_sd"), sem("qk_normed"), sem("qk_cos"),
            sem("qk_rot"), sem("qk_rot_read"), sem("qk_ready"))
        out_done, out_read, stored = sem("out_done"), sem("out_read"), sem("stored")

        def C(name, n=P):
            return const[:, COL_C[name]:COL_C[name] + n]

        def A(name, t=0, n=1):
            return cols_a[:, COL_A[name] + t:COL_A[name] + t + n]

        def B(name, t=0, n=1):
            return cols_b[:, COL_B[name] + t:COL_B[name] + t + n]

        def tl(buf, t, n=1, w=T):
            if isinstance(t, int):
                return buf[:, t * w:(t + n) * w]
            return buf[:, bass.ds(t * w, n * w)]

        def bc(ap, n):
            w = ap.shape[1]
            return ap.rearrange("p (r n) -> p r n", r=1).to_broadcast([P, n, w])

        def v3(ap, n):
            return ap.rearrange("p (r n) -> p r n", r=n)

        ident = C("ident")

        def kmaj(w, c0, n, i=0):
            v = w.rearrange("(k p) n -> p k n", p=P)
            return v[:, :, c0 + i * n:c0 + (i + 1) * n] if isinstance(i, int) else v[:, :, bass.ds(i * n + c0, n)]

        def flat(slot, k, n):
            return raw[slot][:, 0:k * n].rearrange("p (k n) -> p k n", k=k)

        w_in, ada = a["w_in"][0], a["w_ada"][0]
        gla_in, diff_in = a["gla_w_in_2"][0], a["diff_w_in_2"][0]

        def columns(w, c0):
            return lambda i, slot: [(flat(slot, KT, 512), kmaj(w, c0, 512, i))]

        def gate_up(wg, cg, wu, cu):
            def srcs(i, slot):
                v = raw[slot][:, :].rearrange("p (k g n) -> p k g n", k=KT, g=2)
                return [(v[:, :, 0, :], kmaj(wg, cg, 256, i)), (v[:, :, 1, :], kmaj(wu, cu, 256, i))]
            return srcs

        def down(w):
            def srcs(i, slot):
                v, s, h = flat(slot, FT, P), kmaj(w, 0, P, i), FT // 2
                return [(v[:, 0:h, :], s[:, 0:h, :]), (v[:, h:FT, :], s[:, h:FT, :])]
            return srcs

        def idx_slab(i, slot):
            v = flat(slot, KT, 512)
            return ([(v[:, :, 0:256], kmaj(w_in, C_QI, 256))]
                    + [(v[:, :, 256 + 32 * r:288 + 32 * r], kmaj(w_in, C_KI, ID)) for r in range(4)]
                    + [(v[:, :, 384 + 64 * r:448 + 64 * r], kmaj(w_in, C_K, HD)) for r in range(2)])

        def v_slab(i, slot):
            v = flat(slot, KT, 72)
            return [(v[:, :, 0:64], kmaj(w_in, C_V, HD)), (v[:, :, 64:72], kmaj(w_in, C_WI, IH))]

        sources = {
            "ada_a": columns(ada, 0), "ada_b": columns(ada, 2048),
            "in_q": columns(w_in, 0), "in_idx": idx_slab, "in_v": v_slab,
            "in_gc": columns(w_in, C_GC), "in_hc": columns(w_in, C_HC), "in_gb": columns(w_in, C_GB),
            "out0": columns(a["w_out"][0], 0),
            "gate_up0": gate_up(a["w_gate"][0], 0, a["w_up"][0], 0), "down0": down(a["w_down"][0]),
            "gla_z": lambda i, slot: [(flat(slot, KT, 32), kmaj(gla_in, 3072, 32))],
            "gla_q": columns(gla_in, 0), "gla_k": columns(gla_in, 512), "gla_v": columns(gla_in, 1024),
            "gla_r": columns(gla_in, 2048), "out1": columns(a["gla_w_out_2"][0], 0),
            "diff_q": columns(diff_in, 0), "diff_k": columns(diff_in, 1024), "diff_v": columns(diff_in, 2048),
            "out2": columns(a["diff_w_out_2"][0], 0),
        }
        for k in (1, 2):
            f_in, w_p = a["ffn_w_in_2"][k - 1], a["ple_w_proj_2"][k - 1]
            sources[f"gate_up{k}"] = gate_up(f_in, 0, f_in, F)
            sources[f"down{k}"] = down(a["ffn_w_out_2"][k - 1])
            sources[f"ple_proj{k}"] = lambda i, slot, w_p=w_p: [(flat(slot, 2, D), kmaj(w_p, 0, D))]
            sources[f"ple_gate{k}"] = columns(a["ple_w_gate_2"][k - 1], 0)

        def on(name):
            return stop is None or PH[name].s0 < PH[stop].s0

        def bank_of(ph, at, t):
            if ph.tiles == 2:
                return (G[t], 72) if ph.name == "in_v" else (G[2 * at.parity + t], 512)
            return G[{1: at.parity, 4: t, 8: t % 4}[ph.tiles]], T

        def quarters(ph, t):
            return {1: (0, 1, 2, 3), 2: (2 * t, 2 * t + 1), 4: (t,), 8: () if t % 2 else (t // 2,)}[ph.tiles]

        def follow(ph, at):
            if at.it is not None:
                return ph, At(at.i + 1, at.it, at.b + 1)
            if at.i + 1 < ph.n:
                return ph, At(at.i + 1)
            return (ph.next, At(0)) if ph.next else None

        block = ctx.enter_context(nc.Block())

        @block.sync
        def _(sp):
            for ph in PHASES:
                if not on(ph.name):
                    break

                def load(at, ph=ph):
                    slot = (ph.s0 + at.parity) % 2
                    if ph.free[0 if at.it is not None else at.i] is not None:
                        split = {f[0] for f in ph.free} if at.it is not None else {ph.free[at.i][0]}
                        assert len(split) == 1
                        sp.wait_ge(lo_ready if split.pop() else plain_used,
                                   at.of([f[1] if f else 0 for f in ph.free]))
                    for dst, src in sources[ph.name](at.i, slot):
                        sp.dma_start(dst, src).then_inc(landed[slot], 16)

                rounds(sp, ph, load)
            if stop is None:
                for tt in range(TT):
                    sp.wait_ge(out_read, 2 * (tt + 1))
                    sp.dma_start(out[0, tt * P:(tt + 1) * P, :], tl(o_tok, tt, w=D)).then_inc(stored, 16)
                sp.wait_ge(stored, 16 * TT)

        @block.gpsimd
        def _(pool):
            me = Steps(pool, pool_step)
            me.did(pool.memset(ones[:, :], 1.0), set_zero)
            me.did(pool.memset(eps[:, 0:1], EPS1), set_zero)
            me.did(pool.memset(eps[:, 1:2], EPS2), set_zero)

            for r, (src, tiles, cos) in enumerate([(2, (0, 1), "cos_q"), (4, (2, 3), "cos_q"), (8, (4, 7), None),
                                                   (8, (5, 6), "cos_i")]):
                if not on("in_v"):
                    break
                pool.wait_ge(rope_src, src)
                if r == 0:
                    pool.wait_ge(const_in, 16)
                if cos:
                    me.did(pool.tensor_tensor(v3(tl(rope_out, tiles[0], 2), 2), v3(tl(rope_in, tiles[0], 2), 2),
                                              bc(C(cos, T), 2), ALU.mult), rope_cos)
                else:
                    pool.tensor_tensor(tl(rope_out, 4), tl(rope_in, 4), C("cos_q", T), ALU.mult)
                    me.did(pool.tensor_tensor(tl(rope_out, 7), tl(rope_in, 7), C("cos_i", T), ALU.mult), rope_cos)

            def ffn(k):
                ph = PH[f"gate_up{k}"]
                n0 = FT * k

                def body(at):
                    for j in range(2):
                        n = at.lin(n0 + j, 2)
                        t = at.lin(j, 2)
                        wait(pool, silu_done, n + 1)
                        wait(pool, up_in, n + 1)
                        wait(pool, actlo_ready, n - 1)
                        pool.tensor_tensor(tl(prod, j), tl(sg, j), tl(ut, j), ALU.mult).then_inc(prod_done, 1)
                        if not (isinstance(t, int) and t == 0):
                            wait(pool, acthi_ready, n)
                            pool.tensor_tensor(tl(actlo, t - 1), tl(prod, 1 - j), tl(acthi, t - 1).bitcast(F32),
                                               ALU.subtract).then_inc(actlo_ready, 1)

                rounds(pool, ph, body)
                wait(pool, acthi_ready, n0 + FT)
                pool.tensor_tensor(tl(actlo, FT - 1), tl(prod, 1), tl(acthi, FT - 1).bitcast(F32),
                                   ALU.subtract).then_inc(actlo_ready, 1)

            def ple(k):
                for t in range(KT):
                    me.next(ple_sig)
                    if t == 0:
                        me.next(pp_ready, KT)
                    if t >= 2:
                        pool.wait_ge(ple_added, KT * (k - 1) + t - 1)
                    me.did(pool.tensor_tensor(tl(prod, t % 2), tl(sg, t % 2), tl(pp, t), ALU.mult), ple_prod)

            if on("gate_up0"):
                ffn(0)
            if on("gla_z"):
                pool.wait_ge(z_ready, 1)
                for d in range(2):
                    me.link(pool.memset(seg[d][:, :], 1.0))
                    edge = 0 if d == 0 else CH - 1
                    me.did(pool.memset(v3(seg[d][:, :], 16)[:, :, edge:edge + 1], 0.0), seg_ready)
            if on("gla_r"):
                for d in range(2):
                    pool.wait_ge(grow_ready, 2 * d + 2)
                    me.did(pool.tensor_tensor(g_ke[d][:, :], g_k[:, :], g_ke[d][:, :], ALU.mult), ke_ready)
            if on("out1"):
                for h in range(GH):
                    pool.wait_ge(go_read, h + 1)
                    pool.wait_ge(r_act, 2)
                    me.did(pool.tensor_tensor(tl(g_r, 2 * h, 2), tl(g_o, 2 * h, 2), tl(g_r, 2 * h, 2), ALU.mult), gated)
            if on("gate_up1"):
                ffn(1)
            if on("ple_proj1"):
                ple(1)
            if on("diff_v"):
                for r in range(8):
                    me.next(qk_normed)
                    buf, t = (d_q, 2 * r) if r < 4 else (d_k, 2 * r - 8)
                    if r >= 1:
                        pool.wait_ge(qk_ready, r)
                    me.did(pool.tensor_tensor(v3(d_t1[:, :], 2), v3(tl(buf, t, 2), 2), bc(C("cos_d", T), 2),
                                              ALU.mult), qk_cos)
            if on("gate_up2"):
                ffn(2)
            if on("ple_proj2"):
                ple(2)

        @block.scalar
        def _(act):
            me = Steps(act, act_step)

            act.dma_start(const[:, :], a["shape_constants"]).then_inc(const_in, 16)
            act.dma_start(v3(xin[:, :], 2), a["x"][0].rearrange("(t p) n -> p t n", p=P)).then_inc(x_in, 16)
            act.dma_start(pin[:, :].rearrange("p (l t n) -> p l t n", l=2, t=2),
                          a["p_2"].rearrange("l b (t p) n -> p l (b t) n", p=P)).then_inc(x_in, 16)
            for rows, spec in ((rows_a, ROWS_A), (rows_b, ROWS_B)):
                n = 0
                for name, k in spec:
                    ap = a[name]
                    flat_ap = ap.rearrange(" ".join("abc"[:len(ap.shape)]) + " -> (" + " ".join("abc"[:len(ap.shape)]) + ")")
                    act.dma_start(rows[n:n + k, :], flat_ap.rearrange("(r n) -> r n", n=P)).then_inc(params_in, 16)
                    n += k
            for n, name in enumerate(("diff_lam_q1_2", "diff_lam_k1_2", "diff_lam_q2_2", "diff_lam_k2_2")):
                act.dma_start(lam_in[:, n * HD:(n + 1) * HD], a[name].to_broadcast([P, HD])).then_inc(params_in, 16)
            act.dma_start(wgate[0:RANK, :], a["gla_w_gate_f_2"][0]).then_inc(gates_in, 16)
            act.dma_start(wgate[32:32 + RANK, :], a["gla_w_gate_b_2"][0]).then_inc(gates_in, 16)
            act.wait_ge(cols_ready, 1)
            me.did(act.activation(c_act[:, :], B("c", 0, 8), ACT.Silu), c_ready)
            act.wait_ge(lam_sum, 1)
            me.did(act.activation(lam[:, 2:4], lam[:, 0:2], ACT.Exp), lam_exp)

            def split(ph, at, q):
                slot, w = (ph.s0 + at.parity) % 2, ph.cols // 4
                hslot = (ph.j0 + at.parity) % 2
                if q == 0:
                    act.wait_ge(landed[slot], at.of(ph.landed))
                act.activation(whi[hslot][:, q * w:(q + 1) * w], raw[slot][:, q * w:(q + 1) * w],
                               ACT.Copy).then_inc(hi_ready, 1)

            def ahead(ph, at, q):
                nxt = follow(ph, at)
                if nxt is None or not on(nxt[0].name):
                    return
                if q == 0:
                    wait(act, tile_done, at.lin(ph.tile0, ph.tiles))
                split(*nxt, q)

            def prep(order=range(KT), free=None, squares=False, then=None):
                if free:
                    wait(act, tile_done, free)
                for t in order:
                    me.next(om_ready)
                    me.did(act.activation(tl(ohi, t), tl(om, t), ACT.Copy), ohi_ready)
                    if then:
                        then(t)
                    if squares:
                        me.did(act.activation(tl(sq, t), tl(res, t), ACT.Square), sq_ready)

            def root(bank, n, scale, e, dst, done=stat_done, ready=sd_ready):
                me.next(done)
                me.did(act.activation(dst, bank[:, 0:n], ACT.Sqrt, bias=eps[:, e:e + 1], scale=scale), ready)

            def group_root(groups, src, buf, scale, e, banks):
                for n, g in enumerate(groups):
                    me.next(mixed_ready, 2)
                    me.did(act.activation(tl(buf, 2 * g, 2), tl(src, 2 * g, 2), ACT.Square), sq_ready)
                for n, g in enumerate(groups):
                    root(banks[n % len(banks)], 512, scale, e, tl(buf, 2 * g, 2))

            act.wait_ge(set_zero, 3)
            if on("in_q"):
                for q in range(4):
                    split(PH["in_q"], At(0), q)
                prep()

            def evac(dst_of, sem_, scale_of=None):
                def one(ph, at, t):
                    wait(act, tile_done, at.lin(ph.tile0 + t + 1, ph.tiles))
                    bank, n = bank_of(ph, at, t)
                    kw = {"scale": scale_of(t)} if scale_of else {}
                    me.did(act.activation(dst_of(at, t), bank[:, 0:n], ACT.Copy, **kw), sem_)
                return one

            def gemm(name, one=None, after=None):
                if not on(name):
                    return
                ph = PH[name]

                def body(at):
                    for t in range(ph.tiles):
                        for q in quarters(ph, t):
                            ahead(ph, at, q)
                        if one:
                            one(ph, at, t)
                        if after:
                            after(at, t)

                rounds(act, ph, body)

            gemm("in_q", evac(lambda at, t: tl(rope_in, t), rope_src))
            gemm("in_idx", evac(lambda at, t: tl(rope_in, (5, 6, 7, 4)[t]), rope_src))
            gemm("in_v", evac(lambda at, t: vtok[:, 72 * t:72 * t + 72], v_src))
            gemm("in_gc", evac(lambda at, t: tl(gc, t), gc_ready))
            if on("in_hc"):
                for h in range(IH):
                    me.next(idx_done)
                    if h >= 2:
                        act.wait_ge(idx_acc, 2 * (h - 1))
                    me.did(act.activation(tl(relu, h % 2, w=384), G[h % 4][:, 0:384], ACT.Relu), relu_done)
            gemm("in_hc")
            gemm("in_gb")
            if on("ada_b"):
                group_root((2, 3), mixed, mix_sq, 1.0 / HD, 0, X[0:2])
                prep(order=(4, 5, 6, 7), free=PH["in_gb"].tile0 + 4)
                for i in range(NH + 1):
                    if i < NH:
                        me.next(max_ready)
                        for qt, (c0, n) in enumerate(((0, P), (P, 2 * P))):
                            ap = logit[:, 384 * (i % 2) + c0:384 * (i % 2) + c0 + n]
                            ins = act.activation(ap, ap, ACT.Exp, bias=neg_max[:, 2 * (i % 2) + qt:2 * (i % 2) + qt + 1],
                                                 accum_out=sums[:, 2 * (i % 2) + qt:2 * (i % 2) + qt + 1])
                        me.did(ins, exp_done)
                    if i >= 1:
                        me.next(trans_done)
                        if i >= 3:
                            act.wait_ge(pv_done, i - 2)
                        me.did(act.activation(tl(prob_t, (i - 1) % 2, w=384), G[2 + (i - 1) % 2][:, 0:384],
                                              ACT.Copy), pt_ready)
            if on("out0"):
                for q in range(4):
                    split(PH["out0"], At(0), q)
                group_root((0, 1), mixed, mix_sq, 1.0 / HD, 0, X[0:2])
                prep(order=(0, 1, 2, 3))
            gemm("out0")

            def layer_norm(n, squares):
                for t in range(0, KT, 2):
                    me.next(centered)
                    me.did(act.activation(tl(sq, t, 2), tl(res, t, 2), ACT.Square), sq_ready)
                root(X[1], T, 1.0 / D, 0, sd[:, 0:T])
                g, b = (fold[:, 16:24], fold[:, 24:32]) if n == 0 else (A("ln2_g", 0, 8), A("ln2_b", 0, 8))

                def then(t):
                    me.link(act.activation(tl(res, t), tl(res, t), ACT.Identity, bias=b[:, t:t + 1],
                                           scale=g[:, t:t + 1]), res_ready)
                prep(free=PH["out0" if n == 0 else "down0"].tile0 + 8, squares=squares, then=then)

            def ffn(k):
                if not on(f"gate_up{k}"):
                    return
                n0 = FT * k

                def high(n, t, j):
                    wait(act, prod_done, n + 1)
                    act.activation(tl(acthi, t), tl(prod, j), ACT.Copy).then_inc(acthi_ready, 1)

                def after(at, t):
                    if t % 2 == 0:
                        return
                    j = t // 2
                    n, m = at.lin(n0 + j, 2), at.lin(j, 2)
                    wait(act, gate_in, n + 1)
                    wait(act, prod_done, n - 1)
                    act.activation(tl(sg, j), tl(gt, j), ACT.Silu).then_inc(silu_done, 1)
                    if not (isinstance(m, int) and m == 0):
                        high(n - 1, m - 1, 1 - j)

                gemm(f"gate_up{k}", after=after)
                high(n0 + FT - 1, FT - 1, 1)
                gemm(f"down{k}")

            if on("gate_up0"):
                layer_norm(0, False)
            ffn(0)
            if on("gla_z"):
                layer_norm(1, True)
                root(X[0], T + 2, 1.0 / D, 1, sd[:, :])
            gemm("gla_q")
            gemm("gla_k")
            if on("gla_v"):
                for d in range(2):
                    act.wait_ge(la_read, 2 * d + 2)
                    me.link(act.activation(g_b[d][:, :], g_la[d][:, :], ACT.Abs))
                    me.link(act.activation(g_b[d][:, :], g_b[d][:, :], ACT.Exp, scale=-1.0))
                    me.did(act.activation(g_b[d][:, :], g_b[d][:, :], ACT.Ln, bias=ones[:, 0:1]), lg_ready)

            def v_dst(buf):
                return lambda at, t: buf[:, t * D + at.i * 512:t * D + at.i * 512 + 512]

            v_scale = lambda t: rstd[:, T + t:T + t + 1]
            if on("gla_v"):
                act.wait_ge(z_ready, 1)
            ph = PH["gla_v"]
            v_evac = evac(v_dst(g_v), v_ready, v_scale)

            def gla_after(at, t):
                if at.i == 1 and t == 0:
                    for d in range(2):
                        me.next(b_ready)
                        me.did(act.activation(g_la[d][:, :], g_b[d][:, :], ACT.Exp, scale=1.0 / TAU), grow_ready)
                        me.did(act.activation(g_ke[d][:, :], g_b[d][:, :], ACT.Exp, scale=-1.0 / TAU), grow_ready)
                if at.i == 1 and t == 1:
                    for d in range(2):
                        me.next(dist_ready)
                        me.did(act.activation(g_b[d][:, :], g_b[d][:, :], ACT.Exp, scale=1.0 / TAU), fall_ready)

            gemm("gla_v", v_evac, gla_after)
            gemm("gla_r")
            if on("out1"):
                for d in range(2):
                    act.wait_ge(r_ready, 4 * (d + 1))
                    me.did(act.activation(tl(g_r, 4 * d, 4), tl(g_r, 4 * d, 4), ACT.Silu), r_act)
                for h in range(GH):
                    me.next(kt_done)
                    me.did(act.activation(kd_tok[:, :], G[1][:, :], ACT.Copy), kt_ready)
                for h in range(GH):
                    act.wait_ge(go_read, GH)
                    me.did(act.activation(tl(g_sq, 2 * h, 2), tl(g_o, 2 * h, 2), ACT.Square), sq_ready)
                for n in range(2):
                    root(G[n], 512, 1.0 / GDV, 1, g_rs[:, 512 * n:512 * n + 512])
                prep(free=PH["gla_r"].tile0 + 8)
            gemm("out1")

            def rms(free, full):
                prep(free=free, squares=True)
                root(X[0], T + 2 if full else T, 1.0 / D, 1, sd[:, 0:T + 2 if full else T])

            def ple(k):
                if not on(f"ple_proj{k}"):
                    return
                prep(free=PH[f"gate_up{k}"].tile0 + 4 * PH[f"gate_up{k}"].n, squares=True)
                gemm(f"ple_proj{k}", evac(lambda at, t: tl(pp, t), pp_ready))
                root(X[0], T, 1.0 / D, 1, sd[:, 0:T])

                def after(at, t):
                    n = KT * (k - 1) + 4 * at.i + t
                    act.wait_ge(ple_in, n + 1)
                    wait(act, ple_prod, n - 1)
                    act.activation(tl(sg, t % 2), tl(gt, t % 2), ACT.Sigmoid).then_inc(ple_sig, 1)

                gemm(f"ple_gate{k}", after=after)

            if on("gate_up1"):
                rms(PH["out1"].tile0 + 8, False)
            ffn(1)
            ple(1)
            if on("diff_q"):
                rms(PH["ple_gate1"].tile0 + 8, True)
            for base, name in ((0, "diff_q"), (4, "diff_k")):
                def after(at, t, base=base):
                    buf = d_q if base == 0 else d_k
                    if t % 2 == 1:
                        r = base + 2 * at.i + t // 2
                        act.wait_ge(qk_src, 2 * r + 2)
                        if r >= 2:
                            act.wait_ge(qk_stat, r - 1)
                        me.did(act.activation(tl(d_sq, r % 2, w=512), tl(buf, 2 * (r - base), 2), ACT.Square), qk_sq)
                    if t == 3:
                        for r in (base + 2 * at.i, base + 2 * at.i + 1):
                            me.next(qk_stat)
                            if r >= 2:
                                act.wait_ge(qk_normed, r - 1)
                            me.did(act.activation(tl(d_rs, r % 2, w=512), X[r % 2][:, :], ACT.Sqrt, bias=eps[:, 1:2],
                                                  scale=1.0 / HD), qk_sd)
                gemm(name, after=after)
            gemm("diff_v", evac(v_dst(d_v), v_ready, v_scale))
            if on("out2"):
                for i in range(NH + 1):
                    if i < NH:
                        me.next(max_ready)
                        for c in range(2):
                            for qt in range(2):
                                n = 4 * (i % 2) + 2 * c + qt
                                if i >= 2:
                                    act.wait_ge(trans_done, NH + i - 1)
                                ins = act.activation(tl(d_p, 4 * (i % 2) + 2 * c + qt),
                                                     G[2 * (i % 2) + c][:, qt * T:(qt + 1) * T], ACT.Exp,
                                                     bias=neg_max[:, n:n + 1], scale=HD ** -0.5,
                                                     accum_out=sums[:, n:n + 1])
                            me.did(ins, exp_done)
                    if i >= 1:
                        me.next(trans_done)
                        if i >= 3:
                            act.wait_ge(pv_done, NH + i - 2)
                        me.did(act.activation(tl(d_pt, (i - 1) % 2, w=512), X[(i - 1) % 2][:, :], ACT.Copy), pt_ready)
                group_root((0, 1, 2, 3), d_o, d_nsq, 1.0 / (2 * HD), 1, G)
                prep(free=PH["diff_v"].tile0 + 4)
            gemm("out2")
            if on("gate_up2"):
                rms(PH["out2"].tile0 + 8, False)
            ffn(2)
            ple(2)

        @block.vector
        def _(dve):
            me = Steps(dve, dve_step)

            def low(ph, at, q):
                slot, w = (ph.s0 + at.parity) % 2, ph.cols // 4
                hslot = (ph.j0 + at.parity) % 2
                dve.wait_ge(hi_ready, at.lin(4 * ph.j0 + q + 1, 4))
                dve.tensor_tensor(wlo[hslot][:, q * w:(q + 1) * w], raw[slot][:, q * w:(q + 1) * w],
                                  whi[hslot][:, q * w:(q + 1) * w].bitcast(F32), ALU.subtract).then_inc(lo_ready, 1)

            def gemm(name, one=None, after=None):
                if not on(name):
                    return
                ph = PH[name]

                def body(at):
                    for t in range(ph.tiles):
                        nxt = follow(ph, at)
                        if nxt is not None and on(nxt[0].name):
                            for q in quarters(ph, t):
                                low(*nxt, q)
                        if one:
                            wait(dve, tile_done, at.lin(ph.tile0 + t + 1, ph.tiles))
                            one(at, t, bank_of(ph, at, t)[0])
                        if after:
                            after(at, t)

                rounds(dve, ph, body)

            def prep(make, order=range(KT), free=None):
                if free:
                    wait(dve, tile_done, free)

                def rest(t):
                    me.next(ohi_ready)
                    me.did(dve.tensor_tensor(tl(olo, t), tl(om, t), tl(ohi, t).bitcast(F32), ALU.subtract), olo_ready)

                last = None
                for t in order:
                    me.did(make(t), om_ready)
                    if last is not None:
                        rest(last)
                    last = t
                rest(last)

            dve.memset(v3(upad[:, :], 4)[:, :, 0:2], 0.0)
            dve.wait_ge(set_zero, 3)
            me.next(setup_t)
            me.did(dve.tensor_copy(cols_b[:, :], G[0][:, P:P + NB]), cols_ready)
            me.did(dve.tensor_copy(cols_a[:, :], G[0][:, 0:NA]), dve_read)
            for n, bank in enumerate((X[0], X[1], X[2], G[1])):
                me.next(setup_t)
                me.did(dve.tensor_copy(tl(res, n, w=512), bank[:, :]), dve_read)
            for layer in range(2):
                me.next(setup_t)
                bank = G[2 + layer]
                me.link(dve.tensor_copy(tl(p_hi, layer, w=512), bank[:, :]))
                me.did(dve.tensor_tensor(tl(p_lo, layer, w=512), bank[:, :], tl(p_hi, layer, w=512).bitcast(F32),
                                         ALU.subtract), dve_read)
            lam4 = lam_in[:, :].rearrange("p (e s n) -> p e s n", e=2, s=2)
            me.link(dve.tensor_tensor(lam4[:, :, 0, :], lam4[:, :, 0, :], lam4[:, :, 1, :], ALU.mult))
            me.did(dve.tensor_reduce(lam[:, 0:2], lam4[:, :, 0, :], AX, ALU.add), lam_sum)
            me.next(lam_exp)
            me.link(dve.tensor_tensor(lam[:, 4:5], lam[:, 3:4], lam[:, 2:3], ALU.subtract))
            me.link(dve.tensor_scalar(lam[:, 4:5], lam[:, 4:5], -LAMBDA_INIT, None, ALU.add))
            me.did(dve.tensor_scalar(lam[:, 5:6], B("diff_g_sub_2"), 1.0 - LAMBDA_INIT, None, ALU.mult))

            if on("in_q"):
                dve.wait_ge(plain_used, 4)
                me.again(dve_read)
                me.link(dve.tensor_tensor(mod[:, 0:16], X[3][:, 0:16], A("b_ada", 0, 16), ALU.add), mod_read)
                me.link(dve.tensor_scalar(mod[:, 8:16], mod[:, 8:16], 1.0, None, ALU.add))
                for q in range(4):
                    low(PH["in_q"], At(0), q)
                prep(lambda t: dve.tensor_scalar(tl(om, t), tl(res, t), mod[:, 8 + t:9 + t], mod[:, t:t + 1],
                                                 ALU.mult, ALU.add))
                me.did(dve.tensor_scalar(res[:, :], res[:, :], ALPHA, None, ALU.mult))

            def rope(r):
                bank = X[(0, 1, 2, 0)[r]]
                me.next(rot_done)
                if r == 2:
                    dve.tensor_tensor(tl(om, 4), bank[:, 0:T], C("sin_q", T), ALU.mult)
                    me.did(dve.tensor_tensor(tl(om, 7), bank[:, T:2 * T], C("sin_i", T), ALU.mult), rot_read)
                    pairs = ((4, 1), (7, 1))
                else:
                    t = (0, 2, None, 5)[r]
                    me.did(dve.tensor_tensor(v3(tl(om, t, 2), 2), v3(bank[:, :], 2),
                                             bc(C("sin_i" if r == 3 else "sin_q", T), 2), ALU.mult), rot_read)
                    pairs = ((t, 2),)
                me.next(rope_cos)
                me.again(rot_read)
                for t, n in pairs:
                    ins = dve.tensor_tensor(tl(rope_out, t, n), tl(rope_out, t, n), tl(om, t, n), ALU.add)
                me.did(ins, roped)

            gemm("in_q")
            gemm("in_idx")
            if on("in_v"):
                rope(0)
                rope(1)
            gemm("in_v")
            if on("in_gc"):
                rope(2)
                rope(3)
                me.next(v_src, 2)
                me.link(dve.tensor_scalar(v3(vtok[:, :], 2)[:, :, 64:72], v3(vtok[:, :], 2)[:, :, 64:72],
                                          IH ** -0.5 * ID ** -0.5, None, ALU.mult))
            gemm("in_gc")
            BLOCKS = ((0, 0, P), (1, P, 2 * P))
            if on("in_hc"):
                for h in range(IH):
                    me.next(relu_done)
                    for tt, c0, n in BLOCKS:
                        w = vtok[:, 72 * tt + 64 + h:72 * tt + 65 + h]
                        r = relu[:, 384 * (h % 2) + c0:384 * (h % 2) + c0 + n]
                        if h:
                            me.again(idx_acc, less=1)
                            me.did(dve.scalar_tensor_tensor(score[:, c0:c0 + n], r, w, score[:, c0:c0 + n],
                                                            ALU.mult, ALU.add), idx_acc)
                        else:
                            me.did(dve.tensor_scalar(score[:, c0:c0 + n], r, w, None, ALU.mult), idx_acc)

            def short_conv(at, t, bank):
                u = upad[:, (T + 2) * t:(T + 2) * (t + 1)]
                me.next(gc_ready)
                me.link(dve.tensor_tensor(u[:, 2:T + 2], bank[:, 0:T], tl(gc, t), ALU.mult), dve_read)
                me.link(dve.tensor_scalar(tl(conv, t), u[:, 0:T], A("conv_w", t), None, ALU.mult))
                for j in (1, 2):
                    me.link(dve.scalar_tensor_tensor(tl(conv, t), u[:, j:j + T], A("conv_w", 4 * j + t), tl(conv, t),
                                                     ALU.mult, ALU.add))

            gemm("in_hc", short_conv)
            if on("in_gb"):
                me.again(idx_acc)
                me.link(dve.tensor_tensor(kept[:, :], score[:, :], C("causal", 384), ALU.add))
                for _ in range(TOPK // 8):
                    for tt, c0, n in BLOCKS:
                        me.did(dve.max(top8[:, 8 * tt:8 * tt + 8], kept[:, c0:c0 + n]))
                    for tt, c0, n in BLOCKS:
                        me.again(less=1)
                        me.did(dve.match_replace(kept[:, c0:c0 + n], top8[:, 8 * tt:8 * tt + 8], kept[:, c0:c0 + n],
                                                 TAKEN))
                    me.again()
                me.link(dve.tensor_scalar(allow[:, :], kept[:, :], TAKEN / 1e3, NEG, ALU.is_gt, ALU.mult))
                me.did(dve.tensor_tensor(allow[:, :], allow[:, :], C("causal", 384), ALU.add))

            def gated_conv(at, t, bank):
                me.did(dve.tensor_tensor(tl(mixed, 4 + t), bank[:, 0:T], tl(conv, t), ALU.mult), mixed_ready)

            gemm("in_gb", gated_conv)

            def group_make(src, buf, gain):
                def make(t):
                    if t % 2 == 0:
                        me.next(sd_ready)
                        me.link(dve.reciprocal(tl(buf, t, 2), tl(buf, t, 2)))
                    return dve.scalar_tensor_tensor(tl(om, t), tl(src, t), gain(t), tl(buf, t), ALU.mult, ALU.mult)
                return make

            if on("ada_b"):
                mix_make = group_make(mixed, mix_sq, lambda t: A("attn_norm_g", t) if t < 4 else A("conv_norm_g", t - 4))
                me.again(mixed_ready)
                prep(mix_make, order=(4, 5, 6, 7), free=PH["in_gb"].tile0 + 4)
                me.again()
                for i in range(NH + 2):
                    if i < NH:
                        me.next(score_done)
                        if i >= 2:
                            dve.wait_ge(trans_done, i - 1)
                        lg = tl(logit, i % 2, w=384)
                        me.link(dve.scalar_tensor_tensor(lg, G[i % 2][:, 0:384], HD ** -0.5, allow[:, :],
                                                         ALU.mult, ALU.add), score_read)
                        for tt, c0, n in BLOCKS:
                            ins = dve.tensor_reduce(neg_max[:, 2 * (i % 2) + tt:2 * (i % 2) + tt + 1], lg[:, c0:c0 + n],
                                                    AX, ALU.max, negate=True)
                        me.did(ins, max_ready)
                    if 1 <= i <= NH:
                        me.next(exp_done)
                        s = (i - 1) % 2
                        me.link(dve.reciprocal(rsum[:, 2 * s:2 * s + 2], sums[:, 2 * s:2 * s + 2]))
                        for tt, c0, n in BLOCKS:
                            ap = logit[:, 384 * s + c0:384 * s + c0 + n]
                            ins = dve.tensor_scalar(ap, ap, rsum[:, 2 * s + tt:2 * s + tt + 1], None, ALU.mult)
                        me.did(ins, prob_ready)
                    if i >= 3 and i % 2:
                        me.next(pv_done, 2)
                        me.did(dve.tensor_copy(tl(mixed, (i - 2) // 2), X[(i - 2) // 2 % 2][:, 0:T]), mixed_ready)
                dve.wait_ge(plain_used, 12)
                me.link(dve.tensor_tensor(mod[:, 16:48], X[3][:, 16:48], A("b_ada", 16, 32), ALU.add), mod_read)
                me.link(dve.tensor_scalar(mod[:, 32:40], mod[:, 32:40], 1.0, None, ALU.add))
                me.did(dve.tensor_tensor(fold[:, 0:8], A("ln1_g", 0, 8), mod[:, 32:40], ALU.mult))
                me.link(dve.tensor_tensor(fold[:, 8:16], A("ln1_b", 0, 8), mod[:, 32:40], ALU.mult))
                me.did(dve.tensor_tensor(fold[:, 8:16], fold[:, 8:16], mod[:, 24:32], ALU.add))
                me.did(dve.tensor_scalar(fold[:, 16:24], A("ln1_g", 0, 8), ALPHA, None, ALU.mult))
                me.did(dve.tensor_scalar(fold[:, 24:32], A("ln1_b", 0, 8), ALPHA, None, ALU.mult))
                me.did(dve.tensor_tensor(fold[:, 32:40], A("ln2_g", 0, 8), B("norm_mix_2", 0, 8), ALU.mult))
                me.link(dve.tensor_tensor(fold[:, 40:48], A("ln2_b", 0, 8), B("norm_mix_2", 0, 8), ALU.mult))
            if on("out0"):
                for q in range(4):
                    low(PH["out0"], At(0), q)
                me.again(mixed_ready)
                prep(mix_make, order=(0, 1, 2, 3))

            def residual(gate=None):
                def one(at, t, bank):
                    m = at.lin(t, PH_tiles[0])
                    if gate is None:
                        ins = dve.tensor_tensor(tl(res, m), bank[:, 0:T], tl(res, m), ALU.add)
                    else:
                        g = mod[:, gate + m:gate + m + 1] if isinstance(m, int) else mod[:, bass.ds(m + gate, 1)]
                        ins = dve.scalar_tensor_tensor(tl(res, m), bank[:, 0:T], g, tl(res, m), ALU.mult, ALU.add)
                    ins.then_inc(dve_read, 1)
                return one

            PH_tiles = [4]

            def add_to_residual(name, gate=None):
                PH_tiles[0] = PH[name].tiles
                gemm(name, residual(gate))
                if on(name):
                    me.seen(dve_read, PH[name].tiles * PH[name].n)

            add_to_residual("out0", 16)

            def layer_norm(n):
                me.again(dve_read)
                me.next(mean_done)
                me.link(dve.tensor_scalar(mean[:, :], X[0][:, 0:T], 1.0 / D, None, ALU.mult), mean_ready)
                for t in range(0, KT, 2):
                    me.did(dve.tensor_tensor(v3(tl(res, t, 2), 2), v3(tl(res, t, 2), 2), bc(mean[:, :], 2),
                                             ALU.subtract), centered)
                me.next(sd_ready)
                me.link(dve.reciprocal(rstd[:, 0:T], sd[:, 0:T]))
                me.again(centered)
                for t in range(0, KT, 2):
                    me.did(dve.tensor_tensor(v3(tl(res, t, 2), 2), v3(tl(res, t, 2), 2), bc(rstd[:, 0:T], 2),
                                             ALU.mult))
                me.again()
                g, b = (fold[:, 0:8], fold[:, 8:16]) if n == 0 else (fold[:, 32:40], fold[:, 40:48])
                prep(lambda t: dve.tensor_scalar(tl(om, t), tl(res, t), g[:, t:t + 1], b[:, t:t + 1], ALU.mult, ALU.add),
                     free=PH["out0" if n == 0 else "down0"].tile0 + 8)

            def root(n=T):
                me.next(sd_ready)
                me.link(dve.reciprocal(rstd[:, 0:n], sd[:, 0:n]))

            def rms(gain, free):
                me.again(dve_read)
                me.again(ple_added)
                prep(lambda t: dve.tensor_scalar(tl(om, t), tl(res, t), gain(t), None, ALU.mult), free=free)

            def ffn(k):
                if not on(f"gate_up{k}"):
                    return
                n0 = FT * k

                def one(at, t, bank):
                    j = t // 2
                    n = at.lin(n0 + j, 2)
                    wait(dve, silu_done if t % 2 == 0 else prod_done, n - 1)
                    dst = tl(gt if t % 2 == 0 else ut, j)
                    if k == 0:
                        ins = dve.tensor_copy(dst, bank[:, 0:T])
                    else:
                        ins = dve.tensor_tensor(dst, bank[:, 0:T], rstd[:, 0:T], ALU.mult)
                    ins.then_inc(gate_in if t % 2 == 0 else up_in, 1)

                gemm(f"gate_up{k}", one)
                if k == 0:
                    dve.wait_ge(res_ready, KT)
                add_to_residual(f"down{k}", 40 if k == 0 else None)

            def ple(k):
                if not on(f"ple_proj{k}"):
                    return
                rms(lambda t: B("ple_norm_2", KT * (k - 1) + t), PH[f"gate_up{k}"].tile0 + 4 * PH[f"gate_up{k}"].n)
                gemm(f"ple_proj{k}")
                root()

                def add(t):
                    me.next(ple_prod)
                    me.did(dve.tensor_tensor(tl(res, t), tl(res, t), tl(prod, t % 2), ALU.add), ple_added)

                def one(at, t, bank):
                    m = 4 * at.i + t
                    wait(dve, ple_sig, KT * (k - 1) + m - 1)
                    me.did(dve.tensor_tensor(tl(gt, t % 2), bank[:, 0:T], rstd[:, 0:T], ALU.mult), ple_in)
                    if m:
                        add(m - 1)

                gemm(f"ple_gate{k}", one)
                add(KT - 1)

            if on("gate_up0"):
                layer_norm(0)
            ffn(0)

            if on("gla_z"):
                layer_norm(1)
                root(T + 2)
                dve.wait_ge(plain_used, PH["gla_z"].plain0 + 1)
                for o in (0, 32):
                    ins = dve.tensor_tensor(g_z[o:o + RANK, :], X[1][o:o + RANK, 0:T], rstd[o:o + RANK, 0:T], ALU.mult)
                me.did(ins, z_ready)

            def scaled(buf, ready, k=None):
                def one(at, t, bank):
                    m = 4 * at.i + t
                    if k is None:
                        ins = dve.tensor_tensor(tl(buf, m), bank[:, 0:T], rstd[:, 0:T], ALU.mult)
                    else:
                        ins = dve.scalar_tensor_tensor(tl(buf, m), bank[:, 0:T], k, rstd[:, 0:T], ALU.mult, ALU.mult)
                    me.did(ins, ready)
                return one

            gemm("gla_q", scaled(g_q, dve_read, GDK ** -0.5))
            if on("gla_k"):
                for b in range(4):
                    me.next(la_done)
                    for half in range(2):
                        t = 2 * (b % 2) + half
                        ins = dve.tensor_scalar(tl(g_la[b // 2], t), X[b][:, half * T:(half + 1) * T],
                                                B("gla_b_gate_f_2" if b < 2 else "gla_b_gate_b_2", t), None, ALU.add)
                    me.did(ins, la_read)
            gemm("gla_k", scaled(g_k, dve_read))
            ends = lambda buf, d: v3(buf[:, :], 16)[:, :, CH - 1:CH] if d == 0 else v3(buf[:, :], 16)[:, :, 0:1]
            if on("gla_v"):
                for d in range(2):
                    me.next(lg_ready)
                    me.link(dve.scalar_tensor_tensor(g_la[d][:, :], g_la[d][:, :], 0.0, g_b[d][:, :], ALU.min,
                                                     ALU.subtract))
                    me.next(seg_ready)
                    way = (lambda ap: ap[:, :]) if d == 0 else (lambda ap: ap[:, ::-1])
                    me.link(dve.tensor_tensor_scan(way(g_b[d]), way(seg[d]), way(g_la[d]), 0.0, ALU.mult, ALU.add),
                            b_ready)
                    me.did(dve.tensor_copy(v3(total[:, 16 * d:16 * d + 16], 16), ends(g_b[d], d)))

            def gla_after(at, t):
                if at.i == 1 and t == 0:
                    for d in range(2):
                        me.next(grow_ready, 2)
                        me.again()
                        tot = total[:, 16 * d:16 * d + 16].rearrange("p (c n) -> p c n", n=1).to_broadcast([P, 16, CH])
                        me.did(dve.tensor_tensor(v3(g_b[d][:, :], 16), tot, v3(g_b[d][:, :], 16), ALU.subtract),
                               dist_ready)

            gemm("gla_v", None, gla_after)
            if on("gla_r"):
                me.again(dve_read)
                for d in range(2):
                    me.link(dve.tensor_copy(v3(decay[:, 16 * d:16 * d + 16], 16), ends(g_la[d], d)))
                    me.did(dve.tensor_tensor(g_la[d][:, :], g_q[:, :], g_la[d][:, :], ALU.mult), kd_ready)
                    me.next(fall_ready)
                    me.did(dve.tensor_tensor(g_b[d][:, :], g_k[:, :], g_b[d][:, :], ALU.mult), kd_ready)
            gemm("gla_r", scaled(g_r, r_ready))
            if on("out1"):
                def read_out(h):
                    me.next(go_done)
                    if h == 0:
                        dve.wait_ge(ke_ready, 2)
                    me.did(dve.tensor_copy(tl(g_o, 2 * h, 2), X[2 + h % 2][:, :]), go_read)

                for h in range(GH):
                    me.next(gs_done)
                    me.link(dve.tensor_tensor(v3(g_m[:, :], 2), v3(G[0][:, :], 2), bc(C("gla_mask", 2 * P), 2),
                                              ALU.mult), gs_read)
                    m4 = g_m[:, :].rearrange("p (t f n) -> p t f n", t=2, f=2)
                    if h >= 2:
                        dve.wait_ge(go_done, h - 1)
                    me.did(dve.tensor_tensor(v3(tl(g_st, h % 2), 2), m4[:, :, 0, :], m4[:, :, 1, :], ALU.add), st_ready)
                    if h:
                        read_out(h - 1)
                    me.next(u_done)
                    S = lambda n: tl(state, n)
                    dec = lambda d, c: decay[:, 16 * d + 4 * h + c:16 * d + 4 * h + c + 1]
                    step = lambda n, m, k, u: dve.scalar_tensor_tensor(S(n), S(m), k, u, ALU.mult, ALU.add)
                    me.link(dve.tensor_copy(S(3), X[1][:, 0:T]), u_read)
                    me.did(step(4, 3, dec(1, 2), X[0][:, 0:T]), u_read)
                    me.link(dve.tensor_copy(S(0), G[2][:, 0:T]))
                    me.link(step(1, 0, dec(0, 1), G[3][:, 0:T]))
                    me.did(step(2, 1, dec(0, 2), G[2][:, T:2 * T]), u_read)
                    me.did(step(5, 4, dec(1, 1), G[3][:, T:2 * T]), u_read)
                read_out(GH - 1)

                def make(t):
                    if t % 4 == 0:
                        me.next(sd_ready)
                        me.link(dve.reciprocal(tl(g_rs, t // 2, 2), tl(g_rs, t // 2, 2)))
                    if t % 2 == 0:
                        me.next(gated)
                    return dve.scalar_tensor_tensor(tl(om, t), tl(g_r, t), B("gla_g_out_2", t % 2), tl(g_rs, t // 2),
                                                    ALU.mult, ALU.mult)

                prep(make, free=PH["gla_r"].tile0 + 8)
            if on("out1"):
                dve.wait_ge(res_ready, 2 * KT)
            add_to_residual("out1")
            if on("gate_up1"):
                rms(lambda t: B("norm_ffn_2", t), PH["out1"].tile0 + 8)
                root()
            ffn(1)
            ple(1)

            if on("diff_q"):
                rms(lambda t: B("norm_mix_2", KT + t), PH["ple_gate1"].tile0 + 8)
                root(T + 2)

            def pair(r):
                return tl(d_q, 2 * r, 2) if r < 4 else tl(d_k, 2 * r - 8, 2)

            def normalize(r):
                me.next(qk_sd)
                rs = tl(d_rs, r % 2, w=512)
                me.link(dve.reciprocal(rs, rs))
                me.did(dve.scalar_tensor_tensor(pair(r), pair(r), B("diff_g_q_2" if r < 4 else "diff_g_k_2"), rs,
                                                ALU.mult, ALU.mult), qk_normed)

            def turn(r):
                me.next(qk_rot)
                me.again(qk_ready)
                me.did(dve.tensor_tensor(v3(d_t2[:, :], 2), v3(X[2 + r % 2][:, :], 2), bc(C("sin_d", T), 2), ALU.mult),
                       qk_rot_read)
                me.next(qk_cos)
                me.again(qk_rot_read)
                me.did(dve.tensor_tensor(pair(r), d_t1[:, :], d_t2[:, :], ALU.add), qk_ready)

            for base, name in ((0, "diff_q"), (4, "diff_k")):
                def after(at, t, base=base):
                    r = base + 2 * at.i
                    if t == 1 and r:
                        turn(r - 2)
                    if t == 3:
                        if r:
                            turn(r - 1)
                        normalize(r)
                        normalize(r + 1)
                gemm(name, scaled(d_q if base == 0 else d_k, qk_src), after)
            gemm("diff_v", None, lambda at, t: turn(6 + t) if at.i == 0 else None)
            if on("out2"):
                for i in range(NH + 2):
                    if i < NH:
                        me.next(score_done)
                        s = 4 * (i % 2)
                        for c in range(2):
                            me.did(dve.tensor_reduce(neg_max[:, s + 2 * c:s + 2 * c + 2],
                                                     v3(G[2 * (i % 2) + c][:, :], 2), AX, ALU.max, negate=True))
                        me.again()
                        me.did(dve.tensor_scalar(neg_max[:, s:s + 4], neg_max[:, s:s + 4], HD ** -0.5, None, ALU.mult),
                               max_ready)
                    if 1 <= i <= NH:
                        me.next(exp_done, 2)
                        s = 4 * ((i - 1) % 2)
                        me.link(dve.reciprocal(rsum[:, s:s + 4], sums[:, s:s + 4]))
                        me.did(dve.tensor_scalar(rsum[:, s + 2:s + 4], rsum[:, s + 2:s + 4], lam[:, 4:5], None, ALU.mult))
                        for qt in range(2):
                            me.did(dve.tensor_scalar(tl(d_p, s + qt), tl(d_p, s + qt), rsum[:, s + qt:s + qt + 1],
                                                     None, ALU.mult))
                        me.again()
                        for qt in range(2):
                            ins = dve.scalar_tensor_tensor(tl(d_p, s + qt), tl(d_p, s + 2 + qt),
                                                           rsum[:, s + 2 + qt:s + 3 + qt], tl(d_p, s + qt),
                                                           ALU.mult, ALU.add)
                        me.did(ins, prob_ready)
                    if i >= 2:
                        me.next(pv_done)
                        me.did(dve.tensor_copy(tl(d_o, i - 2), X[2 + i % 2][:, 0:T]), mixed_ready)
                me.again(mixed_ready)
                prep(group_make(d_o, d_nsq, lambda t: lam[:, 5:6]), free=PH["diff_v"].tile0 + 4)
            add_to_residual("out2")
            if on("gate_up2"):
                rms(lambda t: B("norm_ffn_2", KT + t), PH["out2"].tile0 + 8)
                root()
            ffn(2)
            ple(2)
            if stop is None:
                for n in range(4):
                    me.next(out_done)
                    me.did(dve.tensor_copy(tl(o_tok, n, w=512), G[n][:, :]), out_read)

        @block.tensor
        def _(pe):
            banks = Banks(pe)
            me = Steps(pe, None)

            def three(dst, st_hi, st_lo, mv_hi, mv_lo, start, stop_):
                pe.matmul(dst, st_hi, mv_hi, start=start, stop=False)
                pe.matmul(dst, st_hi, mv_lo, start=False, stop=False)
                return pe.matmul(dst, st_lo, mv_hi, start=False, stop=stop_)

            def slab_view(ph, buf, shape):
                if shape == "gate_up":
                    return buf[:, :].rearrange("p (k g n) -> p k g n", k=KT, g=2)
                k = {"down": FT, "ple": 2}.get(shape, KT)
                return buf[:, 0:ph.cols].rearrange("p (k n) -> p k n", k=k)

            def gemm(name, freed, shape="plain", olo_from=None, order=range(KT), after=None):
                if not on(name):
                    return
                ph = PH[name]
                base = banks.n.get(freed.name, 0) if freed is not None else 0

                def body(at):
                    hslot = (ph.j0 + at.parity) % 2
                    hi, lo = (slab_view(ph, b[hslot], shape) for b in (whi, wlo))
                    pe.wait_ge(lo_ready, at.lin(4 * (ph.j0 + 1), 4))
                    first = isinstance(at.i, int) and at.i == 0
                    for t in range(ph.tiles):
                        bank, n = bank_of(ph, at, t)
                        if shape == "gate_up":
                            by = gate_in if t % 2 == 0 else up_in
                            if first:
                                banks.claim(bank, by)
                            else:
                                wait(pe, by, at.lin(FT * int(name[-1]) + t // 2 - 1, 2))
                        elif shape == "down":
                            if first:
                                banks.claim(bank, freed)
                            else:
                                if at.i is not None and at.it is None and at.i == 1 or at.it is not None and at.b == 0:
                                    banks.settle(G[1]) if at.it is not None else None
                                wait(pe, freed, at.lin(base - 1, 1))
                        else:
                            banks.claim(bank, freed)
                        if shape == "gate_up":
                            w = lambda v, k: v[:, k, t % 2, (t // 2) * P:(t // 2 + 1) * P]
                        elif ph.tiles == 1:
                            w = lambda v, k: v[:, k, :]
                        else:
                            w = lambda v, k: v[:, k, t * P:(t + 1) * P]
                        ks = {"down": range(FT), "ple": range(2)}.get(shape, order)
                        layer = int(name[-1]) - 1 if shape == "ple" else 0
                        for n_, k in enumerate(ks):
                            if first and t == 0 and olo_from is not None:
                                pe.wait_ge(olo_ready, olo_from + n_ + 1)
                            if first and shape == "down":
                                pe.wait_ge(actlo_ready, FT * int(name[-1]) + k + 1)
                            if shape == "token":
                                st = (tl(ohi, k)[:, t * P:(t + 1) * P], tl(olo, k)[:, t * P:(t + 1) * P])
                                ins = three(bank[:, 0:n], *st, hi[:, k, :], lo[:, k, :], n_ == 0, n_ == len(ks) - 1)
                            else:
                                src = {"down": (acthi, actlo), "ple": (p_hi, p_lo)}.get(shape, (ohi, olo))
                                mv = [tl(b, k + 2 * layer) for b in src]
                                ins = three(bank[:, 0:T], w(hi, k), w(lo, k), *mv, n_ == 0, n_ == len(ks) - 1)
                        ins.then_inc(tile_done, 1)
                        if after:
                            after(at, t)

                if shape == "down":
                    settle_then_rounds(ph, body)
                else:
                    rounds(pe, ph, body)
                if shape == "gate_up":
                    end = FT * (int(name[-1]) + 1)
                    for t in range(4):
                        banks.skip(G[t], gate_in if t % 2 == 0 else up_in, end)
                if shape == "down":
                    banks.skip(G[0], freed, base + ph.n)
                    banks.skip(G[1], freed, base + ph.n)

            def settle_then_rounds(ph, body):
                def one(at):
                    body(at)
                    if at.it is None and at.i == 0:
                        banks.settle(G[1])
                rounds(pe, ph, one)

            def stats(bank, ready, tok=False, src=sq, k=1, done=stat_done, waits=sq_ready, part=1):
                banks.claim(bank, ready)
                for t in range(KT):
                    if t % part == 0 and waits is not None:
                        me.next(waits)
                    ins = pe.matmul(bank[:, 0:T], ones[:, :], tl(src, t), start=(t == 0), stop=(t == KT - 1))
                if tok:
                    for tt in range(TT):
                        for t in range(KT):
                            ins = pe.matmul(bank[:, T + tt:T + tt + 1], tl(src, t)[:, tt * P:(tt + 1) * P], ones[:, 0:1],
                                            start=(t == 0), stop=(t == KT - 1), skip_group_check=True)
                ins.then_inc(done, 1)

            def group_stats(groups, mat, buf, ready_banks):
                for n, g in enumerate(groups):
                    bank = ready_banks[n % len(ready_banks)]
                    banks.claim(bank, sd_ready)
                    me.next(sq_ready)
                    pe.matmul(bank[:, :], mat, tl(buf, 2 * g, 2), start=True, stop=True).then_inc(stat_done, 1)

            pe.wait_ge(params_in, 16 * (len(ROWS_A) + len(ROWS_B) + 4))
            pe.wait_ge(const_in, 16)
            pe.wait_ge(set_zero, 3)
            banks.claim(G[0], dve_read)
            pe.transpose(G[0][:, 0:NA], rows_a[0:NA, :], ident[0:NA, 0:NA])
            pe.transpose(G[0][:, P:P + NB], rows_b[0:NB, :], ident[0:NB, 0:NB]).then_inc(setup_t, 1)
            pe.wait_ge(x_in, 32)
            for n, bank in enumerate((X[0], X[1], X[2], G[1])):
                banks.claim(bank, dve_read)
                for k in range(2):
                    for tt in range(TT):
                        ins = pe.transpose(bank[:, k * T + tt * P:k * T + (tt + 1) * P],
                                           tl(xin, tt, w=D)[:, (2 * n + k) * P:(2 * n + k + 1) * P], ident)
                ins.then_inc(setup_t, 1)
            for layer in range(2):
                bank = G[2 + layer]
                banks.claim(bank, dve_read)
                for k in range(2):
                    for tt in range(TT):
                        o = layer * 512 + tt * 256 + k * P
                        ins = pe.transpose(bank[:, k * T + tt * P:k * T + (tt + 1) * P], pin[:, o:o + P], ident)
                ins.then_inc(setup_t, 1)

            def modulation(i):
                name, j = ("ada_a", i) if i < 4 else ("ada_b", i - 4)
                ph = PH[name]
                slot = (ph.s0 + j) % 2
                pe.wait_ge(landed[slot], ph.landed[j])
                for m in range(4):
                    for k in range(KT):
                        ins = pe.matmul(X[3][:, 4 * i + m:4 * i + m + 1], raw[slot][:, 512 * k + P * m:512 * k + P * m + P],
                                        c_act[:, k:k + 1], start=(k == 0), stop=(k == KT - 1), skip_group_check=True)
                ins.then_inc(plain_used, 1)

            pe.wait_ge(c_ready, 1)
            banks.claim(X[3], mod_read)
            if on("ada_b"):
                pass
            for i in range(4):
                modulation(i)

            gemm("in_q", rope_src, olo_from=0)
            gemm("in_idx", rope_src)

            def rotate(r):
                bank = X[(0, 1, 2, 0)[r]]
                banks.claim(bank, rot_read)
                pe.wait_ge(rope_src, (2, 4, 8, 8)[r])
                if r == 2:
                    pe.matmul(bank[:, 0:T], C("rot_q"), tl(rope_in, 4), start=True, stop=True)
                    ins = pe.matmul(bank[:, T:2 * T], C("rot_i"), tl(rope_in, 7), start=True, stop=True)
                else:
                    ins = pe.matmul(bank[:, :], C("rot_i" if r == 3 else "rot_q"), tl(rope_in, (0, 2, None, 5)[r], 2),
                                    start=True, stop=True)
                ins.then_inc(rot_done, 1)

            if on("in_v"):
                rotate(0)
                rotate(1)
            gemm("in_v", v_src, shape="token")
            if on("in_gc"):
                rotate(2)
                rotate(3)
            gemm("in_gc", gc_ready)
            if on("in_hc"):
                pe.wait_ge(roped, 4)
                for h in range(IH):
                    banks.claim(G[h % 4], relu_done)
                    rows = slice(ID * (h % 4), ID * (h % 4) + ID)
                    q, kk = tl(rope_out, 5 + h // 4), tl(rope_out, 7)
                    pe.matmul(G[h % 4][:, 0:P], q[rows, 0:P], kk[rows, 0:P], start=True, stop=True)
                    pe.matmul(G[h % 4][:, P:3 * P], q[rows, P:2 * P], kk[rows, :], start=True,
                              stop=True).then_inc(idx_done, 1)
            gemm("in_hc", dve_read)
            gemm("in_gb", mixed_ready)
            if on("ada_b"):
                group_stats((2, 3), C("blk"), mix_sq, X[0:2])
                banks.claim(X[3], mod_read)
                for i in range(NH + 2):
                    if i < NH:
                        banks.claim(G[i % 2], score_read)
                        rows = slice(HD * (i % 2), HD * (i % 2) + HD)
                        q, kk = tl(rope_out, i // 2), tl(rope_out, 4)
                        pe.matmul(G[i % 2][:, 0:P], q[rows, 0:P], kk[rows, 0:P], start=True, stop=True)
                        pe.matmul(G[i % 2][:, P:3 * P], q[rows, P:2 * P], kk[rows, :], start=True,
                                  stop=True).then_inc(score_done, 1)
                        modulation(4 + i)
                    if 1 <= i <= NH:
                        bank, lg = G[2 + (i - 1) % 2], tl(logit, (i - 1) % 2, w=384)
                        banks.claim(bank, pt_ready)
                        me.next(prob_ready)
                        for n in range(3):
                            ins = pe.transpose(bank[:, n * P:(n + 1) * P], lg[:, n * P:(n + 1) * P], ident)
                        ins.then_inc(trans_done, 1)
                    if i >= 2:
                        h = i - 2
                        bank, pt = X[h // 2 % 2], tl(prob_t, h % 2, w=384)
                        if h % 2 == 0:
                            banks.claim(bank, mixed_ready)
                        me.next(pt_ready)
                        rows = slice(HD * (h % 2), HD * (h % 2) + HD)
                        pe.matmul(bank[rows, 0:T], vtok[:, 0:HD], pt[:, 0:T], start=True, stop=False,
                                  skip_group_check=True)
                        pe.matmul(bank[rows, P:T], vtok[:, 72:72 + HD], pt[:, T:T + P], start=False, stop=True,
                                  skip_group_check=True).then_inc(pv_done, 1)
            if on("out0"):
                group_stats((0, 1), C("blk"), mix_sq, X[0:2])
            OPERANDS = [8]
            gemm("out0", dve_read, olo_from=8, order=(4, 5, 6, 7, 0, 1, 2, 3))

            def next_operand():
                OPERANDS[0] += KT
                return OPERANDS[0]

            def layer_norm():
                banks.claim(X[0], mean_ready)
                pe.wait_ge(dve_read, banks.n[dve_read.name])
                for t in range(KT):
                    ins = pe.matmul(X[0][:, 0:T], ones[:, :], tl(res, t), start=(t == 0), stop=(t == KT - 1))
                ins.then_inc(mean_done, 1)
                stats(X[1], sd_ready, part=2)

            def ffn(k, stat):
                if not on(f"gate_up{k}"):
                    return

                def after(at, t):
                    if stat and t == 0 and at.it is None and at.i == 0:
                        stats(X[0], sd_ready)

                gemm(f"gate_up{k}", gate_in, shape="gate_up", olo_from=next_operand(), after=after)
                gemm(f"down{k}", dve_read, shape="down")

            def ple(k):
                if not on(f"ple_proj{k}"):
                    return
                start = next_operand()
                gemm(f"ple_proj{k}", pp_ready, shape="ple")
                stats(X[0], sd_ready)
                gemm(f"ple_gate{k}", ple_in, olo_from=start)

            if on("gate_up0"):
                layer_norm()
            ffn(0, False)

            if on("gla_z"):
                layer_norm()
                start = next_operand()
                stats(X[0], sd_ready, tok=True)
                ph = PH["gla_z"]
                slot = ph.s0 % 2
                pe.wait_ge(landed[slot], ph.landed[0])
                banks.claim(X[1], z_ready)
                for k in range(KT):
                    pe.wait_ge(olo_ready, start + k + 1)
                    for d in range(2):
                        o = RANK * (2 * k + d)
                        ins = pe.matmul(X[1][32 * d:32 * d + RANK, 0:T], raw[slot][:, o:o + RANK], tl(om, k),
                                        start=(k == 0), stop=(k == KT - 1), skip_group_check=True)
                ins.then_inc(plain_used, 1)
            gemm("gla_q", dve_read)
            if on("gla_k"):
                pe.wait_ge(z_ready, 1)
                pe.wait_ge(gates_in, 32)
                for b in range(4):
                    banks.claim(X[b], la_read)
                    for half in range(2):
                        t = 2 * (b % 2) + half
                        ins = pe.matmul(X[b][:, half * T:(half + 1) * T],
                                        wgate[32 * (b // 2):32 * (b // 2) + RANK, P * t:P * (t + 1)],
                                        g_z[32 * (b // 2):32 * (b // 2) + RANK, :], start=True, stop=True)
                    ins.then_inc(la_done, 1)
            gemm("gla_k", dve_read)
            gemm("gla_v", v_ready, shape="token")
            gemm("gla_r", r_ready)
            if on("out1"):
                pe.wait_ge(kd_ready, 4)
                pe.wait_ge(ke_ready, 2)
                pe.wait_ge(v_ready, 4)

                def outputs(h):
                    bank = X[2 + h % 2]
                    banks.claim(bank, go_read)
                    pe.wait_ge(st_ready, h + 1)
                    first = True
                    for e in range(2):
                        for tt in range(TT):
                            v = g_v[:, tt * D + h * GDV + e * P:tt * D + h * GDV + e * P + P]
                            pe.matmul(bank[:, e * T + tt * P:e * T + (tt + 1) * P], v,
                                      tl(g_st, h % 2)[:, tt * P:(tt + 1) * P], start=first, stop=False,
                                      skip_group_check=True)
                            first = False
                    pe.wait_ge(u_read, 4 * (h + 1))
                    for e in range(2):
                        for d in range(2):
                            for n in range(3):
                                c = n + 1 if d == 0 else 2 - n
                                ins = pe.matmul(bank[:, e * T + c * CH:e * T + (c + 1) * CH],
                                                tl(state, 3 * d + n)[:, e * P:(e + 1) * P],
                                                tl(g_la[d], h)[:, c * CH:(c + 1) * CH], start=False,
                                                stop=(e == 1 and d == 1 and n == 2), skip_group_check=True)
                    ins.then_inc(go_done, 1)

                for h in range(GH + 1):
                    if h < GH:
                        banks.claim(G[0], gs_read)
                        for tt in range(TT):
                            for d in range(2):
                                o = (2 * tt + d) * P
                                ins = pe.matmul(G[0][:, o:o + P], tl(g_ke[d], h)[:, tt * P:(tt + 1) * P],
                                                tl(g_la[d], h)[:, tt * P:(tt + 1) * P], start=True, stop=True)
                        ins.then_inc(gs_done, 1)
                        banks.claim(G[1], kt_ready)
                        for d in range(2):
                            for tt in range(TT):
                                ins = pe.transpose(G[1][:, (2 * d + tt) * P:(2 * d + tt + 1) * P],
                                                   tl(g_b[d], h)[:, tt * P:(tt + 1) * P], ident)
                        ins.then_inc(kt_done, 1)
                    if h:
                        outputs(h - 1)
                    if h < GH:
                        pe.wait_ge(kt_ready, h + 1)
                        for bank in (X[1], X[0], G[2], G[3]):
                            banks.claim(bank, u_read)
                        for bank, half, d, c in ((X[1], 0, 1, 3), (X[0], 0, 1, 2), (G[2], 0, 0, 0), (G[3], 0, 0, 1),
                                                 (G[2], 1, 0, 2), (G[3], 1, 1, 1)):
                            rows = slice(CH * (c % 2), CH * (c % 2) + CH)
                            tt = c // 2
                            ins = pe.matmul(bank[:, half * T:(half + 1) * T],
                                            kd_tok[rows, (2 * d + tt) * P:(2 * d + tt + 1) * P],
                                            g_v[rows, tt * D + h * GDV:tt * D + (h + 1) * GDV], start=True, stop=True)
                        ins.then_inc(u_done, 1)
                for h in range(GH):
                    if h % 2 == 0:
                        banks.claim(G[h // 2], sd_ready)
                    me.next(sq_ready)
                    for e in range(2):
                        ins = pe.matmul(G[h // 2][:, (h % 2) * T:(h % 2 + 1) * T], ones[:, :], tl(g_sq, 2 * h + e),
                                        start=(e == 0), stop=(e == 1))
                    if h % 2:
                        ins.then_inc(stat_done, 1)
                start = next_operand()
                gemm("out1", dve_read, olo_from=start)
            ffn(1, True)
            ple(1)

            def block_sums(r):
                banks.claim(X[r % 2], qk_sd)
                me.next(qk_sq)
                pe.matmul(X[r % 2][:, :], C("blk"), tl(d_sq, r % 2, w=512), start=True, stop=True).then_inc(qk_stat, 1)

            def partners(r):
                banks.claim(X[2 + r % 2], qk_rot_read)
                pe.wait_ge(qk_normed, r + 1)
                src = tl(d_q, 2 * r, 2) if r < 4 else tl(d_k, 2 * r - 8, 2)
                pe.matmul(X[2 + r % 2][:, :], C("rot_d"), src, start=True, stop=True).then_inc(qk_rot, 1)

            start = next_operand() if on("diff_q") else 0
            for base, name in ((0, "diff_q"), (4, "diff_k")):
                def after(at, t, base=base):
                    r = base + 2 * at.i
                    if r == 0 and t == 0:
                        stats(X[0], sd_ready, tok=True)
                    if t == 1 and r:
                        partners(r - 2)
                    if t == 3:
                        if r:
                            partners(r - 1)
                        block_sums(r)
                        block_sums(r + 1)
                gemm(name, qk_src, olo_from=start if base == 0 else None, after=after)
            gemm("diff_v", v_ready, shape="token", after=lambda at, t: partners(6 + t) if at.i == 0 else None)
            if on("out2"):
                pe.wait_ge(qk_ready, 8)
                pe.wait_ge(v_ready, 8)
                for i in range(NH + 2):
                    if i < NH:
                        for c in range(2):
                            banks.claim(G[2 * (i % 2) + c], exp_done)
                        for qt in range(2):
                            for c in range(2):
                                rows = slice(HD * c, HD * c + HD)
                                ins = pe.matmul(G[2 * (i % 2) + c][:, qt * T:(qt + 1) * T],
                                                tl(d_q, i)[rows, qt * P:(qt + 1) * P], tl(d_k, i)[rows, :],
                                                start=True, stop=True)
                        ins.then_inc(score_done, 1)
                    if 1 <= i <= NH:
                        s = (i - 1) % 2
                        banks.claim(X[s], pt_ready)
                        me.next(prob_ready)
                        for kt in range(2):
                            for qt in range(2):
                                ins = pe.transpose(X[s][:, kt * T + qt * P:kt * T + (qt + 1) * P],
                                                   tl(d_p, 4 * s + qt)[:, kt * P:(kt + 1) * P], ident)
                        ins.then_inc(trans_done, 1)
                    if i >= 2:
                        h = i - 2
                        banks.claim(X[2 + h % 2], mixed_ready)
                        me.next(pt_ready)
                        for kt in range(2):
                            ins = pe.matmul(X[2 + h % 2][:, 0:T], d_v[:, kt * D + h * P:kt * D + (h + 1) * P],
                                            tl(d_pt, h % 2, w=512)[:, kt * T:(kt + 1) * T], start=(kt == 0), stop=(kt == 1))
                        ins.then_inc(pv_done, 1)
                group_stats((0, 1, 2, 3), ones[:, :], d_nsq, G)
                start = next_operand()
                gemm("out2", dve_read, olo_from=start)
            ffn(2, True)
            ple(2)
            if stop is None:
                pe.wait_ge(ple_added, 2 * KT)
                for n in range(4):
                    tt, half = n // 2, n % 2
                    banks.claim(G[n], out_read)
                    for k in range(4):
                        ins = pe.transpose(G[n][:, k * P:(k + 1) * P], tl(res, 4 * half + k)[:, tt * P:(tt + 1) * P], ident)
                    ins.then_inc(out_done, 1)


_INS = ["x", "c", "w_ada", "b_ada", "w_in", "conv_w", "attn_norm_g", "conv_norm_g", "w_out", "ln1_g", "ln1_b", "w_gate",
        "w_up", "w_down", "ln2_g", "ln2_b", "p_2", "norm_mix_2", "norm_ffn_2", "ffn_w_in_2", "ffn_w_out_2", "ple_norm_2",
        "ple_w_gate_2", "ple_w_proj_2", "gla_w_in_2", "gla_w_gate_f_2", "gla_b_gate_f_2", "gla_w_gate_b_2",
        "gla_b_gate_b_2", "gla_g_out_2", "gla_w_out_2", "diff_w_in_2", "diff_g_q_2", "diff_g_k_2", "diff_lam_q1_2",
        "diff_lam_k1_2", "diff_lam_q2_2", "diff_lam_k2_2", "diff_g_sub_2", "diff_w_out_2"]


def kernel(**inputs):
    import concourse.bacc as bacc
    from concourse.bass_utils import run_bass_kernel_spmd

    arrays = {f"in_{n}": np.ascontiguousarray(inputs[n]) for n in _INS}
    arrays["in_shape_constants"] = shape_constants()
    nc = bacc.Bacc("TRN2", target_bir_lowering=False, num_devices=1)
    a = {n[3:]: nc.dram_tensor(n, v.shape, F32, kind="ExternalInput").ap() for n, v in arrays.items()}
    out = nc.dram_tensor("out_0", (1, T, D), F32, kind="ExternalOutput").ap()
    build(nc, a, out)
    r = run_bass_kernel_spmd(nc, [arrays], core_ids=[0])
    return r.results[0]["out_0"]
```

```python
from contextlib import ExitStack

import numpy as np

import concourse.bass as bass
from concourse import mybir

F32 = mybir.dt.float32
F32R = mybir.dt.float32r
ALU = mybir.AluOpType
ACT = mybir.ActivationFunctionType
AX = mybir.AxisListType.X

P = 128
T = 256
D = 1024
KT = D // P
TT = T // P
F = 2816
FT = F // P
HD = 64
NH = 8
IH, ID = 8, 32
TOPK = 64
ALPHA = 2.0 ** 0.25
EPS1, EPS2 = 1e-5, 1e-6
GH, GDK, GDV = 4, 128, 256
CH, NCH = 64, 4
RANK, TAU = 16, 16.0
NEG = -1e30
TAKEN = -3e38
LAMBDA_INIT = 0.8 - 0.6 * float(np.exp(-0.3))
SLAB = 4096

QW = 512
C_K, C_V, C_QI, C_KI, C_WI, C_GB = 512, 576, 640, 896, 928, 936
C_GC, C_HC = C_GB + 512, C_GB + 1024

ROWS_A = [("b_ada", 48), ("ln1_g", 8), ("ln1_b", 8), ("ln2_g", 8), ("ln2_b", 8),
          ("attn_norm_g", 4), ("conv_norm_g", 4), ("conv_w", 12)]
ROWS_B = [("norm_mix_2", 16), ("norm_ffn_2", 16), ("ple_norm_2", 16), ("gla_b_gate_f_2", 4),
          ("gla_b_gate_b_2", 4), ("gla_g_out_2", 2), ("diff_g_sub_2", 1), ("diff_g_q_2", 1),
          ("diff_g_k_2", 1)]


def column_of(rows):
    at, n = {}, 0
    for name, k in rows:
        at[name] = n
        n += k
    return at, n


COL_A, NA = column_of(ROWS_A)
COL_B, NB = column_of(ROWS_B)

CONSTS = [("ident", P), ("blk", P), ("rot_q", P), ("rot_i", P), ("rot_d", P), ("cos_q", T), ("sin_q", T),
          ("cos_i", T), ("sin_i", T), ("cos_d", T), ("sin_d", T), ("causal", 3 * P), ("gla_mask", 2 * P)]
COL_C, NC = column_of(CONSTS)


def shape_constants():
    out = np.zeros((P, NC), np.float32)

    def put(name, a):
        out[:, COL_C[name]:COL_C[name] + a.shape[1]] = a

    p = np.arange(P)
    put("ident", np.eye(P))
    put("blk", (p[:, None] // HD == p[None, :] // HD) * 1.0)
    pos = np.arange(T, dtype=np.float32)
    for tag, width, half, theta in (("q", HD, 8, 500000.0), ("i", ID, 8, 500000.0), ("d", HD, 32, 10000.0)):
        rot = np.zeros((P, P))
        cos, sin = np.ones((P, T)), np.zeros((P, T))
        inv = (theta ** (-(np.arange(half) * 2.0) / (2 * half))).astype(np.float32)
        ang = (pos[None, :] * inv[:, None]).astype(np.float32).astype(np.float64)
        for m in range(P):
            d = m % width
            if d < 2 * half:
                rot[m + half if d < half else m - half, m] = -1.0 if d < half else 1.0
                cos[m], sin[m] = np.cos(ang[d % half]), np.sin(ang[d % half])
        put("rot_" + tag, rot)
        put("cos_" + tag, cos)
        put("sin_" + tag, sin)
    tri = np.where(p[None, :] <= p[:, None], 0.0, NEG)
    put("causal", np.concatenate([tri, np.zeros((P, P)), tri], 1))
    same = p[:, None] // CH == p[None, :] // CH
    put("gla_mask", np.concatenate([same & (p[:, None] <= p[None, :]), same & (p[:, None] > p[None, :])], 1) * 1.0)
    return out


POOL_SLABS = (4, 5, 6, 7)


class Phase:

    def __init__(self, name, n, cols, tiles, dmas, by="split", loop=False, ahead=True, ring=True,
                 slot=None):
        self.name, self.n, self.cols, self.tiles, self.dmas = name, n, cols, tiles, dmas
        self.by, self.split, self.loop, self.ahead, self.ring = by, by == "split", loop, ahead, ring
        self.slot = slot


def plan():
    ffn = lambda k: [Phase(f"gate_up{k}", FT // 2, SLAB, 4, 2, loop=True), Phase(f"down{k}", KT, F, 1, 2, loop=True)]
    ple = lambda k: [Phase(f"ple_proj{k}", 1, 2048, 8, 1), Phase(f"ple_gate{k}", 2, SLAB, 4, 1)]
    ada = lambda i: Phase(f"ada{i}", 1, SLAB, 0, 1, by="pool" if i in POOL_SLABS else "dve", ahead=False,
                          ring=i not in (2, 3), slot=0 if i in (0, 8, 9, 11) else 1)
    phases = [
        ada(0), ada(1), ada(2), ada(3),
        Phase("in_q", 1, SLAB, 4, 1, slot=0), Phase("in_idx", 1, SLAB, 4, 7, slot=1),
        Phase("in_v", 1, 8 * 72, 2, 2, slot=0), ada(4), Phase("in_gc", 1, SLAB, 4, 1, slot=0), ada(5),
        Phase("in_hc", 1, SLAB, 4, 1, slot=0), ada(6), Phase("in_gb", 1, SLAB, 4, 1, ahead=False, slot=0), ada(7),
        *[ada(i) for i in range(8, 12)],
        Phase("out0", 2, SLAB, 4, 1), *ffn(0),
        Phase("gla_z", 1, 8 * 3 * RANK, 0, 2, by="pe"), Phase("gla_q", 1, SLAB, 4, 1),
        Phase("gla_k", 1, SLAB, 4, 1), Phase("gla_v", 2, SLAB, 2, 1), Phase("gla_r", 2, SLAB, 4, 1),
        Phase("out1", 2, SLAB, 4, 1), *ffn(1), *ple(1),
        Phase("diff_q", 2, SLAB, 4, 1), Phase("diff_k", 2, SLAB, 4, 1), Phase("diff_v", 2, SLAB, 2, 1),
        Phase("out2", 2, SLAB, 4, 1), *ffn(2), *ple(2),
    ]
    slabs = []
    used = {"split": 0, "dve": 0, "pool": 0, "pe": 0}
    tile = 0
    slot_dmas, last = [0, 0], [None, None]
    for ph in phases:
        ph.s0, ph.j0, ph.tile0, ph.used0 = len(slabs), used["split"] // 4, tile, used[ph.by]
        if ph.slot is None:
            ph.slot = 1 - slot
        ph.landed, ph.free = [], []
        for _ in range(ph.n):
            used[ph.by] += 4 if ph.split else 1
            tile += ph.tiles
            if ph.ring:
                slot = (ph.slot + _) % 2
                slot_dmas[slot] += ph.dmas if ph.by != "pool" else 0
                ph.landed.append(16 * slot_dmas[slot])
                ph.free.append(last[slot])
                last[slot] = (ph.by, used[ph.by])
                slabs.append(last[slot])
    for n, ph in enumerate(phases):
        ph.next = next((q for q in phases[n + 1:] if q.split), None) if ph.ahead else None
    return phases


PHASES = plan()
PH = {ph.name: ph for ph in PHASES}


class At:

    def __init__(self, i, it=None, b=None):
        self.i, self.it, self.b = i, it, b
        self.parity = i % 2 if it is None else (1 + b) % 2

    def of(self, values):
        if self.it is None:
            return values[self.i]
        step = values[3 + self.b] - values[1 + self.b]
        return self.it * step + values[1 + self.b]

    def lin(self, base, per):
        return base + self.i * per if self.it is None else self.it * (2 * per) + (base + (1 + self.b) * per)


def rounds(eng, ph, body):
    pairs = (ph.n - 2) // 2 if ph.loop else 0
    if not pairs:
        for i in range(ph.n):
            body(At(i))
        return
    body(At(0))
    with eng.Fori(0, pairs) as it:
        for b in range(2):
            body(At(it * 2 + (1 + b), it, b))
    for i in range(1 + 2 * pairs, ph.n):
        body(At(i))


def wait(eng, sem, value):
    if not isinstance(value, int) or value > 0:
        eng.wait_ge(sem, value)


class Steps:

    def __init__(self, eng, own):
        self.eng, self.own, self.n = eng, own, {}

    def seen(self, sem, k=1):
        self.n[sem.name] = self.n.get(sem.name, 0) + k

    def next(self, sem, k=1):
        self.seen(sem, k)
        self.eng.wait_ge(sem, self.n[sem.name])

    def again(self, sem=None, less=0):
        sem = sem or self.own
        wait(self.eng, sem, self.n.get(sem.name, 0) - less)

    def did(self, ins, sem=None):
        sem = sem or self.own
        self.seen(sem)
        ins.then_inc(sem, 1)

    def link(self, ins, sem=None):
        self.did(ins, sem)
        self.again(sem)


class Banks:

    def __init__(self, pe):
        self.pe, self.n, self.last = pe, {}, {}

    def settle(self, b):
        if b.name in self.last:
            self.pe.wait_ge(*self.last[b.name])

    def claim(self, b, sem):
        self.settle(b)
        self.n[sem.name] = self.n.get(sem.name, 0) + 1
        self.last[b.name] = (sem, self.n[sem.name])
        return self.n[sem.name]

    def skip(self, b, sem, total):
        self.n[sem.name] = max(self.n.get(sem.name, 0), total)
        self.last[b.name] = (sem, total)


def build(nc, a, out, stop=None):
    ctx = ExitStack()
    with ctx:
        BASE = 16640
        ARENA = 53168
        ctx.enter_context(nc.sbuf_tensor("arena", [P, (BASE - nc.sbuf_base + 3) // 4 + ARENA], F32))
        taken = [0]
        place = {}

        def sb(name, words, dt=F32, at=None):
            o = taken[0] if at is None else at
            if at is None:
                taken[0] += (words + 7) // 8 * 8
            assert o + words <= ARENA, (name, o + words)
            place[name] = o
            return nc.alloc_sbuf_tensor_at(name, [P, words], dt, offset=BASE + 4 * o)

        raw = [sb(f"raw{i}", SLAB) for i in range(2)]
        whi = [sb(f"whi{i}", SLAB, F32R) for i in range(2)]
        wlo = [sb(f"wlo{i}", SLAB, F32R) for i in range(2)]
        const = sb("const", NC)
        ones = sb("ones", P)
        cols_a, cols_b = sb("cols_a", NA), sb("cols_b", NB)
        mod = sb("mod", 48)
        fold = sb("fold", 48)
        c_act = sb("c_act", 8)
        lam_in = sb("lam_in", 4 * HD)
        lam = sb("lam", 8)
        eps = sb("eps", 2)
        top8 = sb("top8", 16)
        neg_max = sb("neg_max", 2 * 4)
        sums = sb("sums", 2 * 4)
        rsum = sb("rsum", 2 * 4)
        decay = sb("decay", 32)
        total = sb("total", 32)
        wgate = sb("wgate", 512)
        res = sb("res", KT * T)
        om = sb("om", KT * T)
        ohi, olo = sb("ohi", KT * T, F32R), sb("olo", KT * T, F32R)
        p_hi, p_lo = sb("p_hi", 2 * 2 * T, F32R), sb("p_lo", 2 * 2 * T, F32R)
        mean = sb("mean", T)
        sq_sum = sb("sq_sum", T)
        rstd = sb("rstd", T + 2)
        work = sb("work", 2048)
        acthi, actlo = sb("acthi", FT * T, F32R), sb("actlo", FT * T, F32R)
        U = place["acthi"]

        xin, pin = sb("xin", 2048, at=place["work"]), sb("pin", 1024, at=U)
        rows_a, rows_b, rows_c = (sb(f"rows_{n}", P, at=U + 1024 + P * i) for i, n in enumerate("abc"))
        early = [sb(f"early{i}", SLAB, at=U + 1408 + SLAB * i) for i in range(2)]
        sq, pp = sb("sq", 2048, at=U), sb("pp", 2048, at=U + 4096)
        rope_in, rope_out = sb("rope_in", 2048, at=U), sb("rope_out", 2048, at=U + 2048)
        vtok = sb("vtok", 2 * 72, at=U + 4096)
        gc = sb("gc", 4 * T, at=U + 4352)
        upad = sb("upad", 4 * (T + 2), at=U + 5376)
        conv = sb("conv", 4 * T, at=U + 6408)
        mixed = sb("mixed", KT * T, at=U + 7432)
        relu = sb("relu", 2 * 384, at=U + 9480)
        score, kept = sb("score", 384, at=U + 10248), sb("kept", 384, at=U + 10632)
        mix_sq = sb("mix_sq", KT * T, at=U)
        W = place["work"]
        allow = sb("allow", 384, at=W)
        logit = sb("logit", 2 * 384, at=W + 384)
        prob_t = sb("prob_t", 2 * 384, at=W + 1152)
        gt, sg = sb("gt", 2 * T, at=W), sb("sg", 2 * T, at=W + 512)
        ut, prod = sb("ut", 2 * T, at=W + 1024), sb("prod", 2 * T, at=W + 1536)
        g_q, g_k = sb("g_q", 1024, at=U), sb("g_k", 1024, at=U + 1024)
        g_o = sb("g_o", 2048, at=U)
        g_v, g_r = sb("g_v", 2048, at=U + 2048), sb("g_r", 2048, at=U + 4096)
        g_la = [sb(f"g_la{d}", 1024, at=U + 6144 + 1024 * d) for d in range(2)]
        g_b = [sb(f"g_b{d}", 1024, at=U + 8192 + 1024 * d) for d in range(2)]
        g_ke = [sb(f"g_ke{d}", 1024, at=W + 1024 * d) for d in range(2)]
        g_m, g_st = sb("g_m", 512, at=U + 10240), sb("g_st", 512, at=U + 10752)
        g_sq = sb("g_sq", 2048, at=U + 6144)
        g_rs = sb("g_rs", 1024, at=U + 8192)
        O = place["om"]
        seg = [sb(f"seg{d}", 1024, at=O + 1024 * d) for d in range(2)]
        macc = sb("macc", 1024, at=O)
        state, kd_tok = sb("state", 1536, at=O), sb("kd_tok", 512, at=O + 1536)
        g_z = sb("g_z", T, at=place["mean"])
        d_q, d_k = sb("d_q", 2048, at=U), sb("d_k", 2048, at=U + 2048)
        d_v, d_o = sb("d_v", 2048, at=U + 4096), sb("d_o", 2048, at=U + 6144)
        d_p, d_pt = sb("d_p", 2048, at=U + 8192), sb("d_pt", 1024, at=U + 10240)
        d_sq, d_rs = sb("d_sq", 1024, at=U + 8192), sb("d_rs", 1024, at=U + 9216)
        d_t1, d_t2 = sb("d_t1", 512, at=U + 10240), sb("d_t2", 512, at=U + 10752)
        d_nsq = sb("d_nsq", 2048, at=U)
        o_tok = sb("o_tok", 2048, at=O)

        G = [ctx.enter_context(nc.psum_tensor(f"gemm{i}", [P, 512], F32)) for i in range(4)]
        X = [ctx.enter_context(nc.psum_tensor(f"aux{i}", [P, 512], F32)) for i in range(4)]

        def sem(name):
            return ctx.enter_context(nc.semaphore(name))

        landed = [sem("landed0"), sem("landed1")]
        side_in = sem("side_in")
        c_in, early_in = sem("c_in"), [sem("early_in0"), sem("early_in1")]
        params_in, gates_in, const_in, x_in = sem("params_in"), sem("gates_in"), sem("const_in"), sem("x_in")
        set_zero = sem("set_zero")
        hi_ready, lo_ready = sem("hi_ready"), sem("lo_ready")
        scaled_by_c, pool_summed, dve_summed = sem("scaled_by_c"), sem("pool_summed"), sem("dve_summed")
        z_done = sem("z_done")
        tile_done = sem("tile_done")
        dve_read = sem("dve_read")
        act_step, dve_step, pool_step = sem("act_step"), sem("dve_step"), sem("pool_step")
        setup_t, c_ready_t, c_ready, p_in = sem("setup_t"), sem("c_ready_t"), sem("c_ready"), sem("p_in")
        lam_sum, lam_exp = sem("lam_sum"), sem("lam_exp")
        om_ready, ohi_ready, olo_ready = sem("om_ready"), sem("ohi_ready"), sem("olo_ready")
        sq_ready, stat_done, sd_ready = sem("sq_ready"), sem("stat_done"), sem("sd_ready")
        squares_summed = sem("squares_summed")
        mean_done, mean_ready, centered, normed, res_ready = (
            sem("mean_done"), sem("mean_ready"), sem("centered"), sem("normed"), sem("res_ready"))
        rope_src, rope_cos, rot_done, rot_read, roped = (
            sem("rope_src"), sem("rope_cos"), sem("rot_done"), sem("rot_read"), sem("roped"))
        v_src, gc_ready, idx_done, relu_done, idx_acc = (
            sem("v_src"), sem("gc_ready"), sem("idx_done"), sem("relu_done"), sem("idx_acc"))
        mixed_ready, mod_done, mod_read = sem("mixed_ready"), sem("mod_done"), sem("mod_read")
        score_done, score_read, max_ready, exp_done, prob_ready = (
            sem("score_done"), sem("score_read"), sem("max_ready"), sem("exp_done"), sem("prob_ready"))
        trans_done, pt_ready, pv_done, pv_read = sem("trans_done"), sem("pt_ready"), sem("pv_done"), sem("pv_read")
        gate_in, up_in, silu_done, prod_done, acthi_ready, actlo_ready = (
            sem("gate_in"), sem("up_in"), sem("silu_done"), sem("prod_done"), sem("acthi_ready"), sem("actlo_ready"))
        pp_ready, ple_in, ple_sig, ple_prod = sem("pp_ready"), sem("ple_in"), sem("ple_sig"), sem("ple_prod")
        ple_added = sem("ple_added")
        z_ready, la_done, la_read, lg_ready, seg_ready, b_ready = (
            sem("z_ready"), sem("la_done"), sem("la_read"), sem("lg_ready"), sem("seg_ready"),
            sem("b_ready"))
        dist_ready, grow_ready, fall_ready, kd_ready, v_ready, r_ready, r_act = (
            sem("dist_ready"), sem("grow_ready"), sem("fall_ready"), sem("kd_ready"), sem("v_ready"),
            sem("r_ready"), sem("r_act"))
        ke_ready = sem("ke_ready")
        gs_done, gs_read, st_ready, kt_done, kt_ready, u_done, u_read, go_done, go_read, gated = (
            sem("gs_done"), sem("gs_read"), sem("st_ready"), sem("kt_done"), sem("kt_ready"), sem("u_done"),
            sem("u_read"), sem("go_done"), sem("go_read"), sem("gated"))
        qk_src, qk_sq, qk_stat, qk_sd, qk_normed, qk_cos, qk_rot, qk_rot_read, qk_ready = (
            sem("qk_src"), sem("qk_sq"), sem("qk_stat"), sem("qk_sd"), sem("qk_normed"), sem("qk_cos"),
            sem("qk_rot"), sem("qk_rot_read"), sem("qk_ready"))
        out_done, out_read, stored = sem("out_done"), sem("out_read"), sem("stored")

        def C(name, n=P):
            return const[:, COL_C[name]:COL_C[name] + n]

        def A(name, t=0, n=1):
            return cols_a[:, COL_A[name] + t:COL_A[name] + t + n]

        def B(name, t=0, n=1):
            return cols_b[:, COL_B[name] + t:COL_B[name] + t + n]

        def tl(buf, t, n=1, w=T):
            if isinstance(t, int):
                return buf[:, t * w:(t + n) * w]
            return buf[:, bass.ds(t * w, n * w)]

        def bc(ap, n):
            w = ap.shape[1]
            return ap.rearrange("p (r n) -> p r n", r=1).to_broadcast([P, n, w])

        def v3(ap, n):
            return ap.rearrange("p (r n) -> p r n", r=n)

        ident = C("ident")
        MOD_STEPS, MOD_TAKEN = {0: 8, 2: 9, 4: 10, 5: 11}, {0: (6,), 1: (8,), 3: (9, 7), 5: (10,), 6: (11,)}
        MOD_ORDER = (0, 1, 2, 3, 4, 5, 6, 8, 9, 7, 10, 11)
        mod_half = lambda i: i % 2 if i < 4 else int(i in POOL_SLABS)

        def half_free(i):
            before = [j for j in range(i) if mod_half(j) == mod_half(i)]
            return MOD_ORDER.index(before[-1]) + 1 if before else 0

        def kmaj(w, c0, n, i=0):
            v = w.rearrange("(k p) n -> p k n", p=P)
            return v[:, :, c0 + i * n:c0 + (i + 1) * n] if isinstance(i, int) else v[:, :, bass.ds(i * n + c0, n)]

        def flat(slot, k, n):
            buf = raw[slot] if isinstance(slot, int) else slot
            return buf[:, 0:k * n].rearrange("p (k n) -> p k n", k=k)

        w_in, ada = a["w_in"][0], a["w_ada"][0]
        gla_in, diff_in = a["gla_w_in_2"][0], a["diff_w_in_2"][0]

        def columns(w, c0):
            return lambda i, slot: [(flat(slot, KT, 512), kmaj(w, c0, 512, i))]

        def gate_up(wg, cg, wu, cu):
            def srcs(i, slot):
                v = raw[slot][:, :].rearrange("p (k g n) -> p k g n", k=KT, g=2)
                return [(v[:, :, 0, :], kmaj(wg, cg, 256, i)), (v[:, :, 1, :], kmaj(wu, cu, 256, i))]
            return srcs

        def down(w):
            def srcs(i, slot):
                v, s, h = flat(slot, FT, P), kmaj(w, 0, P, i), FT // 2
                return [(v[:, 0:h, :], s[:, 0:h, :]), (v[:, h:FT, :], s[:, h:FT, :])]
            return srcs

        def idx_slab(i, slot):
            v = flat(slot, KT, 512)
            return ([(v[:, :, 0:256], kmaj(w_in, C_QI, 256))]
                    + [(v[:, :, 256 + 32 * r:288 + 32 * r], kmaj(w_in, C_KI, ID)) for r in range(4)]
                    + [(v[:, :, 384 + 64 * r:448 + 64 * r], kmaj(w_in, C_K, HD)) for r in range(2)])

        def v_slab(i, slot):
            v = flat(slot, KT, 72)
            return [(v[:, :, 0:64], kmaj(w_in, C_V, HD)), (v[:, :, 64:72], kmaj(w_in, C_WI, IH))]

        def z_slab(i, slot):
            v = flat(slot, KT, 48)
            return [(v[:, :, 0:32], kmaj(gla_in, 3072, 32)), (v[:, :, 32:48], kmaj(gla_in, 3088, 16))]

        sources = {
            **{f"ada{i}": columns(ada, 512 * i) for i in range(12)},
            "in_q": columns(w_in, 0), "in_idx": idx_slab, "in_v": v_slab,
            "in_gc": columns(w_in, C_GC), "in_hc": columns(w_in, C_HC), "in_gb": columns(w_in, C_GB),
            "out0": columns(a["w_out"][0], 0),
            "gate_up0": gate_up(a["w_gate"][0], 0, a["w_up"][0], 0), "down0": down(a["w_down"][0]),
            "gla_z": z_slab,
            "gla_q": columns(gla_in, 0), "gla_k": columns(gla_in, 512), "gla_v": columns(gla_in, 1024),
            "gla_r": columns(gla_in, 2048), "out1": columns(a["gla_w_out_2"][0], 0),
            "diff_q": columns(diff_in, 0), "diff_k": columns(diff_in, 1024), "diff_v": columns(diff_in, 2048),
            "out2": columns(a["diff_w_out_2"][0], 0),
        }
        for k in (1, 2):
            f_in, w_p = a["ffn_w_in_2"][k - 1], a["ple_w_proj_2"][k - 1]
            sources[f"gate_up{k}"] = gate_up(f_in, 0, f_in, F)
            sources[f"down{k}"] = down(a["ffn_w_out_2"][k - 1])
            sources[f"ple_proj{k}"] = lambda i, slot, w_p=w_p: [(flat(slot, 2, D), kmaj(w_p, 0, D))]
            sources[f"ple_gate{k}"] = columns(a["ple_w_gate_2"][k - 1], 0)

        def on(name):
            return stop is None or PH[name].s0 < PH[stop].s0

        def bank_of(ph, at, t):
            if ph.tiles == 2:
                return (G[t], 72) if ph.name == "in_v" else (G[2 * at.parity + t], 512)
            return G[{1: at.parity, 4: t, 8: t % 4}[ph.tiles]], T

        def quarters(ph, t):
            return {1: (0, 1, 2, 3), 2: (2 * t, 2 * t + 1), 4: (t,), 8: () if t % 2 else (t // 2,)}[ph.tiles]

        def follow(ph, at):
            if at.it is not None:
                return ph, At(at.i + 1, at.it, at.b + 1)
            if at.i + 1 < ph.n:
                return ph, At(at.i + 1)
            return (ph.next, At(0)) if ph.next else None

        reader_done = {"split": lo_ready, "dve": dve_summed, "pool": pool_summed, "pe": z_done}
        block = ctx.enter_context(nc.Block())

        @block.sync
        def _(sp):
            sp.dma_start(rows_c[0:KT, :], a["c"][0].rearrange("(r n) -> r n", n=P)).then_inc(c_in, 16)
            sp.dma_start(ident, a["shape_constants"][:, 0:P]).then_inc(c_in, 16)
            for ph in PHASES:
                if not on(ph.name):
                    break
                if ph.by == "pool":
                    continue
                if not ph.ring:
                    i = int(ph.name[3:]) - 2
                    for dst, src in sources[ph.name](0, early[i]):
                        sp.dma_start(dst, src).then_inc(early_in[i], 16)
                    continue

                def load(at, ph=ph):
                    slot = (ph.slot + at.parity) % 2
                    if ph.free[0 if at.it is not None else at.i] is not None:
                        by = {f[0] for f in (ph.free[1:] if at.it is not None else [ph.free[at.i]])}
                        assert len(by) == 1
                        done = reader_done[by.pop()]
                        sp.wait_ge(done, at.of([f[1] if f else 0 for f in ph.free]))
                    for dst, src in sources[ph.name](at.i, slot):
                        sp.dma_start(dst, src).then_inc(landed[slot], 16)

                rounds(sp, ph, load)
                if ph.name == "ada1":
                    sp.dma_start(v3(xin[:, :], 2), a["x"][0].rearrange("(t p) n -> p t n", p=P)).then_inc(x_in, 16)
            if stop is None:
                for tt in range(TT):
                    sp.wait_ge(out_read, 2 * (tt + 1))
                    sp.dma_start(out[0, tt * P:(tt + 1) * P, :], tl(o_tok, tt, w=D)).then_inc(stored, 16)
                sp.wait_ge(stored, 16 * TT)

        @block.gpsimd
        def _(pool):
            me = Steps(pool, pool_step)
            me.did(pool.memset(ones[:, :], 1.0), set_zero)
            me.did(pool.memset(eps[:, 0:1], EPS1), set_zero)
            me.did(pool.memset(eps[:, 1:2], EPS2), set_zero)

            def rope_cosines(r):
                src, tiles, cos = ((2, (0, 1), "cos_q"), (4, (2, 3), "cos_q"), (8, (4, 7), None), (8, (5, 6), "cos_i"))[r]
                pool.wait_ge(rope_src, src)
                if r == 0:
                    pool.wait_ge(const_in, 16)
                if cos:
                    me.did(pool.tensor_tensor(v3(tl(rope_out, tiles[0], 2), 2), v3(tl(rope_in, tiles[0], 2), 2),
                                              bc(C(cos, T), 2), ALU.mult), rope_cos)
                else:
                    pool.tensor_tensor(tl(rope_out, 4), tl(rope_in, 4), C("cos_q", T), ALU.mult)
                    me.did(pool.tensor_tensor(tl(rope_out, 7), tl(rope_in, 7), C("cos_i", T), ALU.mult), rope_cos)

            if on("in_v"):
                rope_cosines(0)
                rope_cosines(1)
            POOL_ROPES = {4: (2, 3)}

            def sum_slab(i):
                ph = PH[f"ada{i}"]
                w = raw[ph.slot]
                me.next(scaled_by_c)
                me.link(pool.tensor_tensor(w[:, 0:2048], w[:, 0:2048], w[:, 2048:4096], ALU.add))
                me.link(pool.tensor_tensor(w[:, 0:1024], w[:, 0:1024], w[:, 1024:2048], ALU.add))
                wait(pool, mod_done, half_free(i))
                pool.wait_ge(olo_ready, KT)
                me.did(pool.tensor_tensor(tl(macc, mod_half(i), w=512), w[:, 0:512], w[:, 512:1024], ALU.add), pool_summed)

            for i in POOL_SLABS:
                ph = PH[f"ada{i}"]
                if on(ph.name):
                    by, count = ph.free[0]
                    pool.wait_ge(reader_done[by], count)
                    for dst, src in sources[ph.name](0, ph.slot):
                        pool.dma_start(dst, src).then_inc(side_in, 16)
                    if i in POOL_ROPES:
                        for r in POOL_ROPES[i]:
                            rope_cosines(r)
                    sum_slab(i)

            def ffn(k):
                ph = PH[f"gate_up{k}"]
                n0 = FT * k

                def body(at):
                    for j in range(2):
                        n = at.lin(n0 + j, 2)
                        t = at.lin(j, 2)
                        wait(pool, silu_done, n + 1)
                        wait(pool, up_in, n + 1)
                        wait(pool, actlo_ready, n - 1)
                        pool.tensor_tensor(tl(prod, j), tl(sg, j), tl(ut, j), ALU.mult).then_inc(prod_done, 1)
                        if not (isinstance(t, int) and t == 0):
                            wait(pool, acthi_ready, n)
                            pool.tensor_tensor(tl(actlo, t - 1), tl(prod, 1 - j), tl(acthi, t - 1).bitcast(F32),
                                               ALU.subtract).then_inc(actlo_ready, 1)

                rounds(pool, ph, body)
                wait(pool, acthi_ready, n0 + FT)
                pool.tensor_tensor(tl(actlo, FT - 1), tl(prod, 1), tl(acthi, FT - 1).bitcast(F32),
                                   ALU.subtract).then_inc(actlo_ready, 1)

            SQ_BEFORE = {"gla_z": 4 + 4 + 4, "gate_up1": GH, "gate_up2": 4}

            def skip_squares(name):
                me.seen(sq_ready, SQ_BEFORE[name])

            def sum_squares():
                me.next(sq_ready, 2)
                me.did(pool.tensor_tensor(sq_sum[:, :], tl(sq, 0), tl(sq, 1), ALU.add))
                for t in range(2, KT):
                    me.next(sq_ready)
                    me.again()
                    ins = pool.tensor_tensor(sq_sum[:, :], sq_sum[:, :], tl(sq, t), ALU.add)
                    me.did(ins) if t < KT - 1 else me.did(ins, squares_summed)

            def ple(k):
                for t in range(KT):
                    me.next(ple_sig)
                    if t == 0:
                        me.next(pp_ready, KT)
                    if t >= 2:
                        pool.wait_ge(ple_added, KT * (k - 1) + t - 1)
                    me.did(pool.tensor_tensor(tl(prod, t % 2), tl(sg, t % 2), tl(pp, t), ALU.mult), ple_prod)

            if on("gate_up0"):
                ffn(0)
            if on("gla_z"):
                skip_squares("gla_z")
                sum_squares()
                pool.wait_ge(z_ready, 1)
                for d in range(2):
                    me.link(pool.memset(seg[d][:, :], 1.0))
                    edge = 0 if d == 0 else CH - 1
                    me.did(pool.memset(v3(seg[d][:, :], 16)[:, :, edge:edge + 1], 0.0), seg_ready)
            if on("gla_r"):
                for d in range(2):
                    pool.wait_ge(grow_ready, 2 * d + 2)
                    me.did(pool.tensor_tensor(g_ke[d][:, :], g_k[:, :], g_ke[d][:, :], ALU.mult), ke_ready)
            if on("out1"):
                for h in range(GH):
                    pool.wait_ge(go_read, h + 1)
                    pool.wait_ge(r_act, 2)
                    me.did(pool.tensor_tensor(tl(g_r, 2 * h, 2), tl(g_o, 2 * h, 2), tl(g_r, 2 * h, 2), ALU.mult), gated)
            if on("gate_up1"):
                skip_squares("gate_up1")
                sum_squares()
                ffn(1)
            if on("ple_proj1"):
                sum_squares()
                ple(1)
            if on("diff_q"):
                sum_squares()
            if on("diff_v"):
                for r in range(8):
                    me.next(qk_normed)
                    buf, t = (d_q, 2 * r) if r < 4 else (d_k, 2 * r - 8)
                    if r >= 1:
                        pool.wait_ge(qk_ready, r)
                    me.did(pool.tensor_tensor(v3(d_t1[:, :], 2), v3(tl(buf, t, 2), 2), bc(C("cos_d", T), 2),
                                              ALU.mult), qk_cos)
            if on("gate_up2"):
                skip_squares("gate_up2")
                sum_squares()
                ffn(2)
            if on("ple_proj2"):
                sum_squares()
                ple(2)

        @block.scalar
        def _(act):
            me = Steps(act, act_step)

            act.wait_ge(c_ready_t, 1)
            me.did(act.activation(c_act[:, :], X[3][:, 48:56], ACT.Silu), c_ready)
            act.dma_start(const[:, P:NC], a["shape_constants"][:, P:NC]).then_inc(const_in, 16)
            act.dma_start(pin[:, :].rearrange("p (l t n) -> p l t n", l=2, t=2),
                          a["p_2"].rearrange("l b (t p) n -> p l (b t) n", p=P)).then_inc(p_in, 16)
            for rows, spec in ((rows_a, ROWS_A), (rows_b, ROWS_B)):
                n = 0
                for name, k in spec:
                    ap = a[name]
                    flat_ap = ap.rearrange(" ".join("abc"[:len(ap.shape)]) + " -> (" + " ".join("abc"[:len(ap.shape)]) + ")")
                    act.dma_start(rows[n:n + k, :], flat_ap.rearrange("(r n) -> r n", n=P)).then_inc(params_in, 16)
                    n += k
            for n, name in enumerate(("diff_lam_q1_2", "diff_lam_k1_2", "diff_lam_q2_2", "diff_lam_k2_2")):
                act.dma_start(lam_in[:, n * HD:(n + 1) * HD], a[name].to_broadcast([P, HD])).then_inc(params_in, 16)
            act.dma_start(wgate[0:RANK, :], a["gla_w_gate_f_2"][0]).then_inc(gates_in, 16)
            act.dma_start(wgate[32:32 + RANK, :], a["gla_w_gate_b_2"][0]).then_inc(gates_in, 16)

            def split(ph, at, q):
                slot, w = (ph.slot + at.parity) % 2, ph.cols // 4
                hslot = (ph.j0 + at.parity) % 2
                if q == 0:
                    act.wait_ge(landed[slot], at.of(ph.landed))
                act.activation(whi[hslot][:, q * w:(q + 1) * w], raw[slot][:, q * w:(q + 1) * w],
                               ACT.Copy).then_inc(hi_ready, 1)

            def ahead(ph, at, q):
                nxt = follow(ph, at)
                if nxt is None or not on(nxt[0].name):
                    return
                if q == 0:
                    wait(act, tile_done, at.lin(ph.tile0, ph.tiles))
                split(*nxt, q)

            def prep(order=range(KT), free=None, squares=False, then=None):
                if free:
                    wait(act, tile_done, free)
                for t in order:
                    me.next(om_ready)
                    me.did(act.activation(tl(ohi, t), tl(om, t), ACT.Copy), ohi_ready)
                    if then:
                        then(t)
                    if squares:
                        me.did(act.activation(tl(sq, t), tl(res, t), ACT.Square), sq_ready)

            def root(bank, n, scale, e, dst, done=stat_done, ready=sd_ready):
                me.next(done)
                me.link(act.activation(dst, bank[:, 0:n], ACT.Ln, bias=eps[:, e:e + 1], scale=scale))
                me.did(act.activation(dst, dst, ACT.Exp, scale=-0.5), ready)

            def roots(pairs, scale, e, done=stat_done, ready=sd_ready):
                for bank, dst in pairs:
                    me.next(done)
                    me.did(act.activation(dst, bank[:, :], ACT.Ln, bias=eps[:, e:e + 1], scale=scale))
                me.again()
                for bank, dst in pairs:
                    me.did(act.activation(dst, dst, ACT.Exp, scale=-0.5), ready)

            def group_root(groups, src, buf, scale, e, banks, then=None):
                for n, g in enumerate(groups):
                    me.next(mixed_ready, 2)
                    me.did(act.activation(tl(buf, 2 * g, 2), tl(src, 2 * g, 2), ACT.Square), sq_ready)
                if then:
                    then()
                roots([(banks[n], tl(buf, 2 * g, 2)) for n, g in enumerate(groups)], scale, e)

            act.wait_ge(set_zero, 3)
            if on("in_q"):
                for q in range(4):
                    split(PH["in_q"], At(0), q)
                prep()
            act.wait_ge(lam_sum, 1)
            me.did(act.activation(lam[:, 2:4], lam[:, 0:2], ACT.Exp), lam_exp)

            def evac(dst_of, sem_, scale_of=None):
                def one(ph, at, t):
                    wait(act, tile_done, at.lin(ph.tile0 + t + 1, ph.tiles))
                    bank, n = bank_of(ph, at, t)
                    kw = {"scale": scale_of(t)} if scale_of else {}
                    me.did(act.activation(dst_of(at, t), bank[:, 0:n], ACT.Copy, **kw), sem_)
                return one

            def gemm(name, one=None, after=None):
                if not on(name):
                    return
                ph = PH[name]

                def body(at):
                    for t in range(ph.tiles):
                        for q in quarters(ph, t):
                            ahead(ph, at, q)
                        if one:
                            one(ph, at, t)
                        if after:
                            after(at, t)

                rounds(act, ph, body)

            def scale_by_c(i):
                ph = PH[f"ada{i}"]
                act.wait_ge(side_in, 16 * (POOL_SLABS.index(i) + 1))
                for k in range(KT):
                    w = raw[ph.slot][:, 512 * k:512 * (k + 1)]
                    ins = act.activation(w, w, ACT.Copy, scale=c_act[:, k:k + 1])
                me.did(ins, scaled_by_c)

            gemm("in_q", evac(lambda at, t: tl(rope_in, t), rope_src))
            gemm("in_idx", evac(lambda at, t: tl(rope_in, (5, 6, 7, 4)[t]), rope_src))
            gemm("in_v", evac(lambda at, t: vtok[:, 72 * t:72 * t + 72], v_src))
            if on("ada4"):
                scale_by_c(4)
            gemm("in_gc", evac(lambda at, t: tl(gc, t), gc_ready))
            if on("in_hc"):
                for h in range(IH):
                    me.next(idx_done)
                    if h >= 2:
                        act.wait_ge(idx_acc, 2 * (h - 1))
                    me.did(act.activation(tl(relu, h % 2, w=384), G[h % 4][:, 0:384], ACT.Relu), relu_done)
            if on("ada6"):
                scale_by_c(5)
            gemm("in_hc")
            if on("ada6"):
                scale_by_c(6)
            gemm("in_gb")
            if on("ada11"):
                group_root((2, 3), mixed, mix_sq, 1.0 / HD, 0, X[0:2])
                prep(order=(4, 5, 6, 7), free=PH["in_gb"].tile0 + 4)
                scale_by_c(7)
                for i in range(NH + 1):
                    if i < NH:
                        me.next(max_ready)
                        for qt, (c0, n) in enumerate(((0, P), (P, 2 * P))):
                            ap = logit[:, 384 * (i % 2) + c0:384 * (i % 2) + c0 + n]
                            ins = act.activation(ap, ap, ACT.Exp, bias=neg_max[:, 2 * (i % 2) + qt:2 * (i % 2) + qt + 1],
                                                 accum_out=sums[:, 2 * (i % 2) + qt:2 * (i % 2) + qt + 1])
                        me.did(ins, exp_done)
                    if i >= 1:
                        me.next(trans_done)
                        if i >= 3:
                            act.wait_ge(pv_done, i - 2)
                        me.did(act.activation(tl(prob_t, (i - 1) % 2, w=384), G[2 + (i - 1) % 2][:, 0:384],
                                              ACT.Copy), pt_ready)
            if on("out0"):
                group_root((0, 1), mixed, mix_sq, 1.0 / HD, 0, X[0:2],
                           lambda: [split(PH["out0"], At(0), q) for q in range(4)])
                prep(order=(0, 1, 2, 3))
            gemm("out0")

            def layer_norm(n, squares):
                for t in range(0, KT, 2):
                    me.next(centered)
                    me.did(act.activation(tl(sq, t, 2), tl(res, t, 2), ACT.Square), sq_ready)
                root(X[1], T, 1.0 / D, 0, rstd[:, 0:T])
                g, b = (fold[:, 16:24], fold[:, 24:32]) if n == 0 else (A("ln2_g", 0, 8), A("ln2_b", 0, 8))

                def then(t):
                    me.link(act.activation(tl(res, t), tl(res, t), ACT.Identity, bias=b[:, t:t + 1],
                                           scale=g[:, t:t + 1]), res_ready)
                prep(free=PH["out0" if n == 0 else "down0"].tile0 + 8, squares=squares, then=then)

            def ffn(k):
                if not on(f"gate_up{k}"):
                    return
                n0 = FT * k

                def high(n, t, j):
                    wait(act, prod_done, n + 1)
                    act.activation(tl(acthi, t), tl(prod, j), ACT.Copy).then_inc(acthi_ready, 1)

                def after(at, t):
                    if t % 2 == 0:
                        return
                    j = t // 2
                    n, m = at.lin(n0 + j, 2), at.lin(j, 2)
                    wait(act, gate_in, n + 1)
                    wait(act, prod_done, n - 1)
                    act.activation(tl(sg, j), tl(gt, j), ACT.Silu).then_inc(silu_done, 1)
                    if not (isinstance(m, int) and m == 0):
                        high(n - 1, m - 1, 1 - j)

                gemm(f"gate_up{k}", after=after)
                high(n0 + FT - 1, FT - 1, 1)
                gemm(f"down{k}")

            if on("gate_up0"):
                layer_norm(0, False)
            ffn(0)
            if on("gla_z"):
                layer_norm(1, True)
                root(X[0], T + 2, 1.0 / D, 1, rstd[:, :])
            gemm("gla_q")
            gemm("gla_k")
            if on("gla_v"):
                for d in range(2):
                    act.wait_ge(la_read, 2 * d + 2)
                    me.link(act.activation(g_b[d][:, :], g_la[d][:, :], ACT.Abs))
                    me.link(act.activation(g_b[d][:, :], g_b[d][:, :], ACT.Exp, scale=-1.0))
                    me.did(act.activation(g_b[d][:, :], g_b[d][:, :], ACT.Ln, bias=ones[:, 0:1]), lg_ready)

            def v_dst(buf):
                return lambda at, t: buf[:, t * D + at.i * 512:t * D + at.i * 512 + 512]

            v_scale = lambda t: rstd[:, T + t:T + t + 1]
            if on("gla_v"):
                act.wait_ge(z_ready, 1)
            ph = PH["gla_v"]
            v_evac = evac(v_dst(g_v), v_ready, v_scale)

            def gla_after(at, t):
                if at.i == 1 and t == 0:
                    for d in range(2):
                        me.next(b_ready)
                        me.did(act.activation(g_la[d][:, :], g_b[d][:, :], ACT.Exp, scale=1.0 / TAU), grow_ready)
                        me.did(act.activation(g_ke[d][:, :], g_b[d][:, :], ACT.Exp, scale=-1.0 / TAU), grow_ready)
                if at.i == 1 and t == 1:
                    for d in range(2):
                        me.next(dist_ready)
                        me.did(act.activation(g_b[d][:, :], g_b[d][:, :], ACT.Exp, scale=1.0 / TAU), fall_ready)

            gemm("gla_v", v_evac, gla_after)
            gemm("gla_r")
            if on("out1"):
                for d in range(2):
                    act.wait_ge(r_ready, 4 * (d + 1))
                    me.did(act.activation(tl(g_r, 4 * d, 4), tl(g_r, 4 * d, 4), ACT.Silu), r_act)
                for h in range(GH):
                    me.next(kt_done)
                    me.did(act.activation(kd_tok[:, :], G[1][:, :], ACT.Copy), kt_ready)
                for h in range(GH):
                    act.wait_ge(go_read, GH)
                    me.did(act.activation(tl(g_sq, 2 * h, 2), tl(g_o, 2 * h, 2), ACT.Square), sq_ready)
                roots([(G[n], g_rs[:, 512 * n:512 * n + 512]) for n in range(2)], 1.0 / GDV, 1)
                prep(free=PH["gla_r"].tile0 + 8)
            gemm("out1")

            def rms(free, full):
                prep(free=free, squares=True)
                root(X[0], T + 2 if full else T, 1.0 / D, 1, rstd[:, 0:T + 2 if full else T])

            def ple(k):
                if not on(f"ple_proj{k}"):
                    return
                prep(free=PH[f"gate_up{k}"].tile0 + 4 * PH[f"gate_up{k}"].n, squares=True)
                gemm(f"ple_proj{k}", evac(lambda at, t: tl(pp, t), pp_ready))
                root(X[0], T, 1.0 / D, 1, rstd[:, 0:T])

                def after(at, t):
                    n = KT * (k - 1) + 4 * at.i + t
                    act.wait_ge(ple_in, n + 1)
                    wait(act, ple_prod, n - 1)
                    act.activation(tl(sg, t % 2), tl(gt, t % 2), ACT.Sigmoid).then_inc(ple_sig, 1)

                gemm(f"ple_gate{k}", after=after)

            if on("gate_up1"):
                rms(PH["out1"].tile0 + 8, False)
            ffn(1)
            ple(1)
            if on("diff_q"):
                rms(PH["ple_gate1"].tile0 + 8, True)
            for base, name in ((0, "diff_q"), (4, "diff_k")):
                def after(at, t, base=base):
                    buf = d_q if base == 0 else d_k
                    if t % 2 == 1:
                        r = base + 2 * at.i + t // 2
                        act.wait_ge(qk_src, 2 * r + 2)
                        if r >= 2:
                            act.wait_ge(qk_stat, r - 1)
                        me.did(act.activation(tl(d_sq, r % 2, w=512), tl(buf, 2 * (r - base), 2), ACT.Square), qk_sq)
                    if t == 3:
                        r = base + 2 * at.i
                        if r >= 2:
                            act.wait_ge(qk_normed, r)
                        roots([(X[n], tl(d_rs, n, w=512)) for n in range(2)], 1.0 / HD, 1, qk_stat, qk_sd)
                gemm(name, after=after)
            gemm("diff_v", evac(v_dst(d_v), v_ready, v_scale))
            if on("out2"):
                for i in range(NH + 1):
                    if i < NH:
                        me.next(max_ready)
                        for c in range(2):
                            for qt in range(2):
                                n = 4 * (i % 2) + 2 * c + qt
                                if i >= 2:
                                    act.wait_ge(trans_done, NH + i - 1)
                                ins = act.activation(tl(d_p, 4 * (i % 2) + 2 * c + qt),
                                                     G[2 * (i % 2) + c][:, qt * T:(qt + 1) * T], ACT.Exp,
                                                     bias=neg_max[:, n:n + 1], scale=HD ** -0.5,
                                                     accum_out=sums[:, n:n + 1])
                            me.did(ins, exp_done)
                    if i >= 1:
                        me.next(trans_done)
                        if i >= 3:
                            act.wait_ge(pv_done, NH + i - 2)
                        me.did(act.activation(tl(d_pt, (i - 1) % 2, w=512), X[(i - 1) % 2][:, :], ACT.Copy), pt_ready)
                group_root((0, 1, 2, 3), d_o, d_nsq, 1.0 / (2 * HD), 1, G)
                prep(free=PH["diff_v"].tile0 + 4)
            gemm("out2")
            if on("gate_up2"):
                rms(PH["out2"].tile0 + 8, False)
            ffn(2)
            ple(2)

        @block.vector
        def _(dve):
            me = Steps(dve, dve_step)

            def low(ph, at, q):
                slot, w = (ph.slot + at.parity) % 2, ph.cols // 4
                hslot = (ph.j0 + at.parity) % 2
                dve.wait_ge(hi_ready, at.lin(4 * ph.j0 + q + 1, 4))
                dve.tensor_tensor(wlo[hslot][:, q * w:(q + 1) * w], raw[slot][:, q * w:(q + 1) * w],
                                  whi[hslot][:, q * w:(q + 1) * w].bitcast(F32), ALU.subtract).then_inc(lo_ready, 1)

            def gemm(name, one=None, after=None):
                if not on(name):
                    return
                ph = PH[name]

                def body(at):
                    for t in range(ph.tiles):
                        nxt = follow(ph, at)
                        if nxt is not None and on(nxt[0].name):
                            for q in quarters(ph, t):
                                low(*nxt, q)
                        if one:
                            wait(dve, tile_done, at.lin(ph.tile0 + t + 1, ph.tiles))
                            one(at, t, bank_of(ph, at, t)[0])
                        if after:
                            after(at, t)

                rounds(dve, ph, body)

            def prep(make, order=range(KT), free=None):
                if free:
                    wait(dve, tile_done, free)

                def rest(t):
                    me.next(ohi_ready)
                    me.did(dve.tensor_tensor(tl(olo, t), tl(om, t), tl(ohi, t).bitcast(F32), ALU.subtract), olo_ready)

                last = None
                for t in order:
                    me.did(make(t), om_ready)
                    if last is not None:
                        rest(last)
                    last = t
                rest(last)

            def modulate(i):
                ph = PH[f"ada{i}"]
                if ph.ring:
                    src, came = raw[ph.slot], (landed[ph.slot], ph.landed[0])
                else:
                    src, came = early[i - 2], (early_in[i - 2], 16)
                acc = tl(macc, mod_half(i), w=512)
                dve.wait_ge(*came)
                wait(dve, mod_done, half_free(i))
                me.link(dve.tensor_scalar(acc, src[:, 0:512], c_act[:, 0:1], None, ALU.mult))
                for k in range(1, KT - 1):
                    me.link(dve.scalar_tensor_tensor(acc, src[:, 512 * k:512 * (k + 1)], c_act[:, k:k + 1], acc,
                                                     ALU.mult, ALU.add))
                k = KT - 1
                me.did(dve.scalar_tensor_tensor(acc, src[:, 512 * k:512 * (k + 1)], c_act[:, k:k + 1], acc,
                                                ALU.mult, ALU.add), dve_summed)

            dve.wait_ge(set_zero, 3)
            dve.wait_ge(c_ready, 1)
            modulate(0)
            modulate(1)
            for n, bank in enumerate((X[0], X[1], X[2], G[1])):
                me.next(setup_t)
                me.did(dve.tensor_copy(tl(res, n, w=512), bank[:, :]), dve_read)
            modulate(2)
            modulate(3)
            me.next(setup_t)
            me.did(dve.tensor_copy(cols_b[:, :], G[0][:, P:P + NB]))
            me.did(dve.tensor_copy(cols_a[:, :], G[0][:, 0:NA]), dve_read)
            dve.wait_ge(mod_done, 4)
            me.again(dve_read)
            me.link(dve.tensor_tensor(mod[:, 0:16], X[3][:, 0:16], A("b_ada", 0, 16), ALU.add), mod_read)
            me.link(dve.tensor_scalar(mod[:, 8:16], mod[:, 8:16], 1.0, None, ALU.add))
            if on("in_q"):
                prep(lambda t: dve.tensor_scalar(tl(om, t), tl(res, t), mod[:, 8 + t:9 + t], mod[:, t:t + 1],
                                                 ALU.mult, ALU.add))
                for q in range(4):
                    low(PH["in_q"], At(0), q)
            me.did(dve.tensor_scalar(res[:, :], res[:, :], ALPHA, None, ALU.mult))
            for layer in range(2):
                me.next(setup_t)
                bank = G[2 + layer]
                me.link(dve.tensor_copy(tl(p_hi, layer, w=512), bank[:, :]))
                me.did(dve.tensor_tensor(tl(p_lo, layer, w=512), bank[:, :], tl(p_hi, layer, w=512).bitcast(F32),
                                         ALU.subtract), dve_read)
            me.did(dve.memset(v3(upad[:, :], 4)[:, :, 0:2], 0.0))
            lam4 = lam_in[:, :].rearrange("p (e s n) -> p e s n", e=2, s=2)
            me.link(dve.tensor_tensor(lam4[:, :, 0, :], lam4[:, :, 0, :], lam4[:, :, 1, :], ALU.mult))
            me.did(dve.tensor_reduce(lam[:, 0:2], lam4[:, :, 0, :], AX, ALU.add), lam_sum)
            me.next(lam_exp)
            me.link(dve.tensor_tensor(lam[:, 4:5], lam[:, 3:4], lam[:, 2:3], ALU.subtract))
            me.link(dve.tensor_scalar(lam[:, 4:5], lam[:, 4:5], -LAMBDA_INIT, None, ALU.add))
            me.did(dve.tensor_scalar(lam[:, 5:6], B("diff_g_sub_2"), 1.0 - LAMBDA_INIT, None, ALU.mult))

            def rope(r):
                bank = X[(0, 1, 2, 0)[r]]
                me.next(rot_done)
                if r == 2:
                    dve.tensor_tensor(tl(mixed, 4), bank[:, 0:T], C("sin_q", T), ALU.mult)
                    me.did(dve.tensor_tensor(tl(mixed, 7), bank[:, T:2 * T], C("sin_i", T), ALU.mult), rot_read)
                    pairs = ((4, 1), (7, 1))
                else:
                    t = (0, 2, None, 5)[r]
                    me.did(dve.tensor_tensor(v3(tl(mixed, t, 2), 2), v3(bank[:, :], 2),
                                             bc(C("sin_i" if r == 3 else "sin_q", T), 2), ALU.mult), rot_read)
                    pairs = ((t, 2),)
                me.next(rope_cos)
                me.again(rot_read)
                for t, n in pairs:
                    ins = dve.tensor_tensor(tl(rope_out, t, n), tl(rope_out, t, n), tl(mixed, t, n), ALU.add)
                me.did(ins, roped)

            gemm("in_q")
            gemm("in_idx")
            if on("in_v"):
                rope(0)
                rope(1)
            gemm("in_v")
            if on("in_gc"):
                rope(2)
                rope(3)
                me.next(v_src, 2)
                me.link(dve.tensor_scalar(v3(vtok[:, :], 2)[:, :, 64:72], v3(vtok[:, :], 2)[:, :, 64:72],
                                          IH ** -0.5 * ID ** -0.5, None, ALU.mult))
            gemm("in_gc")
            BLOCKS = ((0, 0, P), (1, P, 2 * P))
            if on("in_hc"):
                for h in range(IH):
                    me.next(relu_done)
                    for tt, c0, n in BLOCKS:
                        w = vtok[:, 72 * tt + 64 + h:72 * tt + 65 + h]
                        r = relu[:, 384 * (h % 2) + c0:384 * (h % 2) + c0 + n]
                        if h:
                            me.again(idx_acc, less=1)
                            me.did(dve.scalar_tensor_tensor(score[:, c0:c0 + n], r, w, score[:, c0:c0 + n],
                                                            ALU.mult, ALU.add), idx_acc)
                        else:
                            me.did(dve.tensor_scalar(score[:, c0:c0 + n], r, w, None, ALU.mult), idx_acc)

            def short_conv(at, t, bank):
                u = upad[:, (T + 2) * t:(T + 2) * (t + 1)]
                me.next(gc_ready)
                me.link(dve.tensor_tensor(u[:, 2:T + 2], bank[:, 0:T], tl(gc, t), ALU.mult), dve_read)
                me.link(dve.tensor_scalar(tl(conv, t), u[:, 0:T], A("conv_w", t), None, ALU.mult))
                for j in (1, 2):
                    me.link(dve.scalar_tensor_tensor(tl(conv, t), u[:, j:j + T], A("conv_w", 4 * j + t), tl(conv, t),
                                                     ALU.mult, ALU.add))

            gemm("in_hc", short_conv)
            if on("in_gb"):
                me.again(idx_acc)
                me.link(dve.tensor_tensor(kept[:, :], score[:, :], C("causal", 384), ALU.add))
                for _ in range(TOPK // 8):
                    for tt, c0, n in BLOCKS:
                        me.did(dve.max(top8[:, 8 * tt:8 * tt + 8], kept[:, c0:c0 + n]))
                    for tt, c0, n in BLOCKS:
                        me.again(less=1)
                        me.did(dve.match_replace(kept[:, c0:c0 + n], top8[:, 8 * tt:8 * tt + 8], kept[:, c0:c0 + n],
                                                 TAKEN))
                    me.again()
                me.link(dve.tensor_scalar(allow[:, :], kept[:, :], TAKEN / 1e3, NEG, ALU.is_gt, ALU.mult))
                me.did(dve.tensor_tensor(allow[:, :], allow[:, :], C("causal", 384), ALU.add))

            def gated_conv(at, t, bank):
                me.did(dve.tensor_tensor(tl(mixed, 4 + t), bank[:, 0:T], tl(conv, t), ALU.mult), mixed_ready)

            gemm("in_gb", gated_conv)

            def group_make(src, buf, gain):
                def make(t):
                    if t % 2 == 0:
                        me.next(sd_ready)
                    return dve.scalar_tensor_tensor(tl(om, t), tl(src, t), gain(t), tl(buf, t), ALU.mult, ALU.mult)
                return make

            if on("ada11"):
                mix_make = group_make(mixed, mix_sq, lambda t: A("attn_norm_g", t) if t < 4 else A("conv_norm_g", t - 4))
                me.again(mixed_ready)
                prep(mix_make, order=(4, 5, 6, 7), free=PH["in_gb"].tile0 + 4)
                me.again()
                for i in range(NH + 2):
                    if i < NH:
                        me.next(score_done)
                        if i >= 2:
                            dve.wait_ge(trans_done, i - 1)
                        lg = tl(logit, i % 2, w=384)
                        me.link(dve.scalar_tensor_tensor(lg, G[i % 2][:, 0:384], HD ** -0.5, allow[:, :],
                                                         ALU.mult, ALU.add), score_read)
                        for tt, c0, n in BLOCKS:
                            ins = dve.tensor_reduce(neg_max[:, 2 * (i % 2) + tt:2 * (i % 2) + tt + 1], lg[:, c0:c0 + n],
                                                    AX, ALU.max, negate=True)
                        me.did(ins, max_ready)
                    if i in MOD_STEPS:
                        modulate(MOD_STEPS[i])
                    if 1 <= i <= NH:
                        me.next(exp_done)
                        s = (i - 1) % 2
                        me.link(dve.reciprocal(rsum[:, 2 * s:2 * s + 2], sums[:, 2 * s:2 * s + 2]))
                        for tt, c0, n in BLOCKS:
                            ap = logit[:, 384 * s + c0:384 * s + c0 + n]
                            ins = dve.tensor_scalar(ap, ap, rsum[:, 2 * s + tt:2 * s + tt + 1], None, ALU.mult)
                        me.did(ins, prob_ready)
                    if i >= 3 and i % 2:
                        me.next(pv_done, 2)
                        me.did(dve.tensor_copy(tl(mixed, (i - 2) // 2), X[(i - 2) // 2 % 2][:, 0:T]), mixed_ready)
                dve.wait_ge(mod_done, 12)
                me.link(dve.tensor_tensor(mod[:, 16:48], X[3][:, 16:48], A("b_ada", 16, 32), ALU.add), mod_read)
                me.link(dve.tensor_scalar(mod[:, 32:40], mod[:, 32:40], 1.0, None, ALU.add))
                me.did(dve.tensor_tensor(fold[:, 0:8], A("ln1_g", 0, 8), mod[:, 32:40], ALU.mult))
                me.link(dve.tensor_tensor(fold[:, 8:16], A("ln1_b", 0, 8), mod[:, 32:40], ALU.mult))
                me.did(dve.tensor_tensor(fold[:, 8:16], fold[:, 8:16], mod[:, 24:32], ALU.add))
                me.did(dve.tensor_scalar(fold[:, 16:24], A("ln1_g", 0, 8), ALPHA, None, ALU.mult))
                me.did(dve.tensor_scalar(fold[:, 24:32], A("ln1_b", 0, 8), ALPHA, None, ALU.mult))
                me.did(dve.tensor_tensor(fold[:, 32:40], A("ln2_g", 0, 8), B("norm_mix_2", 0, 8), ALU.mult))
                me.link(dve.tensor_tensor(fold[:, 40:48], A("ln2_b", 0, 8), B("norm_mix_2", 0, 8), ALU.mult))
            if on("out0"):
                for q in range(4):
                    low(PH["out0"], At(0), q)
                me.again(mixed_ready)
                prep(mix_make, order=(0, 1, 2, 3))

            def residual(gate=None):
                def one(at, t, bank):
                    m = at.lin(t, PH_tiles[0])
                    if gate is None:
                        ins = dve.tensor_tensor(tl(res, m), bank[:, 0:T], tl(res, m), ALU.add)
                    else:
                        g = mod[:, gate + m:gate + m + 1] if isinstance(m, int) else mod[:, bass.ds(m + gate, 1)]
                        ins = dve.scalar_tensor_tensor(tl(res, m), bank[:, 0:T], g, tl(res, m), ALU.mult, ALU.add)
                    ins.then_inc(dve_read, 1)
                return one

            PH_tiles = [4]

            def add_to_residual(name, gate=None):
                PH_tiles[0] = PH[name].tiles
                gemm(name, residual(gate))
                if on(name):
                    me.seen(dve_read, PH[name].tiles * PH[name].n)

            add_to_residual("out0", 16)

            def layer_norm(n):
                me.again(dve_read)
                me.next(mean_done)
                me.link(dve.tensor_scalar(mean[:, :], X[0][:, 0:T], 1.0 / D, None, ALU.mult), mean_ready)
                for t in range(0, KT, 2):
                    me.did(dve.tensor_tensor(v3(tl(res, t, 2), 2), v3(tl(res, t, 2), 2), bc(mean[:, :], 2),
                                             ALU.subtract), centered)
                me.next(sd_ready)
                me.again(centered)
                for t in range(0, KT, 2):
                    me.did(dve.tensor_tensor(v3(tl(res, t, 2), 2), v3(tl(res, t, 2), 2), bc(rstd[:, 0:T], 2),
                                             ALU.mult))
                me.again()
                g, b = (fold[:, 0:8], fold[:, 8:16]) if n == 0 else (fold[:, 32:40], fold[:, 40:48])
                prep(lambda t: dve.tensor_scalar(tl(om, t), tl(res, t), g[:, t:t + 1], b[:, t:t + 1], ALU.mult, ALU.add),
                     free=PH["out0" if n == 0 else "down0"].tile0 + 8)

            def root():
                me.next(sd_ready)

            def rms(gain, free):
                me.again(dve_read)
                me.again(ple_added)
                prep(lambda t: dve.tensor_scalar(tl(om, t), tl(res, t), gain(t), None, ALU.mult), free=free)

            def ffn(k):
                if not on(f"gate_up{k}"):
                    return
                n0 = FT * k

                def one(at, t, bank):
                    j = t // 2
                    n = at.lin(n0 + j, 2)
                    wait(dve, silu_done if t % 2 == 0 else prod_done, n - 1)
                    dst = tl(gt if t % 2 == 0 else ut, j)
                    if k == 0:
                        ins = dve.tensor_copy(dst, bank[:, 0:T])
                    else:
                        ins = dve.tensor_tensor(dst, bank[:, 0:T], rstd[:, 0:T], ALU.mult)
                    ins.then_inc(gate_in if t % 2 == 0 else up_in, 1)

                gemm(f"gate_up{k}", one)
                if k == 0:
                    dve.wait_ge(res_ready, KT)
                add_to_residual(f"down{k}", 40 if k == 0 else None)

            def ple(k):
                if not on(f"ple_proj{k}"):
                    return
                rms(lambda t: B("ple_norm_2", KT * (k - 1) + t), PH[f"gate_up{k}"].tile0 + 4 * PH[f"gate_up{k}"].n)
                gemm(f"ple_proj{k}")
                root()

                def add(t):
                    me.next(ple_prod)
                    me.did(dve.tensor_tensor(tl(res, t), tl(res, t), tl(prod, t % 2), ALU.add), ple_added)

                def one(at, t, bank):
                    m = 4 * at.i + t
                    wait(dve, ple_sig, KT * (k - 1) + m - 1)
                    me.did(dve.tensor_tensor(tl(gt, t % 2), bank[:, 0:T], rstd[:, 0:T], ALU.mult), ple_in)
                    if m:
                        add(m - 1)

                gemm(f"ple_gate{k}", one)
                add(KT - 1)

            if on("gate_up0"):
                layer_norm(0)
            ffn(0)

            if on("gla_z"):
                layer_norm(1)
                root()
                me.next(z_done)
                for o in (0, 32):
                    ins = dve.tensor_tensor(g_z[o:o + RANK, :], X[1][o:o + RANK, 0:T], rstd[o:o + RANK, 0:T], ALU.mult)
                me.did(ins, z_ready)

            def scaled(buf, ready, k=None):
                def one(at, t, bank):
                    m = 4 * at.i + t
                    if k is None:
                        ins = dve.tensor_tensor(tl(buf, m), bank[:, 0:T], rstd[:, 0:T], ALU.mult)
                    else:
                        ins = dve.scalar_tensor_tensor(tl(buf, m), bank[:, 0:T], k, rstd[:, 0:T], ALU.mult, ALU.mult)
                    me.did(ins, ready)
                return one

            gemm("gla_q", scaled(g_q, dve_read, GDK ** -0.5))
            if on("gla_k"):
                for b in range(4):
                    me.next(la_done)
                    for half in range(2):
                        t = 2 * (b % 2) + half
                        ins = dve.tensor_scalar(tl(g_la[b // 2], t), X[b][:, half * T:(half + 1) * T],
                                                B("gla_b_gate_f_2" if b < 2 else "gla_b_gate_b_2", t), None, ALU.add)
                    me.did(ins, la_read)
            gemm("gla_k", scaled(g_k, dve_read))
            ends = lambda buf, d: v3(buf[:, :], 16)[:, :, CH - 1:CH] if d == 0 else v3(buf[:, :], 16)[:, :, 0:1]
            if on("gla_v"):
                for d in range(2):
                    me.next(lg_ready)
                    me.link(dve.scalar_tensor_tensor(g_la[d][:, :], g_la[d][:, :], 0.0, g_b[d][:, :], ALU.min,
                                                     ALU.subtract))
                    me.next(seg_ready)
                    way = (lambda ap: ap[:, :]) if d == 0 else (lambda ap: ap[:, ::-1])
                    me.link(dve.tensor_tensor_scan(way(g_b[d]), way(seg[d]), way(g_la[d]), 0.0, ALU.mult, ALU.add),
                            b_ready)
                    me.did(dve.tensor_copy(v3(total[:, 16 * d:16 * d + 16], 16), ends(g_b[d], d)))

            def gla_after(at, t):
                if at.i == 1 and t == 0:
                    for d in range(2):
                        me.next(grow_ready, 2)
                        me.again()
                        tot = total[:, 16 * d:16 * d + 16].rearrange("p (c n) -> p c n", n=1).to_broadcast([P, 16, CH])
                        me.did(dve.tensor_tensor(v3(g_b[d][:, :], 16), tot, v3(g_b[d][:, :], 16), ALU.subtract),
                               dist_ready)

            gemm("gla_v", None, gla_after)
            if on("gla_r"):
                me.again(dve_read)
                for d in range(2):
                    me.link(dve.tensor_copy(v3(decay[:, 16 * d:16 * d + 16], 16), ends(g_la[d], d)))
                    me.did(dve.tensor_tensor(g_la[d][:, :], g_q[:, :], g_la[d][:, :], ALU.mult), kd_ready)
                    me.next(fall_ready)
                    me.did(dve.tensor_tensor(g_b[d][:, :], g_k[:, :], g_b[d][:, :], ALU.mult), kd_ready)
            gemm("gla_r", scaled(g_r, r_ready))
            if on("out1"):
                def read_out(h):
                    me.next(go_done)
                    if h == 0:
                        dve.wait_ge(ke_ready, 2)
                    me.did(dve.tensor_copy(tl(g_o, 2 * h, 2), X[2 + h % 2][:, :]), go_read)

                for h in range(GH):
                    me.next(gs_done)
                    me.link(dve.tensor_tensor(v3(g_m[:, :], 2), v3(G[0][:, :], 2), bc(C("gla_mask", 2 * P), 2),
                                              ALU.mult), gs_read)
                    m4 = g_m[:, :].rearrange("p (t f n) -> p t f n", t=2, f=2)
                    if h >= 2:
                        dve.wait_ge(go_done, h - 1)
                    me.did(dve.tensor_tensor(v3(tl(g_st, h % 2), 2), m4[:, :, 0, :], m4[:, :, 1, :], ALU.add), st_ready)
                    if h:
                        read_out(h - 1)
                    me.next(u_done)
                    S = lambda n: tl(state, n)
                    dec = lambda d, c: decay[:, 16 * d + 4 * h + c:16 * d + 4 * h + c + 1]
                    step = lambda n, m, k, u: dve.scalar_tensor_tensor(S(n), S(m), k, u, ALU.mult, ALU.add)
                    me.link(dve.tensor_copy(S(3), X[1][:, 0:T]), u_read)
                    me.did(step(4, 3, dec(1, 2), X[0][:, 0:T]), u_read)
                    me.link(dve.tensor_copy(S(0), G[2][:, 0:T]))
                    me.link(step(1, 0, dec(0, 1), G[3][:, 0:T]))
                    me.did(step(2, 1, dec(0, 2), G[2][:, T:2 * T]), u_read)
                    me.did(step(5, 4, dec(1, 1), G[3][:, T:2 * T]), u_read)
                read_out(GH - 1)

                def make(t):
                    if t % 4 == 0:
                        me.next(sd_ready)
                    if t % 2 == 0:
                        me.next(gated)
                    return dve.scalar_tensor_tensor(tl(om, t), tl(g_r, t), B("gla_g_out_2", t % 2), tl(g_rs, t // 2),
                                                    ALU.mult, ALU.mult)

                prep(make, free=PH["gla_r"].tile0 + 8)
            if on("out1"):
                dve.wait_ge(res_ready, 2 * KT)
            add_to_residual("out1")
            if on("gate_up1"):
                rms(lambda t: B("norm_ffn_2", t), PH["out1"].tile0 + 8)
                root()
            ffn(1)
            ple(1)

            if on("diff_q"):
                rms(lambda t: B("norm_mix_2", KT + t), PH["ple_gate1"].tile0 + 8)
                root()

            def pair(r):
                return tl(d_q, 2 * r, 2) if r < 4 else tl(d_k, 2 * r - 8, 2)

            def normalize(r):
                me.next(qk_sd)
                rs = tl(d_rs, r % 2, w=512)
                me.did(dve.scalar_tensor_tensor(pair(r), pair(r), B("diff_g_q_2" if r < 4 else "diff_g_k_2"), rs,
                                                ALU.mult, ALU.mult), qk_normed)

            def turn(r):
                me.next(qk_rot)
                me.again(qk_ready)
                me.did(dve.tensor_tensor(v3(d_t2[:, :], 2), v3(X[2 + r % 2][:, :], 2), bc(C("sin_d", T), 2), ALU.mult),
                       qk_rot_read)
                me.next(qk_cos)
                me.again(qk_rot_read)
                me.did(dve.tensor_tensor(pair(r), d_t1[:, :], d_t2[:, :], ALU.add), qk_ready)

            for base, name in ((0, "diff_q"), (4, "diff_k")):
                def after(at, t, base=base):
                    r = base + 2 * at.i
                    if t == 1 and r:
                        turn(r - 2)
                    if t == 3:
                        if r:
                            turn(r - 1)
                        normalize(r)
                        normalize(r + 1)
                gemm(name, scaled(d_q if base == 0 else d_k, qk_src), after)
            gemm("diff_v", None, lambda at, t: turn(6 + t) if at.i == 0 else None)
            if on("out2"):
                for i in range(NH + 2):
                    if i < NH:
                        me.next(score_done)
                        s = 4 * (i % 2)
                        for c in range(2):
                            me.did(dve.tensor_reduce(neg_max[:, s + 2 * c:s + 2 * c + 2],
                                                     v3(G[2 * (i % 2) + c][:, :], 2), AX, ALU.max, negate=True))
                        me.again()
                        me.did(dve.tensor_scalar(neg_max[:, s:s + 4], neg_max[:, s:s + 4], HD ** -0.5, None, ALU.mult),
                               max_ready)
                    if 1 <= i <= NH:
                        me.next(exp_done, 2)
                        s = 4 * ((i - 1) % 2)
                        me.link(dve.reciprocal(rsum[:, s:s + 4], sums[:, s:s + 4]))
                        me.did(dve.tensor_scalar(rsum[:, s + 2:s + 4], rsum[:, s + 2:s + 4], lam[:, 4:5], None, ALU.mult))
                        for qt in range(2):
                            me.did(dve.tensor_scalar(tl(d_p, s + qt), tl(d_p, s + qt), rsum[:, s + qt:s + qt + 1],
                                                     None, ALU.mult))
                        me.again()
                        for qt in range(2):
                            ins = dve.scalar_tensor_tensor(tl(d_p, s + qt), tl(d_p, s + 2 + qt),
                                                           rsum[:, s + 2 + qt:s + 3 + qt], tl(d_p, s + qt),
                                                           ALU.mult, ALU.add)
                        me.did(ins, prob_ready)
                    if i >= 2:
                        me.next(pv_done)
                        me.did(dve.tensor_copy(tl(d_o, i - 2), X[2 + i % 2][:, 0:T]), mixed_ready)
                me.again(mixed_ready)
                prep(group_make(d_o, d_nsq, lambda t: lam[:, 5:6]), free=PH["diff_v"].tile0 + 4)
            add_to_residual("out2")
            if on("gate_up2"):
                rms(lambda t: B("norm_ffn_2", KT + t), PH["out2"].tile0 + 8)
                root()
            ffn(2)
            ple(2)
            if stop is None:
                for n in range(4):
                    me.next(out_done)
                    me.did(dve.tensor_copy(tl(o_tok, n, w=512), G[n][:, :]), out_read)

        @block.tensor
        def _(pe):
            banks = Banks(pe)
            me = Steps(pe, None)

            def three(dst, st_hi, st_lo, mv_hi, mv_lo, start, stop_):
                pe.matmul(dst, st_hi, mv_hi, start=start, stop=False)
                pe.matmul(dst, st_hi, mv_lo, start=False, stop=False)
                return pe.matmul(dst, st_lo, mv_hi, start=False, stop=stop_)

            def slab_view(ph, buf, shape):
                if shape == "gate_up":
                    return buf[:, :].rearrange("p (k g n) -> p k g n", k=KT, g=2)
                k = {"down": FT, "ple": 2}.get(shape, KT)
                return buf[:, 0:ph.cols].rearrange("p (k n) -> p k n", k=k)

            def gemm(name, freed, shape="plain", olo_from=None, order=range(KT), after=None, before=None):
                if not on(name):
                    return
                ph = PH[name]
                base = banks.n.get(freed.name, 0) if freed is not None else 0

                def body(at):
                    if before:
                        before(at)
                    hslot = (ph.j0 + at.parity) % 2
                    hi, lo = (slab_view(ph, b[hslot], shape) for b in (whi, wlo))
                    pe.wait_ge(lo_ready, at.lin(4 * (ph.j0 + 1), 4))
                    first = isinstance(at.i, int) and at.i == 0
                    for t in range(ph.tiles):
                        bank, n = bank_of(ph, at, t)
                        if shape == "gate_up":
                            by = gate_in if t % 2 == 0 else up_in
                            if first:
                                banks.claim(bank, by)
                            else:
                                wait(pe, by, at.lin(FT * int(name[-1]) + t // 2 - 1, 2))
                        elif shape == "down":
                            if first:
                                banks.claim(bank, freed)
                            else:
                                if at.i is not None and at.it is None and at.i == 1 or at.it is not None and at.b == 0:
                                    banks.settle(G[1]) if at.it is not None else None
                                wait(pe, freed, at.lin(base - 1, 1))
                        else:
                            banks.claim(bank, freed)
                        if shape == "gate_up":
                            w = lambda v, k: v[:, k, t % 2, (t // 2) * P:(t // 2 + 1) * P]
                        elif ph.tiles == 1:
                            w = lambda v, k: v[:, k, :]
                        else:
                            w = lambda v, k: v[:, k, t * P:(t + 1) * P]
                        ks = {"down": range(FT), "ple": range(2)}.get(shape, order)
                        layer = int(name[-1]) - 1 if shape == "ple" else 0
                        for n_, k in enumerate(ks):
                            if first and t == 0 and olo_from is not None:
                                pe.wait_ge(olo_ready, olo_from + n_ + 1)
                            if first and shape == "down":
                                pe.wait_ge(actlo_ready, FT * int(name[-1]) + k + 1)
                            if shape == "token":
                                st = (tl(ohi, k)[:, t * P:(t + 1) * P], tl(olo, k)[:, t * P:(t + 1) * P])
                                ins = three(bank[:, 0:n], *st, hi[:, k, :], lo[:, k, :], n_ == 0, n_ == len(ks) - 1)
                            else:
                                src = {"down": (acthi, actlo), "ple": (p_hi, p_lo)}.get(shape, (ohi, olo))
                                mv = [tl(b, k + 2 * layer) for b in src]
                                ins = three(bank[:, 0:T], w(hi, k), w(lo, k), *mv, n_ == 0, n_ == len(ks) - 1)
                        ins.then_inc(tile_done, 1)
                        if after:
                            after(at, t)

                if shape == "down":
                    settle_then_rounds(ph, body)
                else:
                    rounds(pe, ph, body)
                if shape == "gate_up":
                    end = FT * (int(name[-1]) + 1)
                    for t in range(4):
                        banks.skip(G[t], gate_in if t % 2 == 0 else up_in, end)
                if shape == "down":
                    banks.skip(G[0], freed, base + ph.n)
                    banks.skip(G[1], freed, base + ph.n)

            def settle_then_rounds(ph, body):
                def one(at):
                    body(at)
                    if at.it is None and at.i == 0:
                        banks.settle(G[1])
                rounds(pe, ph, one)

            def stats(tok=False):
                banks.claim(X[0], sd_ready)
                me.next(squares_summed)
                me.seen(sq_ready, KT)
                ins = pe.matmul(X[0][:, 0:T], ones[:, :], sq_sum[:, :], start=True, stop=True)
                for tt in range(TT if tok else 0):
                    ins = pe.matmul(X[0][:, T + tt:T + tt + 1], sq_sum[:, tt * P:(tt + 1) * P], ones[:, 0:1],
                                    start=True, stop=True, skip_group_check=True)
                ins.then_inc(stat_done, 1)

            def group_stats(groups, mat, buf, ready_banks):
                for n, g in enumerate(groups):
                    bank = ready_banks[n % len(ready_banks)]
                    banks.claim(bank, sd_ready)
                    me.next(sq_ready)
                    pe.matmul(bank[:, :], mat, tl(buf, 2 * g, 2), start=True, stop=True).then_inc(stat_done, 1)

            def modulation(i):
                ph = PH[f"ada{i}"]
                pe.wait_ge(pool_summed if i in POOL_SLABS else dve_summed, ph.used0 + 1)
                for m in range(4):
                    o = 512 * mod_half(i) + P * m
                    ins = pe.matmul(X[3][:, 4 * i + m:4 * i + m + 1], macc[:, o:o + P], ones[:, 0:1],
                                    start=True, stop=True, skip_group_check=True)
                ins.then_inc(mod_done, 1)

            pe.wait_ge(c_in, 32)
            banks.claim(X[3], c_ready)
            pe.transpose(X[3][:, 48:56], rows_c[0:KT, :], ident[0:KT, 0:KT]).then_inc(c_ready_t, 1)
            pe.wait_ge(x_in, 16)
            for n, bank in enumerate((X[0], X[1], X[2], G[1])):
                banks.claim(bank, dve_read)
                for k in range(2):
                    for tt in range(TT):
                        ins = pe.transpose(bank[:, k * T + tt * P:k * T + (tt + 1) * P],
                                           tl(xin, tt, w=D)[:, (2 * n + k) * P:(2 * n + k + 1) * P], ident)
                ins.then_inc(setup_t, 1)
            pe.wait_ge(set_zero, 3)
            banks.claim(X[3], mod_read)
            for i in range(2):
                modulation(i)
            pe.wait_ge(params_in, 16 * (len(ROWS_A) + len(ROWS_B) + 4))
            banks.claim(G[0], dve_read)
            pe.transpose(G[0][:, 0:NA], rows_a[0:NA, :], ident[0:NA, 0:NA])
            pe.transpose(G[0][:, P:P + NB], rows_b[0:NB, :], ident[0:NB, 0:NB]).then_inc(setup_t, 1)
            for i in range(2, 4):
                modulation(i)
            pe.wait_ge(const_in, 16)
            pe.wait_ge(p_in, 16)
            for layer in range(2):
                bank = G[2 + layer]
                banks.claim(bank, dve_read)
                for k in range(2):
                    for tt in range(TT):
                        o = layer * 512 + tt * 256 + k * P
                        ins = pe.transpose(bank[:, k * T + tt * P:k * T + (tt + 1) * P], pin[:, o:o + P], ident)
                ins.then_inc(setup_t, 1)

            banks.claim(X[3], mod_read)
            gemm("in_q", rope_src, olo_from=0)
            gemm("in_idx", rope_src)

            def rotate(r):
                bank = X[(0, 1, 2, 0)[r]]
                banks.claim(bank, rot_read)
                pe.wait_ge(rope_src, (2, 4, 8, 8)[r])
                if r == 2:
                    pe.matmul(bank[:, 0:T], C("rot_q"), tl(rope_in, 4), start=True, stop=True)
                    ins = pe.matmul(bank[:, T:2 * T], C("rot_i"), tl(rope_in, 7), start=True, stop=True)
                else:
                    ins = pe.matmul(bank[:, :], C("rot_i" if r == 3 else "rot_q"), tl(rope_in, (0, 2, None, 5)[r], 2),
                                    start=True, stop=True)
                ins.then_inc(rot_done, 1)

            if on("in_v"):
                rotate(0)
                rotate(1)
            gemm("in_v", v_src, shape="token")
            if on("in_gc"):
                rotate(2)
                rotate(3)
            gemm("in_gc", gc_ready)
            if on("ada5"):
                modulation(4)
            if on("in_hc"):
                pe.wait_ge(roped, 4)
                for h in range(IH):
                    banks.claim(G[h % 4], relu_done)
                    rows = slice(ID * (h % 4), ID * (h % 4) + ID)
                    q, kk = tl(rope_out, 5 + h // 4), tl(rope_out, 7)
                    pe.matmul(G[h % 4][:, 0:P], q[rows, 0:P], kk[rows, 0:P], start=True, stop=True)
                    pe.matmul(G[h % 4][:, P:3 * P], q[rows, P:2 * P], kk[rows, :], start=True,
                              stop=True).then_inc(idx_done, 1)
            gemm("in_hc", dve_read)
            if on("ada6"):
                modulation(5)
            gemm("in_gb", mixed_ready)
            if on("ada11"):
                group_stats((2, 3), C("blk"), mix_sq, X[0:2])
                def scores(i):
                    banks.claim(G[i % 2], score_read)
                    rows = slice(HD * (i % 2), HD * (i % 2) + HD)
                    q, kk = tl(rope_out, i // 2), tl(rope_out, 4)
                    pe.matmul(G[i % 2][:, 0:P], q[rows, 0:P], kk[rows, 0:P], start=True, stop=True)
                    pe.matmul(G[i % 2][:, P:3 * P], q[rows, P:2 * P], kk[rows, :], start=True,
                              stop=True).then_inc(score_done, 1)

                scores(0)
                for i in range(NH + 2):
                    if i + 1 < NH:
                        scores(i + 1)
                    for n in MOD_TAKEN.get(i, ()):
                        modulation(n)
                    if 1 <= i <= NH:
                        bank, lg = G[2 + (i - 1) % 2], tl(logit, (i - 1) % 2, w=384)
                        banks.claim(bank, pt_ready)
                        me.next(prob_ready)
                        for n in range(3):
                            ins = pe.transpose(bank[:, n * P:(n + 1) * P], lg[:, n * P:(n + 1) * P], ident)
                        ins.then_inc(trans_done, 1)
                    if i >= 2:
                        h = i - 2
                        bank, pt = X[h // 2 % 2], tl(prob_t, h % 2, w=384)
                        if h % 2 == 0:
                            banks.claim(bank, mixed_ready)
                        me.next(pt_ready)
                        rows = slice(HD * (h % 2), HD * (h % 2) + HD)
                        pe.matmul(bank[rows, 0:T], vtok[:, 0:HD], pt[:, 0:T], start=True, stop=False,
                                  skip_group_check=True)
                        pe.matmul(bank[rows, P:T], vtok[:, 72:72 + HD], pt[:, T:T + P], start=False, stop=True,
                                  skip_group_check=True).then_inc(pv_done, 1)
            def next_operand():
                OPERANDS[0] += KT
                return OPERANDS[0]

            def mean_sums(tiles):
                for t in tiles:
                    if t == 0:
                        banks.claim(X[0], mean_ready)
                    pe.wait_ge(dve_read, STREAM[0] + t + 1)
                    ins = pe.matmul(X[0][:, 0:T], ones[:, :], tl(res, t), start=(t == 0), stop=(t == KT - 1))
                    if t == KT - 1:
                        ins.then_inc(mean_done, 1)

            def layer_norm():
                mean_sums(range(KT - 1, KT))
                banks.claim(X[1], sd_ready)
                for t in range(KT):
                    if t % 2 == 0:
                        me.next(sq_ready)
                    ins = pe.matmul(X[1][:, 0:T], ones[:, :], tl(sq, t), start=(t == 0), stop=(t == KT - 1))
                ins.then_inc(stat_done, 1)

            if on("out0"):
                group_stats((0, 1), C("blk"), mix_sq, X[0:2])
            OPERANDS = [8]
            STREAM = [banks.n[dve_read.name]]
            gemm("out0", dve_read, olo_from=8, order=(4, 5, 6, 7, 0, 1, 2, 3),
                 after=lambda at, t: mean_sums([4 * at.i + t - 1]) if 4 * at.i + t else None)

            def ffn(k, stat):
                if not on(f"gate_up{k}"):
                    return

                def after(at, t):
                    if stat and t == 0 and at.it is None and at.i == 0:
                        stats()

                gemm(f"gate_up{k}", gate_in, shape="gate_up", olo_from=next_operand(), after=after)
                STREAM[0] = banks.n[dve_read.name]

                def before(at):
                    if k == 0 and at.it is None and at.i == KT - 1:
                        mean_sums(range(KT - 2))

                gemm(f"down{k}", dve_read, shape="down", before=before,
                     after=lambda at, t: mean_sums([KT - 2]) if k == 0 and at.it is None and at.i == KT - 1 else None)

            def ple(k):
                if not on(f"ple_proj{k}"):
                    return
                start = next_operand()
                gemm(f"ple_proj{k}", pp_ready, shape="ple")
                stats()
                gemm(f"ple_gate{k}", ple_in, olo_from=start)

            if on("gate_up0"):
                layer_norm()
            ffn(0, False)

            if on("gla_z"):
                layer_norm()
                start = next_operand()
                stats(tok=True)
                ph = PH["gla_z"]
                slot = ph.slot
                pe.wait_ge(landed[slot], ph.landed[0])
                banks.claim(X[1], z_ready)
                for k in range(KT):
                    pe.wait_ge(olo_ready, start + k + 1)
                    ins = pe.matmul(X[1][0:48, 0:T], raw[slot][:, 48 * k:48 * (k + 1)], tl(om, k),
                                    start=(k == 0), stop=(k == KT - 1))
                ins.then_inc(z_done, 1)
            gemm("gla_q", dve_read)
            if on("gla_k"):
                pe.wait_ge(z_ready, 1)
                pe.wait_ge(gates_in, 32)
                for b in range(4):
                    banks.claim(X[b], la_read)
                    for half in range(2):
                        t = 2 * (b % 2) + half
                        ins = pe.matmul(X[b][:, half * T:(half + 1) * T],
                                        wgate[32 * (b // 2):32 * (b // 2) + RANK, P * t:P * (t + 1)],
                                        g_z[32 * (b // 2):32 * (b // 2) + RANK, :], start=True, stop=True)
                    ins.then_inc(la_done, 1)
            gemm("gla_k", dve_read)
            gemm("gla_v", v_ready, shape="token")
            gemm("gla_r", r_ready)
            if on("out1"):
                pe.wait_ge(kd_ready, 4)
                pe.wait_ge(ke_ready, 2)
                pe.wait_ge(v_ready, 4)

                def outputs(h):
                    bank = X[2 + h % 2]
                    banks.claim(bank, go_read)
                    pe.wait_ge(st_ready, h + 1)
                    first = True
                    for e in range(2):
                        for tt in range(TT):
                            v = g_v[:, tt * D + h * GDV + e * P:tt * D + h * GDV + e * P + P]
                            pe.matmul(bank[:, e * T + tt * P:e * T + (tt + 1) * P], v,
                                      tl(g_st, h % 2)[:, tt * P:(tt + 1) * P], start=first, stop=False,
                                      skip_group_check=True)
                            first = False
                    pe.wait_ge(u_read, 4 * (h + 1))
                    for e in range(2):
                        for d in range(2):
                            for n in range(3):
                                c = n + 1 if d == 0 else 2 - n
                                ins = pe.matmul(bank[:, e * T + c * CH:e * T + (c + 1) * CH],
                                                tl(state, 3 * d + n)[:, e * P:(e + 1) * P],
                                                tl(g_la[d], h)[:, c * CH:(c + 1) * CH], start=False,
                                                stop=(e == 1 and d == 1 and n == 2), skip_group_check=True)
                    ins.then_inc(go_done, 1)

                for h in range(GH + 1):
                    if h < GH:
                        banks.claim(G[0], gs_read)
                        for tt in range(TT):
                            for d in range(2):
                                o = (2 * tt + d) * P
                                ins = pe.matmul(G[0][:, o:o + P], tl(g_ke[d], h)[:, tt * P:(tt + 1) * P],
                                                tl(g_la[d], h)[:, tt * P:(tt + 1) * P], start=True, stop=True)
                        ins.then_inc(gs_done, 1)
                        banks.claim(G[1], kt_ready)
                        for d in range(2):
                            for tt in range(TT):
                                ins = pe.transpose(G[1][:, (2 * d + tt) * P:(2 * d + tt + 1) * P],
                                                   tl(g_b[d], h)[:, tt * P:(tt + 1) * P], ident)
                        ins.then_inc(kt_done, 1)
                    if h:
                        outputs(h - 1)
                    if h < GH:
                        pe.wait_ge(kt_ready, h + 1)
                        for bank in (X[1], X[0], G[2], G[3]):
                            banks.claim(bank, u_read)
                        for bank, half, d, c in ((X[1], 0, 1, 3), (X[0], 0, 1, 2), (G[2], 0, 0, 0), (G[3], 0, 0, 1),
                                                 (G[2], 1, 0, 2), (G[3], 1, 1, 1)):
                            rows = slice(CH * (c % 2), CH * (c % 2) + CH)
                            tt = c // 2
                            ins = pe.matmul(bank[:, half * T:(half + 1) * T],
                                            kd_tok[rows, (2 * d + tt) * P:(2 * d + tt + 1) * P],
                                            g_v[rows, tt * D + h * GDV:tt * D + (h + 1) * GDV], start=True, stop=True)
                        ins.then_inc(u_done, 1)
                for h in range(GH):
                    if h % 2 == 0:
                        banks.claim(G[h // 2], sd_ready)
                    me.next(sq_ready)
                    for e in range(2):
                        ins = pe.matmul(G[h // 2][:, (h % 2) * T:(h % 2 + 1) * T], ones[:, :], tl(g_sq, 2 * h + e),
                                        start=(e == 0), stop=(e == 1))
                    if h % 2:
                        ins.then_inc(stat_done, 1)
                start = next_operand()
                gemm("out1", dve_read, olo_from=start)
            ffn(1, True)
            ple(1)

            def block_sums(r):
                banks.claim(X[r % 2], qk_sd)
                me.next(qk_sq)
                pe.matmul(X[r % 2][:, :], C("blk"), tl(d_sq, r % 2, w=512), start=True, stop=True).then_inc(qk_stat, 1)

            def partners(r):
                banks.claim(X[2 + r % 2], qk_rot_read)
                pe.wait_ge(qk_normed, r + 1)
                src = tl(d_q, 2 * r, 2) if r < 4 else tl(d_k, 2 * r - 8, 2)
                pe.matmul(X[2 + r % 2][:, :], C("rot_d"), src, start=True, stop=True).then_inc(qk_rot, 1)

            start = next_operand() if on("diff_q") else 0
            for base, name in ((0, "diff_q"), (4, "diff_k")):
                def after(at, t, base=base):
                    r = base + 2 * at.i
                    if r == 0 and t == 0:
                        stats(tok=True)
                    if t == 1 and r:
                        partners(r - 2)
                    if t == 3:
                        if r:
                            partners(r - 1)
                        block_sums(r)
                        block_sums(r + 1)
                gemm(name, qk_src, olo_from=start if base == 0 else None, after=after)
            gemm("diff_v", v_ready, shape="token", after=lambda at, t: partners(6 + t) if at.i == 0 else None)
            if on("out2"):
                pe.wait_ge(qk_ready, 8)
                pe.wait_ge(v_ready, 8)
                def scores(i):
                    for c in range(2):
                        banks.claim(G[2 * (i % 2) + c], exp_done)
                    for qt in range(2):
                        for c in range(2):
                            rows = slice(HD * c, HD * c + HD)
                            ins = pe.matmul(G[2 * (i % 2) + c][:, qt * T:(qt + 1) * T],
                                            tl(d_q, i)[rows, qt * P:(qt + 1) * P], tl(d_k, i)[rows, :],
                                            start=True, stop=True)
                    ins.then_inc(score_done, 1)

                banks.n[exp_done.name] = NH
                scores(0)
                for i in range(NH + 2):
                    if i + 1 < NH:
                        scores(i + 1)
                    if 1 <= i <= NH:
                        s = (i - 1) % 2
                        banks.claim(X[s], pt_ready)
                        me.next(prob_ready)
                        for kt in range(2):
                            for qt in range(2):
                                ins = pe.transpose(X[s][:, kt * T + qt * P:kt * T + (qt + 1) * P],
                                                   tl(d_p, 4 * s + qt)[:, kt * P:(kt + 1) * P], ident)
                        ins.then_inc(trans_done, 1)
                    if i >= 2:
                        h = i - 2
                        banks.claim(X[2 + h % 2], mixed_ready)
                        me.next(pt_ready)
                        for kt in range(2):
                            ins = pe.matmul(X[2 + h % 2][:, 0:T], d_v[:, kt * D + h * P:kt * D + (h + 1) * P],
                                            tl(d_pt, h % 2, w=512)[:, kt * T:(kt + 1) * T], start=(kt == 0), stop=(kt == 1))
                        ins.then_inc(pv_done, 1)
                group_stats((0, 1, 2, 3), ones[:, :], d_nsq, G)
                start = next_operand()
                gemm("out2", dve_read, olo_from=start)
            ffn(2, True)
            ple(2)
            if stop is None:
                pe.wait_ge(ple_added, 2 * KT)
                for n in range(4):
                    tt, half = n // 2, n % 2
                    banks.claim(G[n], out_read)
                    for k in range(4):
                        ins = pe.transpose(G[n][:, k * P:(k + 1) * P], tl(res, 4 * half + k)[:, tt * P:(tt + 1) * P], ident)
                    ins.then_inc(out_done, 1)


_INS = ["x", "c", "w_ada", "b_ada", "w_in", "conv_w", "attn_norm_g", "conv_norm_g", "w_out", "ln1_g", "ln1_b", "w_gate",
        "w_up", "w_down", "ln2_g", "ln2_b", "p_2", "norm_mix_2", "norm_ffn_2", "ffn_w_in_2", "ffn_w_out_2", "ple_norm_2",
        "ple_w_gate_2", "ple_w_proj_2", "gla_w_in_2", "gla_w_gate_f_2", "gla_b_gate_f_2", "gla_w_gate_b_2",
        "gla_b_gate_b_2", "gla_g_out_2", "gla_w_out_2", "diff_w_in_2", "diff_g_q_2", "diff_g_k_2", "diff_lam_q1_2",
        "diff_lam_k1_2", "diff_lam_q2_2", "diff_lam_k2_2", "diff_g_sub_2", "diff_w_out_2"]


def kernel(**inputs):
    import concourse.bacc as bacc
    from concourse.bass_utils import run_bass_kernel_spmd

    arrays = {f"in_{n}": np.ascontiguousarray(inputs[n]) for n in _INS}
    arrays["in_shape_constants"] = shape_constants()
    nc = bacc.Bacc("TRN2", target_bir_lowering=False, num_devices=1)
    a = {n[3:]: nc.dram_tensor(n, v.shape, F32, kind="ExternalInput").ap() for n, v in arrays.items()}
    out = nc.dram_tensor("out_0", (1, T, D), F32, kind="ExternalOutput").ap()
    build(nc, a, out)
    r = run_bass_kernel_spmd(nc, [arrays], core_ids=[0])
    return r.results[0]["out_0"]
```

```python
from contextlib import ExitStack

import numpy as np

import concourse.bass as bass
from concourse import mybir

F32 = mybir.dt.float32
F32R = mybir.dt.float32r
ALU = mybir.AluOpType
ACT = mybir.ActivationFunctionType
AX = mybir.AxisListType.X

P = 128
T = 256
D = 1024
KT = D // P
TT = T // P
F = 2816
FT = F // P
HD = 64
NH = 8
IH, ID = 8, 32
TOPK = 64
ALPHA = 2.0 ** 0.25
EPS1, EPS2 = 1e-5, 1e-6
GH, GDK, GDV = 4, 128, 256
CH, NCH = 64, 4
RANK, TAU = 16, 16.0
NEG = -1e30
TAKEN = -3e38
LAMBDA_INIT = 0.8 - 0.6 * float(np.exp(-0.3))
SLAB = 4096

QW = 512
C_K, C_V, C_QI, C_KI, C_WI, C_GB = 512, 576, 640, 896, 928, 936
C_GC, C_HC = C_GB + 512, C_GB + 1024

ROWS_A = [("b_ada", 48), ("ln1_g", 8), ("ln1_b", 8), ("ln2_g", 8), ("ln2_b", 8),
          ("attn_norm_g", 4), ("conv_norm_g", 4), ("conv_w", 12)]
ROWS_B = [("norm_mix_2", 16), ("norm_ffn_2", 16), ("ple_norm_2", 16), ("gla_b_gate_f_2", 4),
          ("gla_b_gate_b_2", 4), ("gla_g_out_2", 2), ("diff_g_sub_2", 1), ("diff_g_q_2", 1),
          ("diff_g_k_2", 1)]


def column_of(rows):
    at, n = {}, 0
    for name, k in rows:
        at[name] = n
        n += k
    return at, n


COL_A, NA = column_of(ROWS_A)
COL_B, NB = column_of(ROWS_B)

CONSTS = [("ident", P), ("blk", P), ("rot_q", P), ("rot_i", P), ("rot_d", P), ("cos_q", T), ("sin_q", T),
          ("cos_i", T), ("sin_i", T), ("cos_d", T), ("sin_d", T), ("causal", 3 * P), ("gla_mask", 2 * P)]
COL_C, NC = column_of(CONSTS)


def shape_constants():
    out = np.zeros((P, NC), np.float32)

    def put(name, a):
        out[:, COL_C[name]:COL_C[name] + a.shape[1]] = a

    p = np.arange(P)
    put("ident", np.eye(P))
    put("blk", (p[:, None] // HD == p[None, :] // HD) * 1.0)
    pos = np.arange(T, dtype=np.float32)
    for tag, width, half, theta in (("q", HD, 8, 500000.0), ("i", ID, 8, 500000.0), ("d", HD, 32, 10000.0)):
        rot = np.zeros((P, P))
        cos, sin = np.ones((P, T)), np.zeros((P, T))
        inv = (theta ** (-(np.arange(half) * 2.0) / (2 * half))).astype(np.float32)
        ang = (pos[None, :] * inv[:, None]).astype(np.float32).astype(np.float64)
        for m in range(P):
            d = m % width
            if d < 2 * half:
                rot[m + half if d < half else m - half, m] = -1.0 if d < half else 1.0
                cos[m], sin[m] = np.cos(ang[d % half]), np.sin(ang[d % half])
        put("rot_" + tag, rot)
        put("cos_" + tag, cos)
        put("sin_" + tag, sin)
    tri = np.where(p[None, :] <= p[:, None], 0.0, NEG)
    put("causal", np.concatenate([tri, np.zeros((P, P)), tri], 1))
    same = p[:, None] // CH == p[None, :] // CH
    put("gla_mask", np.concatenate([same & (p[:, None] <= p[None, :]), same & (p[:, None] > p[None, :])], 1) * 1.0)
    return out


POOL_SLABS = (4, 5, 6, 7, 11)


class Phase:

    def __init__(self, name, n, cols, tiles, dmas, by="split", loop=False, ahead=True, ring=True,
                 slot=None):
        self.name, self.n, self.cols, self.tiles, self.dmas = name, n, cols, tiles, dmas
        self.by, self.split, self.loop, self.ahead, self.ring = by, by == "split", loop, ahead, ring
        self.slot = slot


def plan():
    ffn = lambda k: [Phase(f"gate_up{k}", FT // 2, SLAB, 4, 2, loop=True), Phase(f"down{k}", KT, F, 1, 2, loop=True)]
    ple = lambda k: [Phase(f"ple_proj{k}", 1, 2048, 8, 1), Phase(f"ple_gate{k}", 2, SLAB, 4, 1)]
    ada = lambda i: Phase(f"ada{i}", 1, SLAB, 0, 1, by="pool" if i in POOL_SLABS else "dve",
                          ahead=False, ring=i not in (2, 3), slot=0 if i in (0, 8, 9, 11) else 1)
    phases = [
        ada(0), ada(1), ada(2), ada(3),
        Phase("in_q", 1, SLAB, 4, 1, slot=0), Phase("in_idx", 1, SLAB, 4, 7, slot=1),
        Phase("in_v", 1, 8 * 72, 2, 2, slot=0), ada(4), Phase("in_gc", 1, SLAB, 4, 1, slot=0), ada(5),
        Phase("in_hc", 1, SLAB, 4, 1, slot=0), ada(6), Phase("in_gb", 1, SLAB, 4, 1, ahead=False, slot=0), ada(7),
        ada(8), ada(9), ada(10), ada(11),
        Phase("out0", 2, SLAB, 4, 1, slot=1), *ffn(0),
        Phase("gla_z", 1, 8 * 3 * RANK, 0, 2, by="pe"), Phase("gla_q", 1, SLAB, 4, 1),
        Phase("gla_k", 1, SLAB, 4, 1), Phase("gla_v", 2, SLAB, 2, 1), Phase("gla_r", 2, SLAB, 4, 1),
        Phase("out1", 2, SLAB, 4, 1), *ffn(1), *ple(1),
        Phase("diff_q", 2, SLAB, 4, 1), Phase("diff_k", 2, SLAB, 4, 1), Phase("diff_v", 2, SLAB, 2, 1),
        Phase("out2", 2, SLAB, 4, 1), *ffn(2), *ple(2),
    ]
    slabs = []
    used = {"split": 0, "dve": 0, "pool": 0, "pe": 0}
    tile = 0
    slot_dmas, last = [0, 0], [None, None]
    for ph in phases:
        ph.s0, ph.j0, ph.tile0, ph.used0 = len(slabs), used["split"] // 4, tile, used[ph.by]
        if ph.slot is None:
            ph.slot = 1 - slot
        ph.landed, ph.free = [], []
        for _ in range(ph.n):
            used[ph.by] += 4 if ph.split else 1
            tile += ph.tiles
            if ph.ring:
                slot = (ph.slot + _) % 2
                slot_dmas[slot] += ph.dmas if ph.by != "pool" else 0
                ph.landed.append(16 * slot_dmas[slot])
                ph.free.append(last[slot])
                last[slot] = (ph.by, used[ph.by])
                slabs.append(last[slot])
    for n, ph in enumerate(phases):
        ph.next = next((q for q in phases[n + 1:] if q.split), None) if ph.ahead else None
    return phases


PHASES = plan()
PH = {ph.name: ph for ph in PHASES}


class At:

    def __init__(self, i, it=None, b=None):
        self.i, self.it, self.b = i, it, b
        self.parity = i % 2 if it is None else (1 + b) % 2

    def of(self, values):
        if self.it is None:
            return values[self.i]
        step = values[3 + self.b] - values[1 + self.b]
        return self.it * step + values[1 + self.b]

    def lin(self, base, per):
        return base + self.i * per if self.it is None else self.it * (2 * per) + (base + (1 + self.b) * per)


def rounds(eng, ph, body):
    pairs = (ph.n - 2) // 2 if ph.loop else 0
    if not pairs:
        for i in range(ph.n):
            body(At(i))
        return
    body(At(0))
    with eng.Fori(0, pairs) as it:
        for b in range(2):
            body(At(it * 2 + (1 + b), it, b))
    for i in range(1 + 2 * pairs, ph.n):
        body(At(i))


def wait(eng, sem, value):
    if not isinstance(value, int) or value > 0:
        eng.wait_ge(sem, value)


class Steps:

    def __init__(self, eng, own):
        self.eng, self.own, self.n = eng, own, {}

    def seen(self, sem, k=1):
        self.n[sem.name] = self.n.get(sem.name, 0) + k

    def next(self, sem, k=1):
        self.seen(sem, k)
        self.eng.wait_ge(sem, self.n[sem.name])

    def again(self, sem=None, less=0):
        sem = sem or self.own
        wait(self.eng, sem, self.n.get(sem.name, 0) - less)

    def did(self, ins, sem=None):
        sem = sem or self.own
        self.seen(sem)
        ins.then_inc(sem, 1)

    def link(self, ins, sem=None):
        self.did(ins, sem)
        self.again(sem)


class Banks:

    def __init__(self, pe):
        self.pe, self.n, self.last = pe, {}, {}

    def settle(self, b):
        if b.name in self.last:
            self.pe.wait_ge(*self.last[b.name])

    def claim(self, b, sem):
        self.settle(b)
        self.n[sem.name] = self.n.get(sem.name, 0) + 1
        self.last[b.name] = (sem, self.n[sem.name])
        return self.n[sem.name]

    def skip(self, b, sem, total):
        self.n[sem.name] = max(self.n.get(sem.name, 0), total)
        self.last[b.name] = (sem, total)


def build(nc, a, out):
    ctx = ExitStack()
    with ctx:
        BASE = 16640
        ARENA = 53168
        ctx.enter_context(nc.sbuf_tensor("arena", [P, (BASE - nc.sbuf_base + 3) // 4 + ARENA], F32))
        taken = [0]
        place = {}

        def sb(name, words, dt=F32, at=None):
            o = taken[0] if at is None else at
            if at is None:
                taken[0] += (words + 7) // 8 * 8
            assert o + words <= ARENA, (name, o + words)
            place[name] = o
            return nc.alloc_sbuf_tensor_at(name, [P, words], dt, offset=BASE + 4 * o)

        raw = [sb(f"raw{i}", SLAB) for i in range(2)]
        whi = [sb(f"whi{i}", SLAB, F32R) for i in range(2)]
        wlo = [sb(f"wlo{i}", SLAB, F32R) for i in range(2)]
        const = sb("const", NC)
        ones = sb("ones", P)
        cols_a, cols_b = sb("cols_a", NA), sb("cols_b", NB)
        mod = sb("mod", 48)
        fold = sb("fold", 48)
        c_act = sb("c_act", 8)
        lam_in = sb("lam_in", 4 * HD)
        lam = sb("lam", 8)
        eps = sb("eps", 2)
        top8 = sb("top8", 16)
        neg_max = sb("neg_max", 2 * 4)
        sums = sb("sums", 2 * 4)
        rsum = sb("rsum", 2 * 4)
        decay = sb("decay", 32)
        total = sb("total", 32)
        wgate = sb("wgate", 512)
        res = sb("res", KT * T)
        om = sb("om", KT * T)
        ohi, olo = sb("ohi", KT * T, F32R), sb("olo", KT * T, F32R)
        p_hi, p_lo = sb("p_hi", 2 * 2 * T, F32R), sb("p_lo", 2 * 2 * T, F32R)
        mean = sb("mean", T)
        sq_sum = sb("sq_sum", T)
        rstd = sb("rstd", T + 2)
        work = sb("work", 2048)
        acthi, actlo = sb("acthi", FT * T, F32R), sb("actlo", FT * T, F32R)
        U = place["acthi"]

        xin, pin = sb("xin", 2048, at=place["work"]), sb("pin", 1024, at=U + 9600)
        rows_a, rows_b, rows_c = (sb(f"rows_{n}", P, at=U + 1024 + P * i) for i, n in enumerate("abc"))
        early = [sb(f"early{i}", SLAB, at=U + 1408 + SLAB * i) for i in range(2)]
        sq, pp = sb("sq", 2048, at=U), sb("pp", 2048, at=U + 4096)
        rope_in, rope_out = sb("rope_in", 2048, at=U), sb("rope_out", 2048, at=U + 2048)
        vtok = sb("vtok", 2 * 72, at=U + 4096)
        gc = sb("gc", 4 * T, at=U + 4352)
        upad = sb("upad", 4 * (T + 2), at=U + 5376)
        conv = sb("conv", 4 * T, at=U + 6408)
        mixed = sb("mixed", KT * T, at=U + 7432)
        relu = sb("relu", 2 * 384, at=U + 9480)
        score, kept = sb("score", 384, at=U + 10248), sb("kept", 384, at=U + 10632)
        mix_sq = sb("mix_sq", KT * T, at=U)
        W = place["work"]
        allow = sb("allow", 384, at=W)
        logit = sb("logit", 2 * 384, at=W + 384)
        prob_t = sb("prob_t", 2 * 384, at=W + 1152)
        dsq = sb("dsq", 2 * T, at=W)
        gsq = sb("gsq", 2 * T, at=W + 1024)
        om_next = sb("om_next", 2 * T, at=W + 512)
        xhi, dhi = sb("xhi", KT * T, F32R, at=U + 2048), sb("dhi", KT * T, F32R, at=U + 6144)
        xlo = sb("xlo", KT * T, F32R, at=place["om"])
        gt, sg = sb("gt", 2 * T, at=W), sb("sg", 2 * T, at=W + 512)
        ut, prod = sb("ut", 2 * T, at=W + 1024), sb("prod", 2 * T, at=W + 1536)
        g_q, g_k = sb("g_q", 1024, at=U), sb("g_k", 1024, at=U + 1024)
        g_o = sb("g_o", 2048, at=U)
        g_v, g_r = sb("g_v", 2048, at=U + 2048), sb("g_r", 2048, at=U + 4096)
        g_la = [sb(f"g_la{d}", 1024, at=U + 6144 + 1024 * d) for d in range(2)]
        g_b = [sb(f"g_b{d}", 1024, at=U + 8192 + 1024 * d) for d in range(2)]
        g_ke = [sb(f"g_ke{d}", 1024, at=W + 1024 * d) for d in range(2)]
        g_m, g_st = sb("g_m", 512, at=U + 10240), sb("g_st", 512, at=U + 10752)
        g_sq = sb("g_sq", 2048, at=place["olo"])
        g_rs = sb("g_rs", 1024, at=U + 8192)
        O = place["om"]
        seg = [sb(f"seg{d}", 1024, at=O + 1024 * d) for d in range(2)]
        macc = sb("macc", 1024, at=O)
        state, kd_tok = sb("state", 1536, at=O), sb("kd_tok", 512, at=O + 1536)
        g_z = sb("g_z", T, at=place["mean"])
        d_q, d_k = sb("d_q", 2048, at=U), sb("d_k", 2048, at=U + 2048)
        d_v, d_o = sb("d_v", 2048, at=U + 4096), sb("d_o", 2048, at=U + 6144)
        d_p, d_pt = sb("d_p", 2048, at=U + 8192), sb("d_pt", 1024, at=U + 10240)
        d_sq, d_rs = sb("d_sq", 1024, at=U + 8192), sb("d_rs", 1024, at=U + 9216)
        d_t1, d_t2 = sb("d_t1", 512, at=U + 10240), sb("d_t2", 512, at=U + 10752)
        d_nsq = sb("d_nsq", 2048, at=U)
        o_tok = sb("o_tok", 2048, at=O)

        G = [ctx.enter_context(nc.psum_tensor(f"gemm{i}", [P, 512], F32)) for i in range(4)]
        X = [ctx.enter_context(nc.psum_tensor(f"aux{i}", [P, 512], F32)) for i in range(4)]

        def sem(name):
            return ctx.enter_context(nc.semaphore(name))

        landed = [sem("landed0"), sem("landed1")]
        side_in = sem("side_in")
        late_scaled, sq_added = sem("late_scaled"), sem("sq_added")
        res_in, mod_set = sem("res_in"), sem("mod_set")
        c_in, early_in = sem("c_in"), [sem("early_in0"), sem("early_in1")]
        params_in, gates_in, const_in, x_in = sem("params_in"), sem("gates_in"), sem("const_in"), sem("x_in")
        set_zero = sem("set_zero")
        hi_ready, lo_ready = sem("hi_ready"), sem("lo_ready")
        scaled_by_c, pool_summed, dve_summed = sem("scaled_by_c"), sem("pool_summed"), sem("dve_summed")
        z_done = sem("z_done")
        tile_done = sem("tile_done")
        dve_read = sem("dve_read")
        act_step, dve_step, pool_step = sem("act_step"), sem("dve_step"), sem("pool_step")
        setup_t, c_ready_t, c_ready, p_in = sem("setup_t"), sem("c_ready_t"), sem("c_ready"), sem("p_in")
        lam_sum, lam_exp = sem("lam_sum"), sem("lam_exp")
        om_ready, ohi_ready, olo_ready = sem("om_ready"), sem("ohi_ready"), sem("olo_ready")
        sq_ready, stat_done, sd_ready = sem("sq_ready"), sem("stat_done"), sem("sd_ready")
        squares_summed = sem("squares_summed")
        mean_done, mean_ready, centered, normed, res_ready = (
            sem("mean_done"), sem("mean_ready"), sem("centered"), sem("normed"), sem("res_ready"))
        rope_src, rope_cos, rot_done, rot_read, roped = (
            sem("rope_src"), sem("rope_cos"), sem("rot_done"), sem("rot_read"), sem("roped"))
        v_src, gc_ready, idx_done, relu_done, idx_acc = (
            sem("v_src"), sem("gc_ready"), sem("idx_done"), sem("relu_done"), sem("idx_acc"))
        mixed_ready, mod_done, mod_read = sem("mixed_ready"), sem("mod_done"), sem("mod_read")
        score_done, score_read, max_ready, exp_done, prob_ready = (
            sem("score_done"), sem("score_read"), sem("max_ready"), sem("exp_done"), sem("prob_ready"))
        trans_done, pt_ready, pv_done, pv_read = sem("trans_done"), sem("pt_ready"), sem("pv_done"), sem("pv_read")
        gate_in, up_in, silu_done, prod_done, acthi_ready, actlo_ready = (
            sem("gate_in"), sem("up_in"), sem("silu_done"), sem("prod_done"), sem("acthi_ready"), sem("actlo_ready"))
        pp_ready, ple_in, ple_sig, ple_prod = sem("pp_ready"), sem("ple_in"), sem("ple_sig"), sem("ple_prod")
        ple_added = sem("ple_added")
        z_ready, la_done, la_read, lg_ready, seg_ready, b_ready = (
            sem("z_ready"), sem("la_done"), sem("la_read"), sem("lg_ready"), sem("seg_ready"),
            sem("b_ready"))
        dist_ready, grow_ready, fall_ready, kd_ready, v_ready, r_ready, r_act = (
            sem("dist_ready"), sem("grow_ready"), sem("fall_ready"), sem("kd_ready"), sem("v_ready"),
            sem("r_ready"), sem("r_act"))
        ke_ready = sem("ke_ready")
        gs_done, gs_read, st_ready, kt_done, kt_ready, u_done, u_read, go_done, go_read, gated = (
            sem("gs_done"), sem("gs_read"), sem("st_ready"), sem("kt_done"), sem("kt_ready"), sem("u_done"),
            sem("u_read"), sem("go_done"), sem("go_read"), sem("gated"))
        qk_src, qk_sq, qk_stat, qk_sd, qk_normed, qk_cos, qk_rot, qk_rot_read, qk_ready = (
            sem("qk_src"), sem("qk_sq"), sem("qk_stat"), sem("qk_sd"), sem("qk_normed"), sem("qk_cos"),
            sem("qk_rot"), sem("qk_rot_read"), sem("qk_ready"))
        out_done, out_read, stored = sem("out_done"), sem("out_read"), sem("stored")

        def C(name, n=P):
            return const[:, COL_C[name]:COL_C[name] + n]

        def A(name, t=0, n=1):
            return cols_a[:, COL_A[name] + t:COL_A[name] + t + n]

        def B(name, t=0, n=1):
            return cols_b[:, COL_B[name] + t:COL_B[name] + t + n]

        def tl(buf, t, n=1, w=T):
            if isinstance(t, int):
                return buf[:, t * w:(t + n) * w]
            return buf[:, bass.ds(t * w, n * w)]

        def bc(ap, n):
            w = ap.shape[1]
            return ap.rearrange("p (r n) -> p r n", r=1).to_broadcast([P, n, w])

        def v3(ap, n):
            return ap.rearrange("p (r n) -> p r n", r=n)

        ident = C("ident")
        MOD_STEPS, MOD_TAKEN = {0: 8, 2: 9, 4: 10}, {0: (6,), 1: (8,), 3: (9, 7), 5: (10,), 8: (11,)}
        MOD_ORDER = (0, 1, 2, 3, 4, 5, 6, 8, 9, 7, 10, 11)
        mod_half = lambda i: i % 2 if i < 4 else int(i in POOL_SLABS)

        def half_free(i):
            before = [j for j in range(i) if j in MOD_ORDER and mod_half(j) == mod_half(i)]
            return MOD_ORDER.index(before[-1]) + 1 if before else 0

        def kmaj(w, c0, n, i=0):
            v = w.rearrange("(k p) n -> p k n", p=P)
            return v[:, :, c0 + i * n:c0 + (i + 1) * n] if isinstance(i, int) else v[:, :, bass.ds(i * n + c0, n)]

        def flat(slot, k, n):
            buf = raw[slot] if isinstance(slot, int) else slot
            return buf[:, 0:k * n].rearrange("p (k n) -> p k n", k=k)

        w_in, ada = a["w_in"][0], a["w_ada"][0]
        gla_in, diff_in = a["gla_w_in_2"][0], a["diff_w_in_2"][0]

        def columns(w, c0):
            return lambda i, slot: [(flat(slot, KT, 512), kmaj(w, c0, 512, i))]

        def gate_up(wg, cg, wu, cu):
            def srcs(i, slot):
                v = raw[slot][:, :].rearrange("p (k g n) -> p k g n", k=KT, g=2)
                return [(v[:, :, 0, :], kmaj(wg, cg, 256, i)), (v[:, :, 1, :], kmaj(wu, cu, 256, i))]
            return srcs

        def down(w):
            def srcs(i, slot):
                v, s, h = flat(slot, FT, P), kmaj(w, 0, P, i), FT // 2
                return [(v[:, 0:h, :], s[:, 0:h, :]), (v[:, h:FT, :], s[:, h:FT, :])]
            return srcs

        def idx_slab(i, slot):
            v = flat(slot, KT, 512)
            return ([(v[:, :, 0:256], kmaj(w_in, C_QI, 256))]
                    + [(v[:, :, 256 + 32 * r:288 + 32 * r], kmaj(w_in, C_KI, ID)) for r in range(4)]
                    + [(v[:, :, 384 + 64 * r:448 + 64 * r], kmaj(w_in, C_K, HD)) for r in range(2)])

        def v_slab(i, slot):
            v = flat(slot, KT, 72)
            return [(v[:, :, 0:64], kmaj(w_in, C_V, HD)), (v[:, :, 64:72], kmaj(w_in, C_WI, IH))]

        def z_slab(i, slot):
            v = flat(slot, KT, 48)
            return [(v[:, :, 0:32], kmaj(gla_in, 3072, 32)), (v[:, :, 32:48], kmaj(gla_in, 3088, 16))]

        sources = {
            **{f"ada{i}": columns(ada, 512 * i) for i in range(12)},
            "in_q": columns(w_in, 0), "in_idx": idx_slab, "in_v": v_slab,
            "in_gc": columns(w_in, C_GC), "in_hc": columns(w_in, C_HC), "in_gb": columns(w_in, C_GB),
            "out0": columns(a["w_out"][0], 0),
            "gate_up0": gate_up(a["w_gate"][0], 0, a["w_up"][0], 0), "down0": down(a["w_down"][0]),
            "gla_z": z_slab,
            "gla_q": columns(gla_in, 0), "gla_k": columns(gla_in, 512), "gla_v": columns(gla_in, 1024),
            "gla_r": columns(gla_in, 2048), "out1": columns(a["gla_w_out_2"][0], 0),
            "diff_q": columns(diff_in, 0), "diff_k": columns(diff_in, 1024), "diff_v": columns(diff_in, 2048),
            "out2": columns(a["diff_w_out_2"][0], 0),
        }
        for k in (1, 2):
            f_in, w_p = a["ffn_w_in_2"][k - 1], a["ple_w_proj_2"][k - 1]
            sources[f"gate_up{k}"] = gate_up(f_in, 0, f_in, F)
            sources[f"down{k}"] = down(a["ffn_w_out_2"][k - 1])
            sources[f"ple_proj{k}"] = lambda i, slot, w_p=w_p: [(flat(slot, 2, D), kmaj(w_p, 0, D))]
            sources[f"ple_gate{k}"] = columns(a["ple_w_gate_2"][k - 1], 0)

        def bank_of(ph, at, t):
            if ph.tiles == 2:
                return (G[t], 72) if ph.name == "in_v" else (G[2 * at.parity + t], 512)
            if ph.tiles == 8:
                return (G + X[1:])[t % 7], T
            return G[at.parity if ph.tiles == 1 else t], T

        def quarters(ph, t):
            early = {1: (4,), 2: (2, 2), 4: (1, 1, 1, 1) if ph.name[:3] == "in_" else (2, 2, 0, 0), 8: (4,) + 7 * (0,)}
            each = early[ph.tiles]
            return range(sum(each[:t]), sum(each[:t + 1]))

        def follow(ph, at):
            if at.it is not None:
                return ph, At(at.i + 1, at.it, at.b + 1)
            if at.i + 1 < ph.n:
                return ph, At(at.i + 1)
            return (ph.next, At(0)) if ph.next else None

        reader_done = {"split": lo_ready, "dve": dve_summed, "pool": pool_summed, "pe": z_done}
        block = ctx.enter_context(nc.Block())

        @block.sync
        def _(sp):
            sp.dma_start(rows_c[0:KT, :], a["c"][0].rearrange("(r n) -> r n", n=P)).then_inc(c_in, 16)
            sp.dma_start(ident, a["shape_constants"][:, 0:P]).then_inc(c_in, 16)
            for ph in PHASES:
                if ph.by == "pool":
                    continue
                if not ph.ring:
                    i = int(ph.name[3:]) - 2
                    if i == 0:
                        sp.wait_ge(params_in, 16 * (len(ROWS_A) + len(ROWS_B) + 4))
                    for dst, src in sources[ph.name](0, early[i]):
                        sp.dma_start(dst, src).then_inc(early_in[i], 16)
                    if i == 1:
                        sp.dma_start(v3(xin[:, :], 2), a["x"][0].rearrange("(t p) n -> p t n", p=P)).then_inc(x_in, 16)
                    continue

                def load(at, ph=ph):
                    slot = (ph.slot + at.parity) % 2
                    if ph.free[0 if at.it is not None else at.i] is not None:
                        by = {f[0] for f in (ph.free[1:] if at.it is not None else [ph.free[at.i]])}
                        assert len(by) == 1
                        done = reader_done[by.pop()]
                        sp.wait_ge(done, at.of([f[1] if f else 0 for f in ph.free]))
                    for dst, src in sources[ph.name](at.i, slot):
                        sp.dma_start(dst, src).then_inc(landed[slot], 16)

                rounds(sp, ph, load)
            for tt in range(TT):
                sp.wait_ge(out_read, 2 * (tt + 1))
                sp.dma_start(out[0, tt * P:(tt + 1) * P, :], tl(o_tok, tt, w=D)).then_inc(stored, 16)
            sp.wait_ge(stored, 16 * TT)

        @block.gpsimd
        def _(pool):
            me = Steps(pool, pool_step)
            me.did(pool.memset(ones[:, :], 1.0), set_zero)
            me.did(pool.memset(eps[:, 0:1], EPS1), set_zero)
            me.did(pool.memset(eps[:, 1:2], EPS2), set_zero)

            def rope_cosines(r):
                src, tiles, cos = ((2, (0, 1), "cos_q"), (4, (2, 3), "cos_q"), (8, (4, 7), None), (8, (5, 6), "cos_i"))[r]
                pool.wait_ge(rope_src, src)
                if r == 0:
                    pool.wait_ge(const_in, 16)
                if cos:
                    me.did(pool.tensor_tensor(v3(tl(rope_out, tiles[0], 2), 2), v3(tl(rope_in, tiles[0], 2), 2),
                                              bc(C(cos, T), 2), ALU.mult), rope_cos)
                else:
                    pool.tensor_tensor(tl(rope_out, 4), tl(rope_in, 4), C("cos_q", T), ALU.mult)
                    me.did(pool.tensor_tensor(tl(rope_out, 7), tl(rope_in, 7), C("cos_i", T), ALU.mult), rope_cos)

            pool.wait_ge(res_in, 4)
            pool.wait_ge(mod_set, 1)
            for t in range(KT):
                me.did(pool.tensor_scalar(tl(om, t), tl(res, t), mod[:, 8 + t:9 + t], mod[:, t:t + 1],
                                          ALU.mult, ALU.add), om_ready)
            rope_cosines(0)
            rope_cosines(1)
            POOL_ROPES = {4: (2, 3)}

            def sum_slab(i):
                ph = PH[f"ada{i}"]
                w = raw[ph.slot]
                me.next(scaled_by_c)
                me.link(pool.tensor_tensor(w[:, 0:2048], w[:, 0:2048], w[:, 2048:4096], ALU.add))
                me.link(pool.tensor_tensor(w[:, 0:1024], w[:, 0:1024], w[:, 1024:2048], ALU.add))
                wait(pool, mod_done, half_free(i))
                pool.wait_ge(olo_ready, KT)
                me.did(pool.tensor_tensor(tl(macc, mod_half(i), w=512), w[:, 0:512], w[:, 512:1024], ALU.add), pool_summed)

            def load_slab(i):
                ph = PH[f"ada{i}"]
                by, count = ph.free[0]
                pool.wait_ge(reader_done[by], count)
                for dst, src in sources[ph.name](0, ph.slot):
                    pool.dma_start(dst, src).then_inc(side_in, 16)

            for i in POOL_SLABS:
                ph = PH[f"ada{i}"]
                load_slab(i)
                if i in POOL_ROPES:
                    for r in POOL_ROPES[i]:
                        rope_cosines(r)
                sum_slab(i)

            def ffn(k):
                ph = PH[f"gate_up{k}"]
                n0 = FT * k

                def body(at):
                    for j in range(2):
                        n = at.lin(n0 + j, 2)
                        t = at.lin(j, 2)
                        wait(pool, silu_done, n + 1)
                        wait(pool, up_in, n + 1)
                        wait(pool, actlo_ready, n - 1)
                        pool.tensor_tensor(tl(prod, j), tl(sg, j), tl(ut, j), ALU.mult).then_inc(prod_done, 1)
                        if not (isinstance(t, int) and t == 0):
                            wait(pool, acthi_ready, n)
                            pool.tensor_tensor(tl(actlo, t - 1), tl(prod, 1 - j), tl(acthi, t - 1).bitcast(F32),
                                               ALU.subtract).then_inc(actlo_ready, 1)

                rounds(pool, ph, body)
                wait(pool, acthi_ready, n0 + FT)
                pool.tensor_tensor(tl(actlo, FT - 1), tl(prod, 1), tl(acthi, FT - 1).bitcast(F32),
                                   ALU.subtract).then_inc(actlo_ready, 1)

            SQ_BEFORE = {"gla_z": 4 + 4 + 4, "gate_up1": GH, "gate_up2": 4}

            def skip_squares(name):
                me.seen(sq_ready, SQ_BEFORE[name])

            def sum_squares():
                me.next(sq_ready, 2)
                me.did(pool.tensor_tensor(sq_sum[:, :], tl(sq, 0), tl(sq, 1), ALU.add))
                for t in range(2, KT):
                    me.next(sq_ready)
                    me.again()
                    ins = pool.tensor_tensor(sq_sum[:, :], sq_sum[:, :], tl(sq, t), ALU.add)
                    me.did(ins) if t < KT - 1 else me.did(ins, squares_summed)

            def add_square(m, a0, slots, parity, n=None):
                wait(pool, sq_added, m + a0)
                src = tl(slots, parity)
                if isinstance(m, int) and m == 0:
                    pool.tensor_copy(sq_sum[:, :], src).then_inc(sq_added, 1)
                else:
                    last = isinstance(m, int) and m == KT - 1
                    pool.tensor_tensor(sq_sum[:, :], sq_sum[:, :], src, ALU.add).then_inc(
                        squares_summed if last else sq_added, 1)

            def sum_squares_early(name):
                n, a0, ph = me.n.get(sq_ready.name, 0), me.n.get(sq_added.name, 0), PH[name]

                def body(at):
                    for t in range(ph.tiles):
                        m = at.lin(t, ph.tiles)
                        pool.wait_ge(sq_ready, m + (n + 1))
                        add_square(m, a0, dsq, t % 2 if ph.tiles > 1 else at.parity)

                rounds(pool, ph, body)
                me.seen(sq_ready, KT)
                me.seen(sq_added, KT - 1)
                me.seen(squares_summed)

            def ple(k):
                a0 = me.n.get(sq_added.name, 0)
                for t in range(KT):
                    me.next(ple_sig)
                    if t == 0:
                        me.next(pp_ready, KT)
                    if t >= 2:
                        pool.wait_ge(ple_added, KT * (k - 1) + t - 1)
                    me.did(pool.tensor_tensor(tl(prod, t % 2), tl(sg, t % 2), tl(pp, t), ALU.mult), ple_prod)
                    if k == 1:
                        for m in {KT - 1: (t - 2, t - 1, t)}.get(t, (t - 2,) if t >= 2 else ()):
                            me.next(sq_ready)
                            add_square(m, a0, gsq, m % 2)
                if k == 1:
                    me.seen(sq_added, KT - 1)
                    me.seen(squares_summed)

            def late_tiles(n):
                pool.wait_ge(sd_ready, (5, 6)[n])
                for t in (4, 6):
                    me.did(pool.tensor_tensor(v3(tl(res, t, 2), 2), v3(tl(res, t, 2), 2), bc(rstd[:, 0:T], 2),
                                              ALU.mult), late_scaled)

            late_tiles(0)
            ffn(0)
            late_tiles(1)
            skip_squares("gla_z")
            sum_squares()
            pool.wait_ge(z_ready, 1)
            for d in range(2):
                me.link(pool.memset(seg[d][:, :], 1.0))
                edge = 0 if d == 0 else CH - 1
                me.did(pool.memset(v3(seg[d][:, :], 16)[:, :, edge:edge + 1], 0.0), seg_ready)
            for d in range(2):
                pool.wait_ge(grow_ready, 2 * d + 2)
                me.did(pool.tensor_tensor(g_ke[d][:, :], g_k[:, :], g_ke[d][:, :], ALU.mult), ke_ready)
            for h in range(GH):
                pool.wait_ge(go_read, h + 1)
                pool.wait_ge(r_act, 2)
                me.did(pool.tensor_tensor(tl(g_r, 2 * h, 2), tl(g_o, 2 * h, 2), tl(g_r, 2 * h, 2), ALU.mult), gated)
            skip_squares("gate_up1")
            sum_squares_early("out1")
            ffn(1)
            sum_squares_early("down1")
            ple(1)
            for r in range(8):
                me.next(qk_normed)
                buf, t = (d_q, 2 * r) if r < 4 else (d_k, 2 * r - 8)
                if r >= 1:
                    pool.wait_ge(qk_ready, r)
                me.did(pool.tensor_tensor(v3(d_t1[:, :], 2), v3(tl(buf, t, 2), 2), bc(C("cos_d", T), 2),
                                          ALU.mult), qk_cos)
            skip_squares("gate_up2")
            sum_squares_early("out2")
            ffn(2)
            sum_squares_early("down2")
            ple(2)

        @block.scalar
        def _(act):
            me = Steps(act, act_step)

            act.wait_ge(c_ready_t, 1)
            me.did(act.activation(c_act[:, :], X[3][:, 48:56], ACT.Silu), c_ready)
            for rows, spec in ((rows_a, ROWS_A), (rows_b, ROWS_B)):
                n = 0
                for name, k in spec:
                    ap = a[name]
                    flat_ap = ap.rearrange(" ".join("abc"[:len(ap.shape)]) + " -> (" + " ".join("abc"[:len(ap.shape)]) + ")")
                    act.dma_start(rows[n:n + k, :], flat_ap.rearrange("(r n) -> r n", n=P)).then_inc(params_in, 16)
                    n += k
            for n, name in enumerate(("diff_lam_q1_2", "diff_lam_k1_2", "diff_lam_q2_2", "diff_lam_k2_2")):
                act.dma_start(lam_in[:, n * HD:(n + 1) * HD], a[name].to_broadcast([P, HD])).then_inc(params_in, 16)
            act.dma_start(wgate[0:RANK, :], a["gla_w_gate_f_2"][0]).then_inc(gates_in, 16)
            act.dma_start(wgate[32:32 + RANK, :], a["gla_w_gate_b_2"][0]).then_inc(gates_in, 16)

            act.wait_ge(params_in, 16 * (len(ROWS_A) + len(ROWS_B) + 4))
            me.seen(setup_t)
            for n, bank in enumerate((X[0], X[1], X[2], G[1])):
                me.next(setup_t)
                me.did(act.activation(tl(res, n, w=512), bank[:, :], ACT.Copy), res_in)
            act.wait_ge(early_in[1], 16)
            act.dma_start(const[:, P:NC], a["shape_constants"][:, P:NC]).then_inc(const_in, 16)
            act.dma_start(pin[:, :].rearrange("p (l t n) -> p l t n", l=2, t=2),
                          a["p_2"].rearrange("l b (t p) n -> p l (b t) n", p=P)).then_inc(p_in, 16)

            def split(ph, at, q):
                slot, w = (ph.slot + at.parity) % 2, ph.cols // 4
                hslot = (ph.j0 + at.parity) % 2
                if q == 0:
                    act.wait_ge(landed[slot], at.of(ph.landed))
                act.activation(whi[hslot][:, q * w:(q + 1) * w], raw[slot][:, q * w:(q + 1) * w],
                               ACT.Copy).then_inc(hi_ready, 1)

            def ahead(ph, at, q):
                nxt = follow(ph, at)
                if nxt is None:
                    return
                if q == 0:
                    wait(act, tile_done, at.lin(ph.tile0, ph.tiles))
                split(*nxt, q)

            def high_and_square(m, o, a0, src, hi, slots, parity):
                wait(act, om_ready, m + (o + 1))
                act.activation(tl(hi, m), src, ACT.Copy).then_inc(ohi_ready, 1)
                wait(act, sq_added, m + (a0 - 1))
                act.activation(tl(slots, parity), tl(res, m), ACT.Square).then_inc(sq_ready, 1)

            def next_seen():
                for sem_ in (om_ready, ohi_ready, sq_ready):
                    me.seen(sem_, KT)
                me.seen(sq_added, KT - 1)

            def prep(order=range(KT), free=None, squares=False, then=None, hi=ohi):
                if free:
                    wait(act, tile_done, free)
                for t in order:
                    me.next(om_ready)
                    me.did(act.activation(tl(hi, t), tl(om, t), ACT.Copy), ohi_ready)
                    if then:
                        then(t)
                    if squares:
                        me.did(act.activation(tl(sq, t), tl(res, t), ACT.Square), sq_ready)

            def root(bank, n, scale, e, dst, done=stat_done, ready=sd_ready):
                me.next(done)
                me.link(act.activation(dst, bank[:, 0:n], ACT.Ln, bias=eps[:, e:e + 1], scale=scale))
                me.did(act.activation(dst, dst, ACT.Exp, scale=-0.5), ready)

            def roots(pairs, scale, e, done=stat_done, ready=sd_ready):
                for bank, dst in pairs:
                    me.next(done)
                    me.did(act.activation(dst, bank[:, :], ACT.Ln, bias=eps[:, e:e + 1], scale=scale))
                me.again()
                for bank, dst in pairs:
                    me.did(act.activation(dst, dst, ACT.Exp, scale=-0.5), ready)

            def squares(groups, src, buf):
                for g in groups:
                    me.next(mixed_ready, 2)
                    me.did(act.activation(tl(buf, 2 * g, 2), tl(src, 2 * g, 2), ACT.Square), sq_ready)

            def group_root(groups, src, buf, scale, e, banks, then=None):
                squares(groups, src, buf)
                if then:
                    then()
                roots([(banks[n], tl(buf, 2 * g, 2)) for n, g in enumerate(groups)], scale, e)

            act.wait_ge(set_zero, 3)
            for q in range(4):
                split(PH["in_q"], At(0), q)
            act.wait_ge(mod_set, 1)
            me.again(res_in)
            for t in range(KT):
                me.did(act.activation(tl(ohi, t), tl(res, t), ACT.Identity, bias=mod[:, t:t + 1],
                                      scale=mod[:, 8 + t:9 + t]), ohi_ready)
                me.seen(om_ready)

            def evac(dst_of, sem_, scale_of=None):
                def one(ph, at, t):
                    wait(act, tile_done, at.lin(ph.tile0 + t + 1, ph.tiles))
                    bank, n = bank_of(ph, at, t)
                    kw = {"scale": scale_of(t)} if scale_of else {}
                    me.did(act.activation(dst_of(at, t), bank[:, 0:n], ACT.Copy, **kw), sem_)
                return one

            def gemm(name, one=None, after=None):
                ph = PH[name]

                def body(at):
                    for t in range(ph.tiles):
                        for q in quarters(ph, t):
                            ahead(ph, at, q)
                        if one:
                            one(ph, at, t)
                        if after:
                            after(at, t)

                rounds(act, ph, body)

            def scale_by_c(i):
                ph = PH[f"ada{i}"]
                act.wait_ge(side_in, 16 * (POOL_SLABS.index(i) + 1))
                for k in range(KT):
                    w = raw[ph.slot][:, 512 * k:512 * (k + 1)]
                    ins = act.activation(w, w, ACT.Copy, scale=c_act[:, k:k + 1])
                me.did(ins, scaled_by_c)

            gemm("in_q", evac(lambda at, t: tl(rope_in, t), rope_src))
            act.wait_ge(lam_sum, 1)
            me.did(act.activation(lam[:, 2:4], lam[:, 0:2], ACT.Exp), lam_exp)
            gemm("in_idx", evac(lambda at, t: tl(rope_in, (5, 6, 7, 4)[t]), rope_src))
            gemm("in_v", evac(lambda at, t: vtok[:, 72 * t:72 * t + 72], v_src))
            scale_by_c(4)
            gemm("in_gc", evac(lambda at, t: tl(gc, t), gc_ready))
            for h in range(IH):
                me.next(idx_done)
                if h >= 2:
                    act.wait_ge(idx_acc, 2 * (h - 1))
                me.did(act.activation(tl(relu, h % 2, w=384), G[h % 4][:, 0:384], ACT.Relu), relu_done)
            scale_by_c(5)
            gemm("in_hc")
            scale_by_c(6)
            gemm("in_gb")
            group_root((2, 3), mixed, mix_sq, 1.0 / HD, 0, X[0:2])
            for i in range(NH + 1):
                if i < NH:
                    me.next(max_ready)
                    for qt, (c0, n) in enumerate(((0, P), (P, 2 * P))):
                        ap = logit[:, 384 * (i % 2) + c0:384 * (i % 2) + c0 + n]
                        ins = act.activation(ap, ap, ACT.Exp, bias=neg_max[:, 2 * (i % 2) + qt:2 * (i % 2) + qt + 1],
                                             accum_out=sums[:, 2 * (i % 2) + qt:2 * (i % 2) + qt + 1])
                    me.did(ins, exp_done)
                if i == 1:
                    prep(order=(4, 5, 6, 7), free=PH["in_gb"].tile0 + 4)
                    scale_by_c(7)
                if i == 4:
                    scale_by_c(11)
                if i >= 1:
                    me.next(trans_done)
                    if i >= 3:
                        act.wait_ge(pv_done, i - 2)
                    me.did(act.activation(tl(prob_t, (i - 1) % 2, w=384), G[2 + (i - 1) % 2][:, 0:384],
                                          ACT.Copy), pt_ready)
            group_root((0, 1), mixed, mix_sq, 1.0 / HD, 0, X[0:2],
                       lambda: [split(PH["out0"], At(0), q) for q in range(4)])
            prep(order=(0, 1, 2, 3))
            gemm("out0")

            def layer_norm(n, squares):
                for t in range(0, KT, 2):
                    me.next(centered)
                    me.did(act.activation(tl(sq, t, 2), tl(res, t, 2), ACT.Square), sq_ready)
                root(X[1], T, 1.0 / D, 0, rstd[:, 0:T])
                g, b = (fold[:, 16:24], fold[:, 24:32]) if n == 0 else (A("ln2_g", 0, 8), A("ln2_b", 0, 8))

                prep(free=PH["out0" if n == 0 else "down0"].tile0 + 8)
                for t in range(KT + 1):
                    if t < KT:
                        me.did(act.activation(tl(res, t), tl(res, t), ACT.Identity, bias=b[:, t:t + 1],
                                              scale=g[:, t:t + 1]), res_ready)
                    if squares and t:
                        me.again(res_ready, less=int(t < KT))
                        me.did(act.activation(tl(sq, t - 1), tl(res, t - 1), ACT.Square), sq_ready)

            def ffn(k):
                n0 = FT * k

                def high(n, t, j):
                    wait(act, prod_done, n + 1)
                    act.activation(tl(acthi, t), tl(prod, j), ACT.Copy).then_inc(acthi_ready, 1)

                def after(at, t):
                    if t % 2 == 0:
                        return
                    j = t // 2
                    n, m = at.lin(n0 + j, 2), at.lin(j, 2)
                    wait(act, gate_in, n + 1)
                    wait(act, prod_done, n - 1)
                    act.activation(tl(sg, j), tl(gt, j), ACT.Silu).then_inc(silu_done, 1)
                    if not (isinstance(m, int) and m == 0):
                        high(n - 1, m - 1, 1 - j)

                gemm(f"gate_up{k}", after=after)
                high(n0 + FT - 1, FT - 1, 1)
                o, a0 = me.n.get(om_ready.name, 0), me.n.get(sq_added.name, 0)
                early = lambda at, t: high_and_square(at.i, o, a0, tl(om, at.i), ohi, dsq, at.parity)
                gemm(f"down{k}", after=early if k else None)
                if k:
                    next_seen()

            layer_norm(0, False)
            ffn(0)
            layer_norm(1, True)
            root(X[0], T + 2, 1.0 / D, 1, rstd[:, :])
            def out_gemm(name):
                o, a0 = me.n.get(om_ready.name, 0), me.n.get(sq_added.name, 0)
                gemm(name, after=lambda at, t: high_and_square(4 * at.i + t, o, a0, tl(om_next, t % 2), ohi, dsq, t % 2))
                next_seen()

            gemm("gla_q")
            gemm("gla_k")
            for d in range(2):
                act.wait_ge(la_read, 2 * d + 2)
                me.link(act.activation(g_b[d][:, :], g_la[d][:, :], ACT.Abs))
                me.link(act.activation(g_b[d][:, :], g_b[d][:, :], ACT.Exp, scale=-1.0))
                me.did(act.activation(g_b[d][:, :], g_b[d][:, :], ACT.Ln, bias=ones[:, 0:1]), lg_ready)

            def v_dst(buf):
                return lambda at, t: buf[:, t * D + at.i * 512:t * D + at.i * 512 + 512]

            v_scale = lambda t: rstd[:, T + t:T + t + 1]
            act.wait_ge(z_ready, 1)
            ph = PH["gla_v"]
            v_evac = evac(v_dst(g_v), v_ready, v_scale)

            def gla_after(at, t):
                if at.i == 1 and t == 0:
                    for d in range(2):
                        me.next(b_ready)
                        me.did(act.activation(g_la[d][:, :], g_b[d][:, :], ACT.Exp, scale=1.0 / TAU), grow_ready)
                        me.did(act.activation(g_ke[d][:, :], g_b[d][:, :], ACT.Exp, scale=-1.0 / TAU), grow_ready)
                if at.i == 1 and t == 1:
                    for d in range(2):
                        me.next(dist_ready)
                        me.did(act.activation(g_b[d][:, :], g_b[d][:, :], ACT.Exp, scale=1.0 / TAU), fall_ready)

            gemm("gla_v", v_evac, gla_after)
            gemm("gla_r")
            for d in range(2):
                act.wait_ge(r_ready, 4 * (d + 1))
                me.did(act.activation(tl(g_r, 4 * d, 4), tl(g_r, 4 * d, 4), ACT.Silu), r_act)
            for h in range(GH + 1):
                if h < GH:
                    me.next(kt_done)
                    me.did(act.activation(kd_tok[:, :], G[1][:, :], ACT.Copy), kt_ready)
                if h == 0:
                    wait(act, tile_done, PH["gla_r"].tile0 + 8)
                else:
                    act.wait_ge(go_read, h)
                    me.did(act.activation(tl(g_sq, 2 * h - 2, 2), tl(g_o, 2 * h - 2, 2), ACT.Square), sq_ready)
            roots([(G[n], g_rs[:, 512 * n:512 * n + 512]) for n in range(2)], 1.0 / GDV, 1)
            prep(hi=xhi, free=PH["gla_r"].tile0 + 8)
            out_gemm("out1")

            def ple(k):
                gemm(f"ple_proj{k}", evac(lambda at, t: tl(pp, t), pp_ready))
                root(X[0], T, 1.0 / D, 1, rstd[:, 0:T])

                def after(at, t):
                    n = KT * (k - 1) + 4 * at.i + t
                    act.wait_ge(ple_in, n + 1)
                    wait(act, ple_prod, n - 1)
                    act.activation(tl(sg, t % 2), tl(gt, t % 2), ACT.Sigmoid).then_inc(ple_sig, 1)
                    m = 4 * at.i + t
                    if early and m:
                        high_and_square(m - 1, o, a0, tl(om, m - 1), dhi, gsq, (m - 1) % 2)

                o, a0 = me.n.get(om_ready.name, 0), me.n.get(sq_added.name, 0)
                early = k == 1
                gemm(f"ple_gate{k}", after=after)
                if early:
                    high_and_square(KT - 1, o, a0, tl(om, KT - 1), dhi, gsq, 1)
                    next_seen()

            root(X[0], T, 1.0 / D, 1, rstd[:, 0:T])
            ffn(1)
            ple(1)
            root(X[0], T + 2, 1.0 / D, 1, rstd[:, :])
            for base, name in ((0, "diff_q"), (4, "diff_k")):
                def after(at, t, base=base):
                    buf = d_q if base == 0 else d_k
                    if t % 2 == 1:
                        r = base + 2 * at.i + t // 2
                        act.wait_ge(qk_src, 2 * r + 2)
                        if r >= 2:
                            act.wait_ge(qk_stat, r - 1)
                        me.did(act.activation(tl(d_sq, r % 2, w=512), tl(buf, 2 * (r - base), 2), ACT.Square), qk_sq)
                    if t == 3:
                        r = base + 2 * at.i
                        if r >= 2:
                            act.wait_ge(qk_normed, r)
                        roots([(X[n], tl(d_rs, n, w=512)) for n in range(2)], 1.0 / HD, 1, qk_stat, qk_sd)
                gemm(name, after=after)
            gemm("diff_v", evac(v_dst(d_v), v_ready, v_scale))
            for i in range(NH + 1):
                if i < NH:
                    me.next(max_ready)
                    for c in range(2):
                        for qt in range(2):
                            n = 4 * (i % 2) + 2 * c + qt
                            if i >= 2:
                                act.wait_ge(trans_done, NH + i - 1)
                            ins = act.activation(tl(d_p, 4 * (i % 2) + 2 * c + qt),
                                                 G[2 * (i % 2) + c][:, qt * T:(qt + 1) * T], ACT.Exp,
                                                 bias=neg_max[:, n:n + 1], scale=HD ** -0.5,
                                                 accum_out=sums[:, n:n + 1])
                        me.did(ins, exp_done)
                if i == NH:
                    squares((0, 1), d_o, d_nsq)
                if i >= 1:
                    me.next(trans_done)
                    if i >= 3:
                        act.wait_ge(pv_done, NH + i - 2)
                    me.did(act.activation(tl(d_pt, (i - 1) % 2, w=512), X[(i - 1) % 2][:, :], ACT.Copy), pt_ready)
            squares((2, 3), d_o, d_nsq)
            roots([(G[g], tl(d_nsq, 2 * g, 2)) for g in range(4)], 1.0 / (2 * HD), 1)
            prep(hi=xhi, free=PH["diff_v"].tile0 + 4)
            out_gemm("out2")
            root(X[0], T, 1.0 / D, 1, rstd[:, 0:T])
            ffn(2)
            ple(2)

        @block.vector
        def _(dve):
            me = Steps(dve, dve_step)

            def low(ph, at, q):
                slot, w = (ph.slot + at.parity) % 2, ph.cols // 4
                hslot = (ph.j0 + at.parity) % 2
                dve.wait_ge(hi_ready, at.lin(4 * ph.j0 + q + 1, 4))
                dve.tensor_tensor(wlo[hslot][:, q * w:(q + 1) * w], raw[slot][:, q * w:(q + 1) * w],
                                  whi[hslot][:, q * w:(q + 1) * w].bitcast(F32), ALU.subtract).then_inc(lo_ready, 1)

            def gemm(name, one=None, after=None):
                ph = PH[name]

                def body(at):
                    for t in range(ph.tiles):
                        nxt = follow(ph, at)
                        if nxt is not None:
                            for q in quarters(ph, t):
                                low(*nxt, q)
                        if one:
                            wait(dve, tile_done, at.lin(ph.tile0 + t + 1, ph.tiles))
                            one(at, t, bank_of(ph, at, t)[0])
                        if after:
                            after(at, t)

                rounds(dve, ph, body)

            def low_part(m, src, hi, lo):
                return dve.tensor_tensor(tl(lo, m), src, tl(hi, m).bitcast(F32), ALU.subtract)

            def prep(make, order=range(KT), free=None, hi=ohi, lo=olo):
                if free:
                    wait(dve, tile_done, free)

                def rest(t):
                    me.next(ohi_ready)
                    me.did(low_part(t, tl(om, t), hi, lo), olo_ready)

                last = None
                for t in order:
                    me.did(make(t), om_ready)
                    if last is not None:
                        rest(last)
                    last = t
                rest(last)

            def modulate(i):
                ph = PH[f"ada{i}"]
                if ph.ring:
                    src, came = raw[ph.slot], (landed[ph.slot], ph.landed[0])
                else:
                    src, came = early[i - 2], (early_in[i - 2], 16)
                acc = tl(macc, mod_half(i), w=512)
                dve.wait_ge(*came)
                wait(dve, mod_done, half_free(i))
                me.link(dve.tensor_scalar(acc, src[:, 0:512], c_act[:, 0:1], None, ALU.mult))
                for k in range(1, KT - 1):
                    me.link(dve.scalar_tensor_tensor(acc, src[:, 512 * k:512 * (k + 1)], c_act[:, k:k + 1], acc,
                                                     ALU.mult, ALU.add))
                k = KT - 1
                me.did(dve.scalar_tensor_tensor(acc, src[:, 512 * k:512 * (k + 1)], c_act[:, k:k + 1], acc,
                                                ALU.mult, ALU.add), dve_summed)

            dve.wait_ge(set_zero, 3)
            dve.wait_ge(c_ready, 1)
            modulate(0)
            modulate(1)
            me.next(setup_t)
            me.did(dve.tensor_copy(cols_b[:, :], G[0][:, P:P + NB]))
            me.did(dve.tensor_copy(cols_a[:, :], G[0][:, 0:NA]), dve_read)
            modulate(2)
            modulate(3)
            dve.wait_ge(mod_done, 4)
            me.again(dve_read)
            me.link(dve.tensor_tensor(mod[:, 0:16], X[3][:, 0:16], A("b_ada", 0, 16), ALU.add), mod_read)
            me.did(dve.tensor_scalar(mod[:, 8:16], mod[:, 8:16], 1.0, None, ALU.add), mod_set)
            for q in range(4):
                low(PH["in_q"], At(0), q)
            for t in range(KT):
                dve.wait_ge(om_ready, t + 1)
                me.seen(om_ready)
                me.next(ohi_ready)
                me.did(dve.tensor_tensor(tl(olo, t), tl(om, t), tl(ohi, t).bitcast(F32), ALU.subtract), olo_ready)
            me.did(dve.tensor_scalar(res[:, :], res[:, :], ALPHA, None, ALU.mult))
            def rope(r):
                bank = X[(0, 1, 2, 0)[r]]
                me.next(rot_done)
                if r == 2:
                    dve.tensor_tensor(tl(mixed, 4), bank[:, 0:T], C("sin_q", T), ALU.mult)
                    me.did(dve.tensor_tensor(tl(mixed, 7), bank[:, T:2 * T], C("sin_i", T), ALU.mult), rot_read)
                    pairs = ((4, 1), (7, 1))
                else:
                    t = (0, 2, None, 5)[r]
                    me.did(dve.tensor_tensor(v3(tl(mixed, t, 2), 2), v3(bank[:, :], 2),
                                             bc(C("sin_i" if r == 3 else "sin_q", T), 2), ALU.mult), rot_read)
                    pairs = ((t, 2),)
                me.next(rope_cos)
                me.again(rot_read)
                for t, n in pairs:
                    ins = dve.tensor_tensor(tl(rope_out, t, n), tl(rope_out, t, n), tl(mixed, t, n), ALU.add)
                me.did(ins, roped)

            gemm("in_q")
            for layer in range(2):
                bank = X[1 + layer]
                if layer == 0:
                    me.seen(setup_t, 4)
                me.next(setup_t)
                me.link(dve.tensor_copy(tl(p_hi, layer, w=512), bank[:, :]))
                me.did(dve.tensor_tensor(tl(p_lo, layer, w=512), bank[:, :], tl(p_hi, layer, w=512).bitcast(F32),
                                         ALU.subtract), dve_read)
            me.did(dve.memset(v3(upad[:, :], 4)[:, :, 0:2], 0.0))
            lam4 = lam_in[:, :].rearrange("p (e s n) -> p e s n", e=2, s=2)
            me.link(dve.tensor_tensor(lam4[:, :, 0, :], lam4[:, :, 0, :], lam4[:, :, 1, :], ALU.mult))
            me.did(dve.tensor_reduce(lam[:, 0:2], lam4[:, :, 0, :], AX, ALU.add), lam_sum)
            me.next(lam_exp)
            me.link(dve.tensor_tensor(lam[:, 4:5], lam[:, 3:4], lam[:, 2:3], ALU.subtract))
            me.link(dve.tensor_scalar(lam[:, 4:5], lam[:, 4:5], -LAMBDA_INIT, None, ALU.add))
            me.did(dve.tensor_scalar(lam[:, 5:6], B("diff_g_sub_2"), 1.0 - LAMBDA_INIT, None, ALU.mult))
            gemm("in_idx")
            rope(0)
            rope(1)
            gemm("in_v")
            rope(2)
            rope(3)
            me.next(v_src, 2)
            me.link(dve.tensor_scalar(v3(vtok[:, :], 2)[:, :, 64:72], v3(vtok[:, :], 2)[:, :, 64:72],
                                      IH ** -0.5 * ID ** -0.5, None, ALU.mult))
            gemm("in_gc")
            BLOCKS = ((0, 0, P), (1, P, 2 * P))
            for h in range(IH):
                me.next(relu_done)
                for tt, c0, n in BLOCKS:
                    w = vtok[:, 72 * tt + 64 + h:72 * tt + 65 + h]
                    r = relu[:, 384 * (h % 2) + c0:384 * (h % 2) + c0 + n]
                    if h:
                        me.again(idx_acc, less=1)
                        me.did(dve.scalar_tensor_tensor(score[:, c0:c0 + n], r, w, score[:, c0:c0 + n],
                                                        ALU.mult, ALU.add), idx_acc)
                    else:
                        me.did(dve.tensor_scalar(score[:, c0:c0 + n], r, w, None, ALU.mult), idx_acc)

            def short_conv(at, t, bank):
                u = upad[:, (T + 2) * t:(T + 2) * (t + 1)]
                me.next(gc_ready)
                me.link(dve.tensor_tensor(u[:, 2:T + 2], bank[:, 0:T], tl(gc, t), ALU.mult), dve_read)
                me.link(dve.tensor_scalar(tl(conv, t), u[:, 0:T], A("conv_w", t), None, ALU.mult))
                for j in (1, 2):
                    me.link(dve.scalar_tensor_tensor(tl(conv, t), u[:, j:j + T], A("conv_w", 4 * j + t), tl(conv, t),
                                                     ALU.mult, ALU.add))

            gemm("in_hc", short_conv)
            me.again(idx_acc)
            me.link(dve.tensor_tensor(kept[:, :], score[:, :], C("causal", 384), ALU.add))
            for _ in range(TOPK // 8):
                for tt, c0, n in BLOCKS:
                    me.did(dve.max(top8[:, 8 * tt:8 * tt + 8], kept[:, c0:c0 + n]))
                for tt, c0, n in BLOCKS:
                    me.again(less=1)
                    me.did(dve.match_replace(kept[:, c0:c0 + n], top8[:, 8 * tt:8 * tt + 8], kept[:, c0:c0 + n],
                                             TAKEN))
                me.again()
            me.link(dve.tensor_scalar(allow[:, :], kept[:, :], TAKEN / 1e3, NEG, ALU.is_gt, ALU.mult))
            me.did(dve.tensor_tensor(allow[:, :], allow[:, :], C("causal", 384), ALU.add))

            def gated_conv(at, t, bank):
                me.did(dve.tensor_tensor(tl(mixed, 4 + t), bank[:, 0:T], tl(conv, t), ALU.mult), mixed_ready)

            gemm("in_gb", gated_conv)

            def group_make(src, buf, gain):
                def make(t):
                    if t % 2 == 0:
                        me.next(sd_ready)
                    return dve.scalar_tensor_tensor(tl(om, t), tl(src, t), gain(t), tl(buf, t), ALU.mult, ALU.mult)
                return make

            mix_make = group_make(mixed, mix_sq, lambda t: A("attn_norm_g", t) if t < 4 else A("conv_norm_g", t - 4))
            me.again(mixed_ready)
            me.again()
            for i in range(NH + 3):
                if i < NH:
                    me.next(score_done)
                    if i >= 2:
                        dve.wait_ge(trans_done, i - 1)
                    lg = tl(logit, i % 2, w=384)
                    me.link(dve.scalar_tensor_tensor(lg, G[i % 2][:, 0:384], HD ** -0.5, allow[:, :],
                                                     ALU.mult, ALU.add), score_read)
                    for tt, c0, n in BLOCKS:
                        ins = dve.tensor_reduce(neg_max[:, 2 * (i % 2) + tt:2 * (i % 2) + tt + 1], lg[:, c0:c0 + n],
                                                AX, ALU.max, negate=True)
                    me.did(ins, max_ready)
                if i in MOD_STEPS:
                    modulate(MOD_STEPS[i])
                if 1 <= i <= NH:
                    me.next(exp_done)
                    s = (i - 1) % 2
                    me.link(dve.reciprocal(rsum[:, 2 * s:2 * s + 2], sums[:, 2 * s:2 * s + 2]))
                    for tt, c0, n in BLOCKS:
                        ap = logit[:, 384 * s + c0:384 * s + c0 + n]
                        ins = dve.tensor_scalar(ap, ap, rsum[:, 2 * s + tt:2 * s + tt + 1], None, ALU.mult)
                    me.did(ins, prob_ready)
                if i == 1:
                    prep(mix_make, order=(4, 5, 6, 7), free=PH["in_gb"].tile0 + 4)
                if i >= 4 and i % 2 == 0:
                    me.next(pv_done, 2)
                    me.did(dve.tensor_copy(tl(mixed, (i - 4) // 2), X[(i - 4) // 2 % 2][:, 0:T]), mixed_ready)
            dve.wait_ge(mod_done, 12)
            me.link(dve.tensor_tensor(mod[:, 16:48], X[3][:, 16:48], A("b_ada", 16, 32), ALU.add), mod_read)
            me.link(dve.tensor_scalar(mod[:, 32:40], mod[:, 32:40], 1.0, None, ALU.add))
            me.did(dve.tensor_tensor(fold[:, 0:8], A("ln1_g", 0, 8), mod[:, 32:40], ALU.mult))
            me.link(dve.tensor_tensor(fold[:, 8:16], A("ln1_b", 0, 8), mod[:, 32:40], ALU.mult))
            me.did(dve.tensor_tensor(fold[:, 8:16], fold[:, 8:16], mod[:, 24:32], ALU.add))
            me.did(dve.tensor_scalar(fold[:, 16:24], A("ln1_g", 0, 8), ALPHA, None, ALU.mult))
            me.did(dve.tensor_scalar(fold[:, 24:32], A("ln1_b", 0, 8), ALPHA, None, ALU.mult))
            me.did(dve.tensor_tensor(fold[:, 32:40], A("ln2_g", 0, 8), B("norm_mix_2", 0, 8), ALU.mult))
            me.link(dve.tensor_tensor(fold[:, 40:48], A("ln2_b", 0, 8), B("norm_mix_2", 0, 8), ALU.mult))
            for q in range(4):
                low(PH["out0"], At(0), q)
            me.again(mixed_ready)
            prep(mix_make, order=(0, 1, 2, 3))

            def residual(tiles, gate=None):
                def one(at, t, bank):
                    m = at.lin(t, tiles)
                    if gate is None:
                        ins = dve.tensor_tensor(tl(res, m), bank[:, 0:T], tl(res, m), ALU.add)
                    else:
                        g = mod[:, gate + m:gate + m + 1] if isinstance(m, int) else mod[:, bass.ds(m + gate, 1)]
                        ins = dve.scalar_tensor_tensor(tl(res, m), bank[:, 0:T], g, tl(res, m), ALU.mult, ALU.add)
                    ins.then_inc(dve_read, 1)
                return one

            def add_to_residual(name, gate=None, after=None):
                gemm(name, residual(PH[name].tiles, gate), after)
                me.seen(dve_read, PH[name].tiles * PH[name].n)

            add_to_residual("out0", 16)

            def layer_norm(n):
                me.again(dve_read)
                me.next(mean_done)
                me.link(dve.tensor_scalar(mean[:, :], X[0][:, 0:T], 1.0 / D, None, ALU.mult), mean_ready)
                for t in range(0, KT, 2):
                    me.did(dve.tensor_tensor(v3(tl(res, t, 2), 2), v3(tl(res, t, 2), 2), bc(mean[:, :], 2),
                                             ALU.subtract), centered)
                me.next(sd_ready)
                me.again(centered)
                def scaled_tiles(t):
                    if t in (0, 2):
                        me.link(dve.tensor_tensor(v3(tl(res, t, 2), 2), v3(tl(res, t, 2), 2), bc(rstd[:, 0:T], 2),
                                                  ALU.mult))
                    elif t in (4, 6):
                        me.next(late_scaled)

                g, b = (fold[:, 0:8], fold[:, 8:16]) if n == 0 else (fold[:, 32:40], fold[:, 40:48])
                def make(t):
                    scaled_tiles(t)
                    return dve.tensor_scalar(tl(om, t), tl(res, t), g[:, t:t + 1], b[:, t:t + 1], ALU.mult, ALU.add)

                prep(make, free=PH["out0" if n == 0 else "down0"].tile0 + 8)

            def root():
                me.next(sd_ready)

            def out_gemm(name, row):
                d, l = me.n.get(dve_read.name, 0), me.n.get(olo_ready.name, 0)

                def rest(m):
                    me.next(ohi_ready)
                    me.did(low_part(m, tl(om_next, m % 2), ohi, olo), olo_ready)

                def after(at, t):
                    m = 4 * at.i + t
                    dve.wait_ge(dve_read, d + m + 1)
                    wait(dve, olo_ready, l + m - 1)
                    me.did(dve.tensor_scalar(tl(om_next, m % 2), tl(res, m), B("norm_ffn_2", row + m), None, ALU.mult),
                           om_ready)
                    if m:
                        rest(m - 1)

                add_to_residual(name, None, after)
                rest(KT - 1)

            def ffn(k):
                n0 = FT * k

                def one(at, t, bank):
                    j = t // 2
                    n = at.lin(n0 + j, 2)
                    wait(dve, silu_done if t % 2 == 0 else prod_done, n - 1)
                    dst = tl(gt if t % 2 == 0 else ut, j)
                    if k == 0:
                        ins = dve.tensor_copy(dst, bank[:, 0:T])
                    else:
                        ins = dve.tensor_tensor(dst, bank[:, 0:T], rstd[:, 0:T], ALU.mult)
                    ins.then_inc(gate_in if t % 2 == 0 else up_in, 1)

                gemm(f"gate_up{k}", one)
                if k == 0:
                    dve.wait_ge(res_ready, KT)
                d, h = me.n.get(dve_read.name, 0), me.n.get(ohi_ready.name, 0)

                def early(at, t):
                    m = at.i
                    c = COL_B["ple_norm_2"] + KT * (k - 1)
                    gain = cols_b[:, c + m:c + m + 1] if isinstance(m, int) else cols_b[:, bass.ds(m + c, 1)]
                    dve.wait_ge(dve_read, at.lin(d + 1, 1))
                    dve.tensor_scalar(tl(om, m), tl(res, m), gain, None, ALU.mult).then_inc(om_ready, 1)
                    dve.wait_ge(ohi_ready, at.lin(h + 1, 1))
                    dve.tensor_tensor(tl(olo, m), tl(om, m), tl(ohi, m).bitcast(F32), ALU.subtract).then_inc(olo_ready, 1)

                add_to_residual(f"down{k}", 40 if k == 0 else None, early if k else None)
                if k:
                    for sem_ in (om_ready, ohi_ready, olo_ready):
                        me.seen(sem_, KT)

            def ple(k):
                gemm(f"ple_proj{k}")
                root()

                def rest(t):
                    me.next(ohi_ready)
                    me.did(low_part(t, tl(om, t), dhi, xlo), olo_ready)

                def add(t):
                    me.next(ple_prod)
                    ins = dve.tensor_tensor(tl(res, t), tl(res, t), tl(prod, t % 2), ALU.add)
                    if k == 2:
                        me.did(ins, ple_added)
                        return
                    me.link(ins, ple_added)
                    me.did(dve.tensor_scalar(tl(om, t), tl(res, t), B("norm_mix_2", KT + t), None, ALU.mult), om_ready)
                    if t:
                        rest(t - 1)
                    if t == KT - 1:
                        rest(t)

                def one(at, t, bank):
                    m = 4 * at.i + t
                    wait(dve, ple_sig, KT * (k - 1) + m - 1)
                    me.did(dve.tensor_tensor(tl(gt, t % 2), bank[:, 0:T], rstd[:, 0:T], ALU.mult), ple_in)
                    if m:
                        add(m - 1)

                gemm(f"ple_gate{k}", one)
                add(KT - 1)

            layer_norm(0)
            ffn(0)

            layer_norm(1)
            root()
            me.next(z_done)
            for o in (0, 32):
                ins = dve.tensor_tensor(g_z[o:o + RANK, :], X[1][o:o + RANK, 0:T], rstd[o:o + RANK, 0:T], ALU.mult)
            me.did(ins, z_ready)

            def scaled(buf, ready, k=None):
                def one(at, t, bank):
                    m = 4 * at.i + t
                    if k is None:
                        ins = dve.tensor_tensor(tl(buf, m), bank[:, 0:T], rstd[:, 0:T], ALU.mult)
                    else:
                        ins = dve.scalar_tensor_tensor(tl(buf, m), bank[:, 0:T], k, rstd[:, 0:T], ALU.mult, ALU.mult)
                    me.did(ins, ready)
                return one

            gemm("gla_q", scaled(g_q, dve_read, GDK ** -0.5))
            for b in range(4):
                me.next(la_done)
                for half in range(2):
                    t = 2 * (b % 2) + half
                    ins = dve.tensor_scalar(tl(g_la[b // 2], t), X[b][:, half * T:(half + 1) * T],
                                            B("gla_b_gate_f_2" if b < 2 else "gla_b_gate_b_2", t), None, ALU.add)
                me.did(ins, la_read)
            gemm("gla_k", scaled(g_k, dve_read))
            ends = lambda buf, d: v3(buf[:, :], 16)[:, :, CH - 1:CH] if d == 0 else v3(buf[:, :], 16)[:, :, 0:1]
            for d in range(2):
                me.next(lg_ready)
                me.link(dve.scalar_tensor_tensor(g_la[d][:, :], g_la[d][:, :], 0.0, g_b[d][:, :], ALU.min,
                                                 ALU.subtract))
                me.next(seg_ready)
                way = (lambda ap: ap[:, :]) if d == 0 else (lambda ap: ap[:, ::-1])
                me.link(dve.tensor_tensor_scan(way(g_b[d]), way(seg[d]), way(g_la[d]), 0.0, ALU.mult, ALU.add),
                        b_ready)
                me.did(dve.tensor_copy(v3(total[:, 16 * d:16 * d + 16], 16), ends(g_b[d], d)))

            def gla_after(at, t):
                if at.i == 1 and t == 0:
                    for d in range(2):
                        me.next(grow_ready, 2)
                        me.again()
                        tot = total[:, 16 * d:16 * d + 16].rearrange("p (c n) -> p c n", n=1).to_broadcast([P, 16, CH])
                        me.did(dve.tensor_tensor(v3(g_b[d][:, :], 16), tot, v3(g_b[d][:, :], 16), ALU.subtract),
                               dist_ready)

            gemm("gla_v", None, gla_after)
            me.again(dve_read)
            for d in range(2):
                me.link(dve.tensor_copy(v3(decay[:, 16 * d:16 * d + 16], 16), ends(g_la[d], d)))
                me.did(dve.tensor_tensor(g_la[d][:, :], g_q[:, :], g_la[d][:, :], ALU.mult), kd_ready)
                me.next(fall_ready)
                me.did(dve.tensor_tensor(g_b[d][:, :], g_k[:, :], g_b[d][:, :], ALU.mult), kd_ready)
            gemm("gla_r", scaled(g_r, r_ready))
            def read_out(h):
                me.next(go_done)
                if h == 0:
                    dve.wait_ge(ke_ready, 2)
                me.did(dve.tensor_copy(tl(g_o, 2 * h, 2), X[2 + h % 2][:, :]), go_read)

            for h in range(GH):
                me.next(gs_done)
                me.link(dve.tensor_tensor(v3(g_m[:, :], 2), v3(G[0][:, :], 2), bc(C("gla_mask", 2 * P), 2),
                                          ALU.mult), gs_read)
                m4 = g_m[:, :].rearrange("p (t f n) -> p t f n", t=2, f=2)
                if h >= 2:
                    dve.wait_ge(go_done, h - 1)
                me.did(dve.tensor_tensor(v3(tl(g_st, h % 2), 2), m4[:, :, 0, :], m4[:, :, 1, :], ALU.add), st_ready)
                if h:
                    read_out(h - 1)
                me.next(u_done)
                S = lambda n: tl(state, n)
                dec = lambda d, c: decay[:, 16 * d + 4 * h + c:16 * d + 4 * h + c + 1]
                step = lambda n, m, k, u: dve.scalar_tensor_tensor(S(n), S(m), k, u, ALU.mult, ALU.add)
                me.link(dve.tensor_copy(S(3), X[1][:, 0:T]), u_read)
                me.did(step(4, 3, dec(1, 2), X[0][:, 0:T]), u_read)
                me.link(dve.tensor_copy(S(0), G[2][:, 0:T]))
                me.link(step(1, 0, dec(0, 1), G[3][:, 0:T]))
                me.did(step(2, 1, dec(0, 2), G[2][:, T:2 * T]), u_read)
                me.did(step(5, 4, dec(1, 1), G[3][:, T:2 * T]), u_read)
            read_out(GH - 1)

            def make(t):
                if t % 4 == 0:
                    me.next(sd_ready)
                if t % 2 == 0:
                    me.next(gated)
                return dve.scalar_tensor_tensor(tl(om, t), tl(g_r, t), B("gla_g_out_2", t % 2), tl(g_rs, t // 2),
                                                ALU.mult, ALU.mult)

            prep(make, free=PH["gla_r"].tile0 + 8, hi=xhi, lo=xlo)
            dve.wait_ge(res_ready, 2 * KT)
            out_gemm("out1", 0)
            root()
            ffn(1)
            ple(1)

            root()

            def pair(r):
                return tl(d_q, 2 * r, 2) if r < 4 else tl(d_k, 2 * r - 8, 2)

            def normalize(r):
                me.next(qk_sd)
                rs = tl(d_rs, r % 2, w=512)
                me.did(dve.scalar_tensor_tensor(pair(r), pair(r), B("diff_g_q_2" if r < 4 else "diff_g_k_2"), rs,
                                                ALU.mult, ALU.mult), qk_normed)

            def turn(r):
                me.next(qk_rot)
                me.again(qk_ready)
                me.did(dve.tensor_tensor(v3(d_t2[:, :], 2), v3(X[2 + r % 2][:, :], 2), bc(C("sin_d", T), 2), ALU.mult),
                       qk_rot_read)
                me.next(qk_cos)
                me.again(qk_rot_read)
                me.did(dve.tensor_tensor(pair(r), d_t1[:, :], d_t2[:, :], ALU.add), qk_ready)

            for base, name in ((0, "diff_q"), (4, "diff_k")):
                def after(at, t, base=base):
                    r = base + 2 * at.i
                    if t == 1 and r:
                        turn(r - 2)
                    if t == 3:
                        if r:
                            turn(r - 1)
                        normalize(r)
                        normalize(r + 1)
                gemm(name, scaled(d_q if base == 0 else d_k, qk_src), after)
            gemm("diff_v", None, lambda at, t: turn(6 + t) if at.i == 0 else None)
            for i in range(NH + 3):
                if i < NH:
                    me.next(score_done)
                    s = 4 * (i % 2)
                    for c in range(2):
                        me.did(dve.tensor_reduce(neg_max[:, s + 2 * c:s + 2 * c + 2],
                                                 v3(G[2 * (i % 2) + c][:, :], 2), AX, ALU.max, negate=True))
                    me.again()
                    me.did(dve.tensor_scalar(neg_max[:, s:s + 4], neg_max[:, s:s + 4], HD ** -0.5, None, ALU.mult),
                           max_ready)
                if 1 <= i <= NH:
                    me.next(exp_done, 2)
                    s = 4 * ((i - 1) % 2)
                    me.link(dve.reciprocal(rsum[:, s:s + 4], sums[:, s:s + 4]))
                    me.did(dve.tensor_scalar(rsum[:, s + 2:s + 4], rsum[:, s + 2:s + 4], lam[:, 4:5], None, ALU.mult))
                    for qt in range(2):
                        me.did(dve.tensor_scalar(tl(d_p, s + qt), tl(d_p, s + qt), rsum[:, s + qt:s + qt + 1],
                                                 None, ALU.mult))
                    me.again()
                    for qt in range(2):
                        ins = dve.scalar_tensor_tensor(tl(d_p, s + qt), tl(d_p, s + 2 + qt),
                                                       rsum[:, s + 2 + qt:s + 3 + qt], tl(d_p, s + qt),
                                                       ALU.mult, ALU.add)
                    me.did(ins, prob_ready)
                if i >= 3:
                    me.next(pv_done)
                    me.did(dve.tensor_copy(tl(d_o, i - 3), X[2 + (i - 3) % 2][:, 0:T]), mixed_ready)
            me.again(mixed_ready)
            prep(group_make(d_o, d_nsq, lambda t: lam[:, 5:6]), free=PH["diff_v"].tile0 + 4, hi=xhi, lo=xlo)
            out_gemm("out2", KT)
            root()
            ffn(2)
            ple(2)
            for n in range(4):
                me.next(out_done)
                me.did(dve.tensor_copy(tl(o_tok, n, w=512), G[n][:, :]), out_read)

        @block.tensor
        def _(pe):
            banks = Banks(pe)
            me = Steps(pe, None)

            def three(dst, st_hi, st_lo, mv_hi, mv_lo, start, stop_):
                pe.matmul(dst, st_hi, mv_hi, start=start, stop=False)
                pe.matmul(dst, st_hi, mv_lo, start=False, stop=False)
                return pe.matmul(dst, st_lo, mv_hi, start=False, stop=stop_)

            def slab_view(ph, buf, shape):
                if shape == "gate_up":
                    return buf[:, :].rearrange("p (k g n) -> p k g n", k=KT, g=2)
                k = {"down": FT, "ple": 2}.get(shape, KT)
                return buf[:, 0:ph.cols].rearrange("p (k n) -> p k n", k=k)

            def gemm(name, freed, shape="plain", olo_from=None, order=range(KT), after=None, before=None,
                     operand=(ohi, olo)):
                ph = PH[name]
                base = banks.n.get(freed.name, 0) if freed is not None else 0

                def body(at):
                    if before:
                        before(at)
                    hslot = (ph.j0 + at.parity) % 2
                    hi, lo = (slab_view(ph, b[hslot], shape) for b in (whi, wlo))
                    pe.wait_ge(lo_ready, at.lin(4 * (ph.j0 + 1), 4))
                    first = isinstance(at.i, int) and at.i == 0
                    for t in range(ph.tiles):
                        bank, n = bank_of(ph, at, t)
                        if shape == "gate_up":
                            by = gate_in if t % 2 == 0 else up_in
                            if first:
                                banks.claim(bank, by)
                            else:
                                wait(pe, by, at.lin(FT * int(name[-1]) + t // 2 - 1, 2))
                        elif shape == "down" and not first:
                            wait(pe, freed, at.lin(base - 1, 1))
                        else:
                            banks.claim(bank, freed)
                        if shape == "gate_up":
                            w = lambda v, k: v[:, k, t % 2, (t // 2) * P:(t // 2 + 1) * P]
                        elif ph.tiles == 1:
                            w = lambda v, k: v[:, k, :]
                        else:
                            w = lambda v, k: v[:, k, t * P:(t + 1) * P]
                        ks = {"down": range(FT), "ple": range(2)}.get(shape, order)
                        layer = int(name[-1]) - 1 if shape == "ple" else 0
                        for n_, k in enumerate(ks):
                            if first and t == 0 and olo_from is not None:
                                pe.wait_ge(olo_ready, olo_from + n_ + 1)
                            if first and shape == "down":
                                pe.wait_ge(actlo_ready, FT * int(name[-1]) + k + 1)
                            if shape == "token":
                                st = [tl(b, k)[:, t * P:(t + 1) * P] for b in operand]
                                ins = three(bank[:, 0:n], *st, hi[:, k, :], lo[:, k, :], n_ == 0, n_ == len(ks) - 1)
                            else:
                                src = {"down": (acthi, actlo), "ple": (p_hi, p_lo)}.get(shape, operand)
                                mv = [tl(b, k + 2 * layer) for b in src]
                                ins = three(bank[:, 0:T], w(hi, k), w(lo, k), *mv, n_ == 0, n_ == len(ks) - 1)
                        ins.then_inc(tile_done, 1)
                        if after:
                            after(at, t)
                    if first and shape == "down":
                        banks.settle(G[1])

                rounds(pe, ph, body)
                if shape == "gate_up":
                    end = FT * (int(name[-1]) + 1)
                    for t in range(4):
                        banks.skip(G[t], gate_in if t % 2 == 0 else up_in, end)
                if shape == "down":
                    banks.skip(G[0], freed, base + ph.n)
                    banks.skip(G[1], freed, base + ph.n)

            def stats(tok=False):
                banks.claim(X[0], sd_ready)
                me.next(squares_summed)
                me.seen(sq_ready, KT)
                ins = pe.matmul(X[0][:, 0:T], ones[:, :], sq_sum[:, :], start=True, stop=True)
                for tt in range(TT if tok else 0):
                    ins = pe.matmul(X[0][:, T + tt:T + tt + 1], sq_sum[:, tt * P:(tt + 1) * P], ones[:, 0:1],
                                    start=True, stop=True, skip_group_check=True)
                ins.then_inc(stat_done, 1)

            def group_stats(groups, mat, buf, ready_banks):
                for n, g in enumerate(groups):
                    bank = ready_banks[n % len(ready_banks)]
                    banks.claim(bank, sd_ready)
                    me.next(sq_ready)
                    pe.matmul(bank[:, :], mat, tl(buf, 2 * g, 2), start=True, stop=True).then_inc(stat_done, 1)

            def modulation(i):
                ph = PH[f"ada{i}"]
                pe.wait_ge(pool_summed if i in POOL_SLABS else dve_summed, ph.used0 + 1)
                for m in range(4):
                    o = 512 * mod_half(i) + P * m
                    ins = pe.matmul(X[3][:, 4 * i + m:4 * i + m + 1], macc[:, o:o + P], ones[:, 0:1],
                                    start=True, stop=True, skip_group_check=True)
                ins.then_inc(mod_done, 1)

            pe.wait_ge(c_in, 32)
            banks.claim(X[3], c_ready)
            pe.transpose(X[3][:, 48:56], rows_c[0:KT, :], ident[0:KT, 0:KT]).then_inc(c_ready_t, 1)
            pe.wait_ge(set_zero, 3)
            banks.claim(X[3], mod_read)
            pe.wait_ge(params_in, 16 * (len(ROWS_A) + len(ROWS_B) + 4))
            banks.claim(G[0], dve_read)
            pe.transpose(G[0][:, 0:NA], rows_a[0:NA, :], ident[0:NA, 0:NA])
            pe.transpose(G[0][:, P:P + NB], rows_b[0:NB, :], ident[0:NB, 0:NB]).then_inc(setup_t, 1)
            for i in range(3):
                modulation(i)
            pe.wait_ge(x_in, 16)
            for n, bank in enumerate((X[0], X[1], X[2], G[1])):
                banks.claim(bank, res_in)
                for k in range(2):
                    for tt in range(TT):
                        ins = pe.transpose(bank[:, k * T + tt * P:k * T + (tt + 1) * P],
                                           tl(xin, tt, w=D)[:, (2 * n + k) * P:(2 * n + k + 1) * P], ident)
                ins.then_inc(setup_t, 1)
            modulation(3)
            banks.claim(X[3], mod_read)
            gemm("in_q", rope_src, olo_from=0)
            pe.wait_ge(const_in, 16)
            pe.wait_ge(p_in, 16)
            for layer in range(2):
                bank = X[1 + layer]
                banks.claim(bank, dve_read)
                for k in range(2):
                    for tt in range(TT):
                        o = layer * 512 + tt * 256 + k * P
                        ins = pe.transpose(bank[:, k * T + tt * P:k * T + (tt + 1) * P], pin[:, o:o + P], ident)
                ins.then_inc(setup_t, 1)
            gemm("in_idx", rope_src)

            def rotate(r):
                bank = X[(0, 1, 2, 0)[r]]
                banks.claim(bank, rot_read)
                pe.wait_ge(rope_src, (2, 4, 8, 8)[r])
                if r == 2:
                    pe.matmul(bank[:, 0:T], C("rot_q"), tl(rope_in, 4), start=True, stop=True)
                    ins = pe.matmul(bank[:, T:2 * T], C("rot_i"), tl(rope_in, 7), start=True, stop=True)
                else:
                    ins = pe.matmul(bank[:, :], C("rot_i" if r == 3 else "rot_q"), tl(rope_in, (0, 2, None, 5)[r], 2),
                                    start=True, stop=True)
                ins.then_inc(rot_done, 1)

            rotate(0)
            rotate(1)
            gemm("in_v", v_src, shape="token")
            rotate(2)
            rotate(3)
            gemm("in_gc", gc_ready)
            modulation(4)
            pe.wait_ge(roped, 4)
            for h in range(IH):
                banks.claim(G[h % 4], relu_done)
                rows = slice(ID * (h % 4), ID * (h % 4) + ID)
                q, kk = tl(rope_out, 5 + h // 4), tl(rope_out, 7)
                pe.matmul(G[h % 4][:, 0:P], q[rows, 0:P], kk[rows, 0:P], start=True, stop=True)
                pe.matmul(G[h % 4][:, P:3 * P], q[rows, P:2 * P], kk[rows, :], start=True,
                          stop=True).then_inc(idx_done, 1)
            gemm("in_hc", dve_read)
            modulation(5)
            gemm("in_gb", mixed_ready)
            group_stats((2, 3), C("blk"), mix_sq, X[0:2])
            def scores(i):
                banks.claim(G[i % 2], score_read)
                rows = slice(HD * (i % 2), HD * (i % 2) + HD)
                q, kk = tl(rope_out, i // 2), tl(rope_out, 4)
                pe.matmul(G[i % 2][:, 0:P], q[rows, 0:P], kk[rows, 0:P], start=True, stop=True)
                pe.matmul(G[i % 2][:, P:3 * P], q[rows, P:2 * P], kk[rows, :], start=True,
                          stop=True).then_inc(score_done, 1)

            scores(0)
            for i in range(NH + 2):
                if i + 1 < NH:
                    scores(i + 1)
                for n in MOD_TAKEN.get(i, ()):
                    modulation(n)
                if 1 <= i <= NH:
                    bank, lg = G[2 + (i - 1) % 2], tl(logit, (i - 1) % 2, w=384)
                    banks.claim(bank, pt_ready)
                    me.next(prob_ready)
                    for n in range(3):
                        ins = pe.transpose(bank[:, n * P:(n + 1) * P], lg[:, n * P:(n + 1) * P], ident)
                    ins.then_inc(trans_done, 1)
                if i >= 2:
                    h = i - 2
                    bank, pt = X[h // 2 % 2], tl(prob_t, h % 2, w=384)
                    if h % 2 == 0:
                        banks.claim(bank, mixed_ready)
                    me.next(pt_ready)
                    rows = slice(HD * (h % 2), HD * (h % 2) + HD)
                    pe.matmul(bank[rows, 0:T], vtok[:, 0:HD], pt[:, 0:T], start=True, stop=False,
                              skip_group_check=True)
                    pe.matmul(bank[rows, P:T], vtok[:, 72:72 + HD], pt[:, T:T + P], start=False, stop=True,
                              skip_group_check=True).then_inc(pv_done, 1)
            def next_operand():
                OPERANDS[0] += KT
                return OPERANDS[0]

            def mean_sums(tiles):
                for t in tiles:
                    if t == 0:
                        banks.claim(X[0], mean_ready)
                    pe.wait_ge(dve_read, STREAM[0] + t + 1)
                    ins = pe.matmul(X[0][:, 0:T], ones[:, :], tl(res, t), start=(t == 0), stop=(t == KT - 1))
                    if t == KT - 1:
                        ins.then_inc(mean_done, 1)

            def layer_norm():
                mean_sums(range(KT - 1, KT))
                banks.claim(X[1], sd_ready)
                for t in range(KT):
                    if t % 2 == 0:
                        me.next(sq_ready)
                    ins = pe.matmul(X[1][:, 0:T], ones[:, :], tl(sq, t), start=(t == 0), stop=(t == KT - 1))
                ins.then_inc(stat_done, 1)

            group_stats((0, 1), C("blk"), mix_sq, X[0:2])
            OPERANDS = [8]
            STREAM = [banks.n[dve_read.name]]
            gemm("out0", dve_read, olo_from=8, order=(4, 5, 6, 7, 0, 1, 2, 3),
                 after=lambda at, t: mean_sums([4 * at.i + t - 1]) if 4 * at.i + t else None)

            def ffn(k, stat):

                def after(at, t):
                    if stat and t == 0 and at.it is None and at.i == 0:
                        stats()

                gemm(f"gate_up{k}", gate_in, shape="gate_up", olo_from=next_operand(), after=after)
                STREAM[0] = banks.n[dve_read.name]

                def before(at):
                    if k == 0 and at.it is None and at.i == KT - 1:
                        mean_sums(range(KT - 2))

                gemm(f"down{k}", dve_read, shape="down", before=before,
                     after=lambda at, t: mean_sums([KT - 2]) if k == 0 and at.it is None and at.i == KT - 1 else None)

            def ple(k):
                start = next_operand()
                gemm(f"ple_proj{k}", pp_ready, shape="ple")
                stats()
                gemm(f"ple_gate{k}", ple_in, olo_from=start)

            layer_norm()
            ffn(0, False)

            layer_norm()
            start = next_operand()
            ph = PH["gla_z"]
            slot = ph.slot
            pe.wait_ge(landed[slot], ph.landed[0])
            banks.claim(X[1], z_ready)
            for k in range(KT):
                pe.wait_ge(olo_ready, start + k + 1)
                ins = pe.matmul(X[1][0:48, 0:T], raw[slot][:, 48 * k:48 * (k + 1)], tl(om, k),
                                start=(k == 0), stop=(k == KT - 1))
            ins.then_inc(z_done, 1)
            gemm("gla_q", dve_read, after=lambda at, t: stats(tok=True) if t == 0 else None)
            pe.wait_ge(z_ready, 1)
            pe.wait_ge(gates_in, 32)
            for b in range(4):
                banks.claim(X[b], la_read)
                for half in range(2):
                    t = 2 * (b % 2) + half
                    ins = pe.matmul(X[b][:, half * T:(half + 1) * T],
                                    wgate[32 * (b // 2):32 * (b // 2) + RANK, P * t:P * (t + 1)],
                                    g_z[32 * (b // 2):32 * (b // 2) + RANK, :], start=True, stop=True)
                ins.then_inc(la_done, 1)
            gemm("gla_k", dve_read)
            gemm("gla_v", v_ready, shape="token")
            gemm("gla_r", r_ready)
            pe.wait_ge(kd_ready, 4)
            pe.wait_ge(ke_ready, 2)
            pe.wait_ge(v_ready, 4)

            def outputs(h):
                bank = X[2 + h % 2]
                banks.claim(bank, go_read)
                pe.wait_ge(st_ready, h + 1)
                first = True
                for e in range(2):
                    for tt in range(TT):
                        v = g_v[:, tt * D + h * GDV + e * P:tt * D + h * GDV + e * P + P]
                        pe.matmul(bank[:, e * T + tt * P:e * T + (tt + 1) * P], v,
                                  tl(g_st, h % 2)[:, tt * P:(tt + 1) * P], start=first, stop=False,
                                  skip_group_check=True)
                        first = False
                pe.wait_ge(u_read, 4 * (h + 1))
                for e in range(2):
                    for d in range(2):
                        for n in range(3):
                            c = n + 1 if d == 0 else 2 - n
                            ins = pe.matmul(bank[:, e * T + c * CH:e * T + (c + 1) * CH],
                                            tl(state, 3 * d + n)[:, e * P:(e + 1) * P],
                                            tl(g_la[d], h)[:, c * CH:(c + 1) * CH], start=False,
                                            stop=(e == 1 and d == 1 and n == 2), skip_group_check=True)
                ins.then_inc(go_done, 1)

            for h in range(GH + 1):
                if h < GH:
                    banks.claim(G[0], gs_read)
                    for tt in range(TT):
                        for d in range(2):
                            o = (2 * tt + d) * P
                            ins = pe.matmul(G[0][:, o:o + P], tl(g_ke[d], h)[:, tt * P:(tt + 1) * P],
                                            tl(g_la[d], h)[:, tt * P:(tt + 1) * P], start=True, stop=True)
                    ins.then_inc(gs_done, 1)
                    banks.claim(G[1], kt_ready)
                    for d in range(2):
                        for tt in range(TT):
                            ins = pe.transpose(G[1][:, (2 * d + tt) * P:(2 * d + tt + 1) * P],
                                               tl(g_b[d], h)[:, tt * P:(tt + 1) * P], ident)
                    ins.then_inc(kt_done, 1)
                if h:
                    outputs(h - 1)
                if h < GH:
                    pe.wait_ge(kt_ready, h + 1)
                    for bank in (X[1], X[0], G[2], G[3]):
                        banks.claim(bank, u_read)
                    for bank, half, d, c in ((X[1], 0, 1, 3), (X[0], 0, 1, 2), (G[2], 0, 0, 0), (G[3], 0, 0, 1),
                                             (G[2], 1, 0, 2), (G[3], 1, 1, 1)):
                        rows = slice(CH * (c % 2), CH * (c % 2) + CH)
                        tt = c // 2
                        ins = pe.matmul(bank[:, half * T:(half + 1) * T],
                                        kd_tok[rows, (2 * d + tt) * P:(2 * d + tt + 1) * P],
                                        g_v[rows, tt * D + h * GDV:tt * D + (h + 1) * GDV], start=True, stop=True)
                    ins.then_inc(u_done, 1)
            for h in range(GH):
                if h % 2 == 0:
                    banks.claim(G[h // 2], sd_ready)
                me.next(sq_ready)
                for e in range(2):
                    ins = pe.matmul(G[h // 2][:, (h % 2) * T:(h % 2 + 1) * T], ones[:, :], tl(g_sq, 2 * h + e),
                                    start=(e == 0), stop=(e == 1))
                if h % 2:
                    ins.then_inc(stat_done, 1)
            start = next_operand()
            gemm("out1", dve_read, olo_from=start, operand=(xhi, xlo))
            ffn(1, True)
            ple(1)

            def block_sums(r):
                banks.claim(X[r % 2], qk_sd)
                me.next(qk_sq)
                pe.matmul(X[r % 2][:, :], C("blk"), tl(d_sq, r % 2, w=512), start=True, stop=True).then_inc(qk_stat, 1)

            def partners(r):
                banks.claim(X[2 + r % 2], qk_rot_read)
                pe.wait_ge(qk_normed, r + 1)
                src = tl(d_q, 2 * r, 2) if r < 4 else tl(d_k, 2 * r - 8, 2)
                pe.matmul(X[2 + r % 2][:, :], C("rot_d"), src, start=True, stop=True).then_inc(qk_rot, 1)

            start = next_operand()
            for base, name in ((0, "diff_q"), (4, "diff_k")):
                def after(at, t, base=base):
                    r = base + 2 * at.i
                    if r == 0 and t == 0:
                        stats(tok=True)
                    if t == 1 and r:
                        partners(r - 2)
                    if t == 3:
                        if r:
                            partners(r - 1)
                        block_sums(r)
                        block_sums(r + 1)
                gemm(name, qk_src, olo_from=start if base == 0 else None, after=after, operand=(dhi, xlo))
            gemm("diff_v", v_ready, shape="token", operand=(dhi, xlo), after=lambda at, t: partners(6 + t) if at.i == 0 else None)
            pe.wait_ge(qk_ready, 8)
            pe.wait_ge(v_ready, 8)
            def scores(i):
                for c in range(2):
                    banks.claim(G[2 * (i % 2) + c], exp_done)
                for qt in range(2):
                    for c in range(2):
                        rows = slice(HD * c, HD * c + HD)
                        ins = pe.matmul(G[2 * (i % 2) + c][:, qt * T:(qt + 1) * T],
                                        tl(d_q, i)[rows, qt * P:(qt + 1) * P], tl(d_k, i)[rows, :],
                                        start=True, stop=True)
                ins.then_inc(score_done, 1)

            banks.n[exp_done.name] = NH
            scores(0)
            for i in range(NH + 2):
                if i + 1 < NH:
                    scores(i + 1)
                if 1 <= i <= NH:
                    s = (i - 1) % 2
                    banks.claim(X[s], pt_ready)
                    me.next(prob_ready)
                    for kt in range(2):
                        for qt in range(2):
                            ins = pe.transpose(X[s][:, kt * T + qt * P:kt * T + (qt + 1) * P],
                                               tl(d_p, 4 * s + qt)[:, kt * P:(kt + 1) * P], ident)
                    ins.then_inc(trans_done, 1)
                if i == NH + 1:
                    group_stats((0, 1), ones[:, :], d_nsq, G[0:2])
                if i >= 2:
                    h = i - 2
                    banks.claim(X[2 + h % 2], mixed_ready)
                    me.next(pt_ready)
                    for kt in range(2):
                        ins = pe.matmul(X[2 + h % 2][:, 0:T], d_v[:, kt * D + h * P:kt * D + (h + 1) * P],
                                        tl(d_pt, h % 2, w=512)[:, kt * T:(kt + 1) * T], start=(kt == 0), stop=(kt == 1))
                    ins.then_inc(pv_done, 1)
            group_stats((2, 3), ones[:, :], d_nsq, G[2:4])
            start = next_operand()
            gemm("out2", dve_read, olo_from=start, operand=(xhi, xlo))
            ffn(2, True)
            ple(2)
            pe.wait_ge(ple_added, 2 * KT)
            for n in range(4):
                tt, half = n // 2, n % 2
                banks.claim(G[n], out_read)
                for k in range(4):
                    ins = pe.transpose(G[n][:, k * P:(k + 1) * P], tl(res, 4 * half + k)[:, tt * P:(tt + 1) * P], ident)
                ins.then_inc(out_done, 1)


_INS = ["x", "c", "w_ada", "b_ada", "w_in", "conv_w", "attn_norm_g", "conv_norm_g", "w_out", "ln1_g", "ln1_b", "w_gate",
        "w_up", "w_down", "ln2_g", "ln2_b", "p_2", "norm_mix_2", "norm_ffn_2", "ffn_w_in_2", "ffn_w_out_2", "ple_norm_2",
        "ple_w_gate_2", "ple_w_proj_2", "gla_w_in_2", "gla_w_gate_f_2", "gla_b_gate_f_2", "gla_w_gate_b_2",
        "gla_b_gate_b_2", "gla_g_out_2", "gla_w_out_2", "diff_w_in_2", "diff_g_q_2", "diff_g_k_2", "diff_lam_q1_2",
        "diff_lam_k1_2", "diff_lam_q2_2", "diff_lam_k2_2", "diff_g_sub_2", "diff_w_out_2"]


def kernel(**inputs):
    import concourse.bacc as bacc
    from concourse.bass_utils import run_bass_kernel_spmd

    arrays = {f"in_{n}": np.ascontiguousarray(inputs[n]) for n in _INS}
    arrays["in_shape_constants"] = shape_constants()
    nc = bacc.Bacc("TRN2", target_bir_lowering=False, num_devices=1)
    a = {n[3:]: nc.dram_tensor(n, v.shape, F32, kind="ExternalInput").ap() for n, v in arrays.items()}
    out = nc.dram_tensor("out_0", (1, T, D), F32, kind="ExternalOutput").ap()
    build(nc, a, out)
    r = run_bass_kernel_spmd(nc, [arrays], core_ids=[0])
    return r.results[0]["out_0"]
```
